# Optimizing a Trainium2 kernel written in Bass

```python
import math
import jax, jax.numpy as jnp
from jax import lax
import numpy as np

D_MODEL = 1024
BATCH = 1
SEQ = 1024
DEPTH = 1
DEC_BATCH = 8
DEC_SEQ = 8
PAST_LEN = 2048
PAGE_SIZE = 128

N_HEADS = 8
N_KV_HEADS = 2
REP = N_HEADS // N_KV_HEADS
HEAD_DIM = 64
ATTN_WIDTH = N_HEADS * HEAD_DIM
KV_WIDTH = N_KV_HEADS * HEAD_DIM
WINDOW = 128
ATTN_BLOCK = WINDOW
ROT_DIM = HEAD_DIM // 4
ROPE_THETA = 500000.0
NEG_INF = -1e30
SSM_WIDTH = D_MODEL - ATTN_WIDTH
SSM_GROUP = 16
N_SSM_GROUPS = SSM_WIDTH // SSM_GROUP
SSM_STATE = 64
IN_WIDTH = ATTN_WIDTH + 2 * KV_WIDTH + SSM_WIDTH
PEER_HEADS = 8
N_KEYS = 128
N_EXPERTS = N_KEYS * N_KEYS
PEER_TOPK = 16
PEER_QDIM = 256
PEER_HALF = PEER_QDIM // 2
PEER_CHUNK = 128
RMS_EPS = 1e-5

kernel_name = 'hymba_swa_s5_peer_step'

def rmsnorm(x, g):
    xf = x.astype(jnp.float32)
    y = xf * lax.rsqrt(jnp.mean(xf * xf, axis=-1, keepdims=True) + RMS_EPS)
    return (y * g.astype(jnp.float32)).astype(x.dtype)

def partial_rope(x, pos):
    half = ROT_DIM // 2
    inv_freq = ROPE_THETA ** (-jnp.arange(half, dtype=jnp.float32) * 2.0 / ROT_DIM)
    ang = pos.astype(jnp.float32)[:, None] * inv_freq[None, :]
    cos = jnp.cos(ang)[:, None, :]
    sin = jnp.sin(ang)[:, None, :]
    xf = x.astype(jnp.float32)
    x1 = xf[..., :half]
    x2 = xf[..., half:ROT_DIM]
    out = jnp.concatenate([x1 * cos - x2 * sin, x2 * cos + x1 * sin, xf[..., ROT_DIM:]], axis=-1)
    return out.astype(x.dtype)

def window_attention(q, k, v, q_pos, k_pos, sinks):
    s = jnp.einsum('bnqgrd,bnkgd->bngrqk', q.astype(jnp.float32), k.astype(jnp.float32)) * (HEAD_DIM ** -0.5)
    diff = q_pos[:, :, None] - k_pos[:, None, :]
    mask = (diff >= 0) & (diff < WINDOW) & (k_pos[:, None, :] >= 0)
    s = jnp.where(mask[None, :, None, None], s, NEG_INF)
    sink = sinks.astype(jnp.float32).reshape(N_KV_HEADS, REP)[None, None, :, :, None, None]
    m = jnp.maximum(jnp.max(s, axis=-1, keepdims=True), sink)
    p = jnp.exp(s - m)
    w = p / (jnp.sum(p, axis=-1, keepdims=True) + jnp.exp(sink - m))
    return jnp.einsum('bngrqk,bnkgd->bnqgrd', w, v.astype(jnp.float32))

def _complex_affine_combine(e1, e2):
    a1r, a1i, b1r, b1i = e1
    a2r, a2i, b2r, b2i = e2
    return (a2r * a1r - a2i * a1i,
            a2r * a1i + a2i * a1r,
            a2r * b1r - a2i * b1i + b2r,
            a2r * b1i + a2i * b1r + b2i)

def s5_mixer(u, h0_re, h0_im, lam_re, lam_im, log_step, b_re, b_im, c_re, c_im, d_skip, w_glu, b_glu):
    f32 = jnp.float32
    bsz, t = u.shape[:2]
    uf = u.astype(f32).reshape(bsz, t, N_SSM_GROUPS, SSM_GROUP)
    lr = lam_re.astype(f32)
    li = lam_im.astype(f32)
    dt = jnp.exp(log_step.astype(f32))[:, None]
    mag = jnp.exp(lr * dt)
    ab_re = mag * jnp.cos(li * dt)
    ab_im = mag * jnp.sin(li * dt)
    den = lr * lr + li * li
    z_re = ((ab_re - 1.0) * lr + ab_im * li) / den
    z_im = (ab_im * lr - (ab_re - 1.0) * li) / den
    br = b_re.astype(f32)
    bi = b_im.astype(f32)
    bb_re = z_re[..., None] * br - z_im[..., None] * bi
    bb_im = z_re[..., None] * bi + z_im[..., None] * br
    bu_re = jnp.einsum('btgp,gnp->btgn', uf, bb_re)
    bu_im = jnp.einsum('btgp,gnp->btgn', uf, bb_im)
    h0r = h0_re.astype(f32)
    h0i = h0_im.astype(f32)
    bu_re = bu_re.at[:, 0].add(ab_re * h0r - ab_im * h0i)
    bu_im = bu_im.at[:, 0].add(ab_re * h0i + ab_im * h0r)
    a_re = jnp.broadcast_to(ab_re, bu_re.shape)
    a_im = jnp.broadcast_to(ab_im, bu_im.shape)
    _, _, h_re, h_im = lax.associative_scan(_complex_affine_combine, (a_re, a_im, bu_re, bu_im), axis=1)
    y = (jnp.einsum('btgn,gpn->btgp', h_re, c_re.astype(f32))
         - jnp.einsum('btgn,gpn->btgp', h_im, c_im.astype(f32))
         + d_skip.astype(f32).reshape(N_SSM_GROUPS, SSM_GROUP) * uf)
    y = jax.nn.gelu(y.reshape(bsz, t, SSM_WIDTH), approximate=False)
    y = y * jax.nn.sigmoid(y @ w_glu.astype(f32) + b_glu.astype(f32))
    return y.astype(u.dtype), h_re[:, -1], h_im[:, -1]

def peer_ffn(x, w_query, sub_keys, u_table, v_table):
    f32 = jnp.float32
    n_tok = x.shape[0]
    pad = (-n_tok) % PEER_CHUNK
    xb = jnp.pad(x, ((0, pad), (0, 0))).reshape(-1, PEER_CHUNK, D_MODEL)
    keys = sub_keys.astype(f32)

    def chunk(xc):
        q = (xc @ w_query).astype(f32).reshape(PEER_CHUNK, PEER_HEADS, 2, PEER_HALF)
        s = jnp.einsum('thcd,hckd->thck', q, keys)
        top_s, top_i = lax.top_k(s, PEER_TOPK)
        cand_s = (top_s[:, :, 0, :, None] + top_s[:, :, 1, None, :]).reshape(PEER_CHUNK, PEER_HEADS, PEER_TOPK * PEER_TOPK)
        cand_i = (top_i[:, :, 0, :, None] * N_KEYS + top_i[:, :, 1, None, :]).reshape(PEER_CHUNK, PEER_HEADS, PEER_TOPK * PEER_TOPK)
        best_s, best_j = lax.top_k(cand_s, PEER_TOPK)
        idx = jnp.take_along_axis(cand_i, best_j, axis=-1)
        gate = jax.nn.softmax(best_s, axis=-1)
        act = jax.nn.gelu(jnp.einsum('thkd,td->thk', u_table[idx].astype(f32), xc.astype(f32)), approximate=False)
        return jnp.einsum('thk,thkd->td', gate * act, v_table[idx].astype(f32)).astype(xc.dtype)

    y = lax.map(chunk, xb)
    return y.reshape(-1, D_MODEL)[:n_tok]

def layer(x, k_buf, v_buf, h0_re, h0_im, norm_mix, w_in, b_in, attn_sinks, lam_re, lam_im, log_step,
          b_re, b_im, c_re, c_im, d_skip, w_glu, b_glu, norm_attn_out, norm_ssm_out, w_out,
          norm_ffn, w_query, sub_keys, u_table, v_table):
    bsz, t, _ = x.shape
    xn = rmsnorm(x, norm_mix)
    proj = xn @ w_in + b_in
    q, k, v, u = jnp.split(proj, [ATTN_WIDTH, ATTN_WIDTH + KV_WIDTH, ATTN_WIDTH + 2 * KV_WIDTH], axis=-1)
    q = q.reshape(bsz, t, N_HEADS, HEAD_DIM)
    k = k.reshape(bsz, t, N_KV_HEADS, HEAD_DIM)
    v = v.reshape(bsz, t, N_KV_HEADS, HEAD_DIM)
    if k_buf is None:
        pos = jnp.arange(t, dtype=jnp.int32)
        q = partial_rope(q, pos)
        k = partial_rope(k, pos)
        nb = t // ATTN_BLOCK
        qb = q.reshape(bsz, nb, ATTN_BLOCK, N_KV_HEADS, REP, HEAD_DIM)
        kb = k.reshape(bsz, nb, ATTN_BLOCK, N_KV_HEADS, HEAD_DIM)
        vb = v.reshape(bsz, nb, ATTN_BLOCK, N_KV_HEADS, HEAD_DIM)
        pad_blk = ((0, 0), (1, 0), (0, 0), (0, 0), (0, 0))
        kk = jnp.concatenate([jnp.pad(kb, pad_blk)[:, :-1], kb], axis=2)
        vv = jnp.concatenate([jnp.pad(vb, pad_blk)[:, :-1], vb], axis=2)
        qpos = pos.reshape(nb, ATTN_BLOCK)
        kpos = jnp.concatenate([qpos - ATTN_BLOCK, qpos], axis=1)
        attn = window_attention(qb, kk, vv, qpos, kpos, attn_sinks)
        k_win = k[:, -WINDOW:]
        v_win = v[:, -WINDOW:]
    else:
        pos = PAST_LEN + jnp.arange(t, dtype=jnp.int32)
        q = partial_rope(q, pos)
        k = partial_rope(k, pos)
        kk = jnp.concatenate([k_buf.astype(k.dtype), k], axis=1)
        vv = jnp.concatenate([v_buf.astype(v.dtype), v], axis=1)
        kpos = jnp.concatenate([PAST_LEN - WINDOW + jnp.arange(WINDOW, dtype=jnp.int32), pos])
        attn = window_attention(q.reshape(bsz, 1, t, N_KV_HEADS, REP, HEAD_DIM), kk[:, None], vv[:, None],
                                pos[None], kpos[None], attn_sinks)
        k_win = kk[:, -WINDOW:]
        v_win = vv[:, -WINDOW:]
    attn = attn.reshape(bsz, t, ATTN_WIDTH).astype(x.dtype)
    ssm, h_re, h_im = s5_mixer(u, h0_re, h0_im, lam_re, lam_im, log_step, b_re, b_im, c_re, c_im,
                               d_skip, w_glu, b_glu)
    mix = jnp.concatenate([rmsnorm(attn, norm_attn_out), rmsnorm(ssm, norm_ssm_out)], axis=-1)
    x = x + mix @ w_out
    ffn = peer_ffn(rmsnorm(x, norm_ffn).reshape(-1, D_MODEL), w_query, sub_keys, u_table, v_table)
    x = x + ffn.reshape(x.shape)
    return x, k_win, v_win, h_re, h_im

def setup_inputs(seed: int = 0) -> dict:
    key = jax.random.key(seed)
    ks = jax.random.split(key, 32)
    f32 = jnp.float32
    L = DEPTH

    def nrm(k, shape, scale):
        return jax.random.normal(k, shape, f32) * scale

    n_idx = jnp.arange(SSM_STATE, dtype=f32)
    return {
        'x_prompt': nrm(ks[0], (BATCH, SEQ, D_MODEL), 1.0),
        'x_sample': nrm(ks[1], (DEC_BATCH, DEC_SEQ, D_MODEL), 1.0),
        'cache_k': nrm(ks[2], (L, DEC_BATCH, WINDOW, N_KV_HEADS, HEAD_DIM), 1.0),
        'cache_v': nrm(ks[3], (L, DEC_BATCH, WINDOW, N_KV_HEADS, HEAD_DIM), 1.0),
        'state_ssm_re': nrm(ks[4], (L, DEC_BATCH, N_SSM_GROUPS, SSM_STATE), 0.3),
        'state_ssm_im': nrm(ks[5], (L, DEC_BATCH, N_SSM_GROUPS, SSM_STATE), 0.3),
        'norm_mix': 1.0 + nrm(ks[6], (L, D_MODEL), 0.02),
        'w_in': nrm(ks[7], (L, D_MODEL, IN_WIDTH), D_MODEL ** -0.5),
        'b_in': nrm(ks[8], (L, IN_WIDTH), 0.02),
        'attn_sinks': nrm(ks[9], (L, N_HEADS), 1.0),
        'ssm_lam_re': -0.5 + nrm(ks[10], (L, N_SSM_GROUPS, SSM_STATE), 0.01),
        'ssm_lam_im': math.pi * n_idx + nrm(ks[11], (L, N_SSM_GROUPS, SSM_STATE), 0.01),
        'ssm_log_step': jax.random.uniform(ks[12], (L, N_SSM_GROUPS), f32, math.log(1e-3), math.log(1e-1)),
        'ssm_b_re': nrm(ks[13], (L, N_SSM_GROUPS, SSM_STATE, SSM_GROUP), (2 * SSM_GROUP) ** -0.5),
        'ssm_b_im': nrm(ks[14], (L, N_SSM_GROUPS, SSM_STATE, SSM_GROUP), (2 * SSM_GROUP) ** -0.5),
        'ssm_c_re': nrm(ks[15], (L, N_SSM_GROUPS, SSM_GROUP, SSM_STATE), (2 * SSM_STATE) ** -0.5),
        'ssm_c_im': nrm(ks[16], (L, N_SSM_GROUPS, SSM_GROUP, SSM_STATE), (2 * SSM_STATE) ** -0.5),
        'ssm_d': nrm(ks[17], (L, SSM_WIDTH), 1.0),
        'ssm_w_glu': nrm(ks[18], (L, SSM_WIDTH, SSM_WIDTH), SSM_WIDTH ** -0.5),
        'ssm_b_glu': nrm(ks[19], (L, SSM_WIDTH), 0.02),
        'norm_attn_out': 1.0 + nrm(ks[20], (L, ATTN_WIDTH), 0.02),
        'norm_ssm_out': 1.0 + nrm(ks[21], (L, SSM_WIDTH), 0.02),
        'w_out': nrm(ks[22], (L, D_MODEL, D_MODEL), D_MODEL ** -0.5),
        'norm_ffn': 1.0 + nrm(ks[23], (L, D_MODEL), 0.02),
        'peer_w_query': nrm(ks[24], (L, D_MODEL, PEER_HEADS * PEER_QDIM), D_MODEL ** -0.5),
        'peer_sub_keys': nrm(ks[25], (L, PEER_HEADS, 2, N_KEYS, PEER_HALF), PEER_HALF ** -0.5),
        'peer_u': nrm(ks[26], (L, N_EXPERTS, D_MODEL), D_MODEL ** -0.5),
        'peer_v': nrm(ks[27], (L, N_EXPERTS, D_MODEL), PEER_HEADS ** -0.5),
        'norm_final': 1.0 + nrm(ks[28], (D_MODEL,), 0.02),
    }

def reference(x_prompt, x_sample, cache_k, cache_v, state_ssm_re, state_ssm_im, norm_mix, w_in, b_in,
              attn_sinks, ssm_lam_re, ssm_lam_im, ssm_log_step, ssm_b_re, ssm_b_im, ssm_c_re, ssm_c_im,
              ssm_d, ssm_w_glu, ssm_b_glu, norm_attn_out, norm_ssm_out, w_out, norm_ffn, peer_w_query,
              peer_sub_keys, peer_u, peer_v, norm_final):
    xp = x_prompt
    xs = x_sample
    pk, pv, pr, pim, sk, sv, sr, sim = [], [], [], [], [], [], [], []
    for l in range(DEPTH):
        lp = [w[l] for w in (norm_mix, w_in, b_in, attn_sinks, ssm_lam_re, ssm_lam_im, ssm_log_step,
                             ssm_b_re, ssm_b_im, ssm_c_re, ssm_c_im, ssm_d, ssm_w_glu, ssm_b_glu,
                             norm_attn_out, norm_ssm_out, w_out, norm_ffn, peer_w_query, peer_sub_keys,
                             peer_u, peer_v)]
        h_zero = jnp.zeros((xp.shape[0], N_SSM_GROUPS, SSM_STATE), jnp.float32)
        xp, k1, v1, r1, i1 = layer(xp, None, None, h_zero, h_zero, *lp)
        xs, k2, v2, r2, i2 = layer(xs, cache_k[l], cache_v[l], state_ssm_re[l], state_ssm_im[l], *lp)
        pk.append(k1); pv.append(v1); pr.append(r1); pim.append(i1)
        sk.append(k2); sv.append(v2); sr.append(r2); sim.append(i2)
    y_prompt = rmsnorm(xp, norm_final)
    y_sample = rmsnorm(xs, norm_final)
    return (y_prompt, y_sample, jnp.stack(pk), jnp.stack(pv), jnp.stack(pr), jnp.stack(pim),
            jnp.stack(sk), jnp.stack(sv), jnp.stack(sr), jnp.stack(sim))


_drawn_inputs = setup_inputs


def setup_inputs(seed=0):
    import zlib

    import numpy as np

    out = dict(_drawn_inputs(seed))
    spreads = {}
    factors = {'ssm_lam_re': 15.959,
     'ssm_b_glu': 4.992,
     'norm_attn_out': 10.961,
     'norm_ssm_out': 10.956,
     'norm_ffn': 10.589,
     'norm_final': 7.253}
    for name, (base, spread) in spreads.items():
        noise = np.random.default_rng([zlib.crc32(name.encode()), seed]).standard_normal(out[name].shape)
        drawn = base * np.exp(spread * noise) if base else spread * noise
        out[name] = __import__('jax').numpy.asarray(drawn.astype(out[name].dtype))
    for name, factor in factors.items():
        out[name] = (out[name] * factor).astype(out[name].dtype)
    return out
```

```python
from contextlib import ExitStack

import concourse.bass as bass
import numpy as np
from concourse import mybir

F32 = mybir.dt.float32
U32 = mybir.dt.uint32
ALU = mybir.AluOpType
ACT = mybir.ActivationFunctionType
AX = mybir.AxisListType

P = 128
D = 1024
KD = D // P
SEQ, NB, DEC = 1024, 8, 8
NS_ROWS = NB * DEC
PT = SEQ // P
ROWS_PAD = (PT + 1) * P
PAST = 2048
HEADS, KV, REP, HD = 8, 2, 4, 64
AW = HEADS * HD
W = 128
ROT = HD // 4
HALF = ROT // 2
SW = D - AW
GRP, CH, ST = 32, 16, 64
assert PT % 2 == 0
PAIRS = GRP // 2
L = 8
CK = SEQ // L
NC = CK + NB
IN_W = AW + 2 * KV * HD + SW
U_COL = AW + 2 * KV * HD
EH, KEYS, TOPK, QH = 8, 128, 16, 128
EPS = 1e-5
NEG = float(np.float32(-1e30))
SCALE = HD ** -0.5
TWO_PI = 2 * np.pi
PI_HI = 6.28125
PI_LO = TWO_PI - PI_HI
ROUND = 1.5 * 2.0 ** 23
PI_MAX = 3.1415925


class Count:

    def __init__(self, sem, step=1):
        self.sem, self.step = sem, step
        self.first = 2 if step == 1 else 1

    def prime(self, eng):
        assert self.step == 1
        eng.sem_inc(self.sem, 1)

    def mark(self, ins):
        ins.then_inc(self.sem, 16 if self.step >= 16 else 1)

    def of(self, eng, t):
        if isinstance(t, int) and t + self.first <= 0:
            return
        eng.wait_ge(self.sem, (t + self.first) * self.step)

    def held(self, eng, t):
        self.of(eng, t)
        eng.nop(nofuse=True)


class Steps:

    def __init__(self, sem):
        self.sem, self.n = sem, 0

    def mark(self, ins):
        self.n += 1
        ins.then_inc(self.sem, 1)
        return self.n

    def chain(self, eng, ins):
        self.mark(ins)
        eng.wait_ge(self.sem, self.n)


class Core:

    def __init__(self, nc, ctx, sems):
        self.nc, self.ctx, self.sems = nc, ctx, sems

    def sb(self, name, shape, dt=F32):
        return self.ctx.enter_context(self.nc.sbuf_tensor(name, shape, dt))

    def ps(self, name, shape):
        return self.ctx.enter_context(self.nc.psum_tensor(name, shape, F32))

    def sem(self, name):
        self.sems.append(self.nc.alloc_semaphore(name=name))
        return self.sems[-1]

    def count(self, name, step=1):
        return Count(self.sem(name), step)

    def steps(self, name):
        return Steps(self.sem(name))


def bcast(ap, n, dim):
    shape = list(ap.shape)
    return ap.unsqueeze(dim).to_broadcast(shape[:dim] + [n] + shape[dim:])


def mix_tokens(nc, sems, a, s, shared):
    with ExitStack() as ctx:
        c = Core(nc, ctx, sems)
        w_in = c.sb("w_in", [P, KD, IN_W])
        w_top, g_attn, ident, half = shared.w_top, shared.g_attn, shared.ident, shared.half
        b_in = c.sb("b_in", [P, IN_W])
        g_mix = c.sb("g_mix", [P, KD])
        sink = c.sb("sink", [P, HEADS])
        xt = c.sb("xt", [P, 2, D])
        rope = c.sb("rope", [P, 2, 2 * HALF])
        mask = c.sb("mask", [P, 2, 2 * W])
        xs = c.sb("xs", [P, D])
        xT = c.sb("xT", [P, KD, P])
        pj = c.sb("pj", [P, 2, IN_W])
        rt = c.sb("rt", [P, 4, HEADS + KV, HALF])
        qT = c.sb("qT", [P, REP, P])
        kT = c.sb("kT", [P, 2, P])
        vb = c.sb("vb", [P, 2, P])
        sc = c.sb("sc", [P, HEADS, 2 * W])
        pr = c.sb("pr", [P, HEADS, 2 * W])
        ptr = c.sb("ptr", [P, 2 * HEADS, P])
        at = c.sb("at", [P, AW])
        at2 = c.sb("at2", [P, AW])
        aT = c.sb("aT", [P, AW // P, P])
        small = c.sb("small_a", [P, 8, HEADS])
        stat = c.sb("stat_a", [P, 8])
        mx, nm, sd, es, rs, den, rden = (small[:, i, :] for i in range(7))
        ssx, msx, rsx, ssa, msa, rsa = (stat[:, i:i + 1] for i in range(6))

        PJ = c.ps("PJ", [P, 3, 512])
        SC = c.ps("SC", [P, 4, 2, 2 * W])
        X = c.ps("X", [P, 512])
        QK = SC[:, 2:4, :, :].rearrange("p b c n -> p (b c n)")
        SCf = SC[:, :, :, :].rearrange("p b c n -> p (b c n)")

        weights = c.sem("weights_in")
        kept = c.sem("kv_out")
        zeroed = c.sem("zeroed_a")
        tile_in = c.count("tile_in", 48)
        u_out = c.count("u_out", 16)
        x1_out = c.count("x1_out", 16)
        names = ("ssx_done rsx_done xs_done x_turned xT_done projected pj_done roped v_kept qk_turned "
                 "qkT_done scored maxed shifted probs_done p_turned ptr_act ptr_dve weighed at_done "
                 "ssa_done rsa_done at2_done a_turned aT_done mixed x1_done msx_done msa_done rope_mul "
                 "den_done rden_done").split()
        k = {n: c.count(n) for n in names}
        N_W = 8

        def load(eng, t, p):
            tile_in.mark(eng.dma_start(xt[:, p, :], a["x"][bass.ts(t, P), :]))
            tile_in.mark(eng.dma_start(rope[:, p, :], a["rope"][bass.ts(t, P), :]))
            tile_in.mark(eng.dma_start(mask[:, p, :], a["mask"][bass.ts(t, P), :]))

        with nc.Block() as block:

            @block.sync
            def _(sp):
                def prologue():
                    load(sp, 0, 0)
                    sp.dma_start(w_in[:], a["w_in"].rearrange("(k p) n -> p k n", p=P)).then_inc(weights, 16)
                    sp.dma_start(b_in[:], a["b_in"].to_broadcast([P, IN_W])).then_inc(weights, 16)
                    sp.dma_start(g_mix[:], a["g_mix"]).then_inc(weights, 16)
                    sp.dma_start(g_attn[:], a["g_attn"]).then_inc(weights, 16)
                    sp.dma_start(sink[:], a["sink"].to_broadcast([P, HEADS])).then_inc(weights, 16)
                    sp.dma_start(ident[:], a["ident"]).then_inc(weights, 16)
                    sp.dma_start(w_top[:], a["w_out"][0:AW, :].rearrange("(k p) n -> p k n", p=P)).then_inc(weights, 16)
                    sp.dma_start(half[:], a["minus_half"]).then_inc(weights, 16)

                def step(t, p):
                    load(sp, t + 1, 1 - p)
                    k["pj_done"].held(sp, t + 1)
                    u_out.mark(sp.dma_start(s["u"][bass.ts(t + 1, P), :], pj[:, 1 - p, U_COL:]))
                    k["x1_done"].held(sp, t)
                    x1_out.mark(sp.dma_start(s["x1"][bass.ts(t, P), :], xt[:, p, :]))
                    u_out.held(sp, t + 1)
                    x1_out.held(sp, t)

                prologue()
                k["pj_done"].held(sp, 0)
                u_out.mark(sp.dma_start(s["u"][0:P, :], pj[:, 0, U_COL:]))
                u_out.held(sp, 0)
                with sp.Fori(0, PT // 2) as i:
                    for p in range(2):
                        step(i * 2 + p, p)
                k["roped"].held(sp, PT)
                sp.dma_start(a["new_k_prompt"], pj[:, 1, AW:AW + KV * HD]).then_inc(kept, 16)
                sp.dma_start(a["new_v_prompt"], pj[:, 1, AW + KV * HD:U_COL]).then_inc(kept, 16)
                sp.dma_start(s["pj"], pj[0:NS_ROWS, 0, 0:U_COL]).then_inc(kept, 16)
                sp.dma_start(s["x_s"], xt[0:NS_ROWS, 0, :]).then_inc(kept, 16)
                sp.wait_ge(kept, 16 * 4)

            @block.gpsimd
            def _(pool):
                for n in ("roped", "rsx_done", "msx_done", "v_kept", "rsa_done", "msa_done", "rope_mul"):
                    k[n].prime(pool)

                def rstd(t, src, ms, out, width, ready, mid, done):
                    ready.held(pool, t)
                    mid.mark(pool.tensor_scalar(ms, src, 1.0 / width, EPS, ALU.mult, ALU.add))
                    mid.held(pool, t)
                    done.mark(pool.tensor_tensor(out, ms, half[:], ALU.pow))

                def rotate(t, p):
                    heads = pj[:, p, 0:AW + KV * HD].rearrange("p (h d) -> p h d", d=HD)
                    x1, x2 = heads[:, :, 0:HALF], heads[:, :, HALF:ROT]
                    cos = bcast(rope[:, p, 0:HALF], HEADS + KV, 1)
                    sin = bcast(rope[:, p, HALF:], HEADS + KV, 1)
                    k["pj_done"].held(pool, t)
                    k["roped"].held(pool, t - 1)
                    pool.tensor_tensor(rt[:, 0], x1, cos, ALU.mult)
                    pool.tensor_tensor(rt[:, 1], x2, sin, ALU.mult)
                    pool.tensor_tensor(rt[:, 2], x2, cos, ALU.mult)
                    k["rope_mul"].mark(pool.tensor_tensor(rt[:, 3], x1, sin, ALU.mult))
                    k["rope_mul"].held(pool, t)
                    pool.tensor_tensor(x1, rt[:, 0], rt[:, 1], ALU.subtract)
                    k["roped"].mark(pool.tensor_tensor(x2, rt[:, 2], rt[:, 3], ALU.add))

                def step(t, p):
                    k["weighed"].held(pool, t - 1)
                    k["v_kept"].mark(pool.tensor_copy(vb[:, p, :], pj[:, p, AW + KV * HD:U_COL]))
                    rstd(t + 1, ssx, msx, rsx, D, k["ssx_done"], k["msx_done"], k["rsx_done"])
                    rotate(t + 1, 1 - p)
                    rstd(t, ssa, msa, rsa, AW, k["ssa_done"], k["msa_done"], k["rsa_done"])

                pool.memset(kT[:, 1, :], 0.0).then_inc(zeroed, 1)
                pool.memset(vb[:, 1, :], 0.0).then_inc(zeroed, 1)
                pool.wait_ge(weights, 16 * N_W)
                rstd(0, ssx, msx, rsx, D, k["ssx_done"], k["msx_done"], k["rsx_done"])
                rotate(0, 0)
                with pool.Fori(0, PT // 2) as i:
                    for p in range(2):
                        step(i * 2 + p, p)

            @block.scalar
            def _(act):
                for n in ("ssx_done", "qkT_done", "probs_done", "ptr_act"):
                    k[n].prime(act)

                def squares(t, p):
                    tile_in.of(act, t)
                    k["x_turned"].of(act, t - 1)
                    k["ssx_done"].mark(nc.scalar.activation(xs[:], xt[:, p, :], ACT.Square, accum_out=ssx))

                def step(t, p):
                    k["qk_turned"].of(act, t)
                    k["scored"].of(act, t - 1)
                    act.wait_ge(zeroed, 2)
                    nc.scalar.activation(qT[:].rearrange("p r n -> p (r n)"), QK[:, 0:512], ACT.Copy)
                    k["qkT_done"].mark(nc.scalar.activation(kT[:, p, :], QK[:, 512:512 + P], ACT.Copy))
                    squares(t + 1, 1 - p)
                    k["shifted"].of(act, t)
                    k["p_turned"].of(act, t - 1)
                    k["den_done"].of(act, t - 1)
                    for h in range(HEADS):
                        nc.scalar.activation(pr[:, h, :], sc[:, h, :], ACT.Exp, bias=nm[:, h:h + 1],
                                             accum_out=rs[:, h:h + 1])
                    k["probs_done"].mark(nc.scalar.activation(es, sd, ACT.Exp))
                    k["p_turned"].of(act, t)
                    k["weighed"].of(act, t - 1)
                    nc.scalar.activation(ptr[:, 0:4, :].rearrange("p a n -> p (a n)"), SCf[:, 0:512], ACT.Copy)
                    k["ptr_act"].mark(nc.scalar.activation(
                        ptr[:, 4:8, :].rearrange("p a n -> p (a n)"), SCf[:, 512:1024], ACT.Copy))

                squares(0, 0)
                with act.Fori(0, PT // 2) as i:
                    for p in range(2):
                        step(i * 2 + p, p)

            @block.vector
            def _(dve):
                for n in ("xs_done", "xT_done", "pj_done", "maxed", "shifted", "ptr_dve", "at_done", "ssa_done",
                          "at2_done", "aT_done", "x1_done", "den_done", "rden_done"):
                    k[n].prime(dve)

                def project(t, p):
                    k["rsx_done"].of(dve, t)
                    k["ssx_done"].of(dve, t)
                    k["xs_done"].mark(nc.vector.tensor_scalar(xs[:], xt[:, p, :], rsx, None, ALU.mult))
                    k["x_turned"].of(dve, t)
                    k["projected"].of(dve, t - 1)
                    for b in range(2):
                        ins = nc.vector.tensor_tensor(
                            xT[:, 4 * b:4 * b + 4, :], PJ[:, b, :].rearrange("p (k n) -> p k n", n=P),
                            bcast(g_mix[:, 4 * b:4 * b + 4], P, 2), ALU.mult)
                    k["xT_done"].mark(ins)
                    k["projected"].of(dve, t)
                    tile_in.of(dve, t)
                    k["v_kept"].of(dve, t - 2)
                    for b, (lo, hi) in enumerate(((0, 512), (512, U_COL), (U_COL, IN_W))):
                        ins = nc.vector.tensor_tensor(pj[:, p, lo:hi], PJ[:, b, 0:hi - lo], b_in[:, lo:hi], ALU.add)
                    k["pj_done"].mark(ins)

                def step(t, p):
                    k["scored"].of(dve, t)
                    k["probs_done"].of(dve, t - 1)
                    tile_in.held(dve, t)
                    for h in range(HEADS):
                        ins = nc.vector.tensor_tensor_reduce(
                            sc[:, h, :], SC[:, h // 2, h % 2, :], mask[:, p, :], SCALE, sink[:, h:h + 1],
                            ALU.add, ALU.max, mx[:, h:h + 1])
                    k["maxed"].mark(ins)
                    k["maxed"].of(dve, t)
                    nc.vector.tensor_scalar(nm, mx, -1.0, None, ALU.mult)
                    k["shifted"].mark(nc.vector.tensor_tensor(sd, sink[:], mx, ALU.subtract))
                    project(t + 1, 1 - p)
                    k["probs_done"].of(dve, t)
                    k["at_done"].of(dve, t - 1)
                    k["den_done"].mark(nc.vector.tensor_tensor(den, rs, es, ALU.add))
                    k["den_done"].of(dve, t)
                    k["rden_done"].mark(nc.vector.reciprocal(rden, den))
                    k["p_turned"].of(dve, t)
                    k["weighed"].of(dve, t - 1)
                    nc.vector.tensor_copy(ptr[:, 8:12, :].rearrange("p a n -> p (a n)"), SCf[:, 1024:1536])
                    k["ptr_dve"].mark(nc.vector.tensor_copy(
                        ptr[:, 12:16, :].rearrange("p a n -> p (a n)"), SCf[:, 1536:2048]))
                    k["weighed"].of(dve, t)
                    k["rden_done"].of(dve, t)
                    k["at2_done"].of(dve, t - 1)
                    k["at_done"].mark(nc.vector.tensor_tensor(
                        at[:].rearrange("p (h d) -> p h d", d=HD), X[:].rearrange("p (h d) -> p h d", d=HD),
                        bcast(rden, HD, 2), ALU.mult))
                    k["at_done"].of(dve, t)
                    k["a_turned"].of(dve, t - 1)
                    k["ssa_done"].mark(nc.vector.tensor_tensor_reduce(at2[:], at[:], at[:], 1.0, 0.0,
                                                                      ALU.mult, ALU.add, ssa))
                    k["ssa_done"].of(dve, t)
                    k["rsa_done"].of(dve, t)
                    k["at2_done"].mark(nc.vector.tensor_scalar(at2[:], at[:], rsa, None, ALU.mult))
                    k["a_turned"].of(dve, t)
                    k["aT_done"].mark(nc.vector.tensor_tensor(
                        aT[:], X[:].rearrange("p (k n) -> p k n", n=P), bcast(g_attn[:], P, 2), ALU.mult))
                    k["mixed"].of(dve, t)
                    for b in range(2):
                        half_row = xt[:, p, 512 * b:512 * b + 512]
                        ins = nc.vector.tensor_tensor(half_row, PJ[:, b, :], half_row, ALU.add)
                    k["x1_done"].mark(ins)

                dve.wait_ge(weights, 16 * N_W)
                project(0, 0)
                with dve.Fori(0, PT // 2) as i:
                    for p in range(2):
                        step(i * 2 + p, p)

            @block.tensor
            def _(pe):
                for n in ("x_turned", "projected", "qk_turned", "scored", "p_turned", "weighed", "a_turned", "mixed"):
                    k[n].prime(pe)

                def project(t):
                    k["xs_done"].of(pe, t)
                    k["x1_done"].of(pe, t - 2)
                    k["pj_done"].of(pe, t - 1)
                    for j in range(KD):
                        ins = nc.tensor.transpose(PJ[:, j // 4, (j % 4) * P:(j % 4 + 1) * P],
                                                  xs[:, j * P:(j + 1) * P], ident[:])
                    k["x_turned"].mark(ins)
                    k["xT_done"].of(pe, t)
                    for b, (lo, hi) in enumerate(((0, 512), (512, U_COL), (U_COL, IN_W))):
                        for j in range(KD):
                            ins = nc.tensor.matmul(PJ[:, b, 0:hi - lo], xT[:, j, :], w_in[:, j, lo:hi],
                                                   start=(j == 0), stop=(j == KD - 1))
                    k["projected"].mark(ins)

                def step(t, p):
                    k["roped"].of(pe, t)
                    k["ptr_act"].of(pe, t - 1)
                    k["ptr_dve"].of(pe, t - 1)
                    for r in range(REP):
                        nc.tensor.transpose(QK[:, r * P:(r + 1) * P], pj[:, p, r * P:(r + 1) * P], ident[:])
                    k["qk_turned"].mark(nc.tensor.transpose(
                        QK[:, 512:512 + P], pj[:, p, AW:AW + KV * HD], ident[:]))
                    k["qkT_done"].of(pe, t)
                    for h in range(HEADS):
                        g, r = divmod(h, REP)
                        ins = nc.tensor.matmul(SC[:, h // 2, h % 2, :], qT[g * HD:(g + 1) * HD, r, :],
                                               kT[g * HD:(g + 1) * HD, :, :].rearrange("p a n -> p (a n)"),
                                               start=True, stop=True)
                    k["scored"].mark(ins)
                    project(t + 1)
                    k["probs_done"].of(pe, t)
                    k["maxed"].of(pe, t)
                    for h in range(HEADS):
                        for w in range(2):
                            n = 2 * h + w
                            ins = nc.tensor.transpose(SCf[:, n * P:(n + 1) * P], pr[:, h, w * W:(w + 1) * W], ident[:])
                    k["p_turned"].mark(ins)
                    k["ptr_act"].of(pe, t)
                    k["ptr_dve"].of(pe, t)
                    k["v_kept"].of(pe, t)
                    k["aT_done"].of(pe, t - 1)
                    for h in range(HEADS):
                        g = h // REP
                        for w in range(2):
                            ins = nc.tensor.matmul(X[:, h * HD:(h + 1) * HD], ptr[:, 2 * h + w, :],
                                                   vb[:, w, g * HD:(g + 1) * HD], start=(w == 0), stop=(w == 1))
                    k["weighed"].mark(ins)
                    k["at2_done"].of(pe, t)
                    for j in range(AW // P):
                        ins = nc.tensor.transpose(X[:, j * P:(j + 1) * P], at2[:, j * P:(j + 1) * P], ident[:])
                    k["a_turned"].mark(ins)
                    k["aT_done"].of(pe, t)
                    k["pj_done"].of(pe, t + 1)
                    for b in range(2):
                        for j in range(AW // P):
                            ins = nc.tensor.matmul(PJ[:, b, :], aT[:, j, :], w_top[:, j, 512 * b:512 * b + 512],
                                                   start=(j == 0), stop=(j == AW // P - 1))
                    k["mixed"].mark(ins)

                pe.wait_ge(weights, 16 * N_W)
                project(0)
                with pe.Fori(0, PT // 2) as i:
                    for p in range(2):
                        step(i * 2 + p, p)


class Once:

    def __init__(self, core, phase):
        self.core, self.phase, self.sems = core, phase, {}

    def __getitem__(self, name):
        if name not in self.sems:
            self.sems[name] = self.core.sem(f"{self.phase}_{name}")
        return self.sems[name]


def mix_samples(nc, sems, a, s, shared):
    with ExitStack() as ctx:
        c = Core(nc, ctx, sems)
        w_top, g_attn, ident, half = shared.w_top, shared.g_attn, shared.ident, shared.half
        R, NK = NS_ROWS, W + DEC
        qkv = c.sb("qkv_s", [R, U_COL])
        xr = c.sb("xr_s", [R, D])
        kc = c.sb("kc", [P, NB, P])
        vc = c.sb("vc", [P, NB, P])
        vn = c.sb("vn", [DEC, NB, P])
        mask = c.sb("mask_s", [P, NK])
        sink = c.sb("sink_s", [P, KV])
        qT = c.sb("qT_s", [P, NB, REP, DEC])
        kT = c.sb("kT_s", [P, NB, NK])
        sc = c.sb("sc_s", [P, 4, NK])
        pr = c.sb("pr_s", [P, 4, NK])
        ptb = c.sb("ptb", [P, 4, P])
        ptn = c.sb("ptn", [DEC, 4, P])
        small = c.sb("small_s", [P, 8, 4])
        stat = c.sb("stat_s", [P, 4])
        oS = c.sb("o_s", [P, 4, HD])
        at = c.sb("at_s", [R, AW])
        at2 = c.sb("at2_s", [R, AW])
        aT = c.sb("aT_s", [P, AW // P, R])
        zero = c.sb("zero_s", [R, D])
        mx, nm, sd, es, rs, den, rden = (small[:, i, :] for i in range(7))
        ss, ms, rstd = (stat[0:R, i:i + 1] for i in range(3))
        TR = c.ps("TR", [P, 512])
        KB = c.ps("KB", [P, NB, P])
        SS = c.ps("SS", [P, KV, 512])
        PO = c.ps("PO", [P, 2, 512])
        ev = Once(c, "s")
        loads, qkv_in, back_in, stores = c.sem("loads_s"), c.sem("qkv_in"), c.sem("back_in"), c.sem("stores_s")

        with nc.Block() as block:

            @block.sync
            def _(sp):
                sp.dma_start(qkv[:], s["pj"]).then_inc(qkv_in, 16)
                sp.dma_start(kc[:], a["cache_k"].rearrange("b j n -> j b n")).then_inc(loads, 16)
                sp.dma_start(vc[:], a["cache_v"].rearrange("b j n -> j b n")).then_inc(loads, 16)
                sp.dma_start(vn[:], s["pj"][:, AW + KV * HD:U_COL].rearrange("(b i) n -> i b n", i=DEC)).then_inc(loads, 16)
                sp.dma_start(mask[:], a["mask_s"]).then_inc(loads, 16)
                sp.dma_start(sink[:], a["sink_s"]).then_inc(loads, 16)
                sp.dma_start(xr[:], s["x_s"]).then_inc(loads, 16)
                for n, lo in (("k", AW), ("v", AW + KV * HD)):
                    out = a[f"new_{n}_sample"]
                    sp.dma_start(out[:, 0:W - DEC, :], a[f"cache_{n}"][:, DEC:W, :]).then_inc(stores, 16)
                    sp.dma_start(out[:, W - DEC:W, :], s["pj"][:, lo:lo + KV * HD].rearrange("(b i) n -> b i n", i=DEC)).then_inc(stores, 16)
                sp.wait_ge(ev["zero"], 1)
                sp.dma_start(s["x1"][SEQ + R:ROWS_PAD, :], zero[:]).then_inc(stores, 16)
                sp.dma_start(s["y_ssm"][SEQ + R:ROWS_PAD, :], zero[:, 0:SW]).then_inc(stores, 16)
                sp.wait_ge(ev["o_done"], 1)
                sp.dma_start(s["attn_s"], oS[:].rearrange("p n d -> p (n d)")).then_inc(ev["o_out"], 16)
                sp.wait_ge(ev["o_out"], 16)
                for b in range(NB):
                    for g in range(KV):
                        src = s["attn_s"][32 * (b % 4):32 * (b % 4) + 32, (2 * g + b // 4) * HD:(2 * g + b // 4 + 1) * HD]
                        sp.dma_start(at[b * DEC:(b + 1) * DEC, g * 256:(g + 1) * 256].rearrange("i (r d) -> i r d", d=HD),
                                     src.rearrange("(r i) d -> i r d", i=DEC)).then_inc(back_in, 16)
                sp.wait_ge(ev["x1"], 1)
                sp.dma_start(s["x1"][SEQ:SEQ + R, :], xr[:]).then_inc(stores, 16)
                sp.wait_ge(stores, 16 * 7)

            @block.gpsimd
            def _(pool):
                pool.memset(zero[:], 0.0).then_inc(ev["zero"], 1)
                pool.wait_ge(ev["ss"], 1)
                pool.tensor_scalar(ms, ss, 1.0 / AW, EPS, ALU.mult, ALU.add).then_inc(ev["ms"], 1)
                pool.wait_ge(ev["ms"], 1)
                pool.tensor_tensor(rstd, ms, half[0:R, :], ALU.pow).then_inc(ev["rstd"], 1)

            @block.scalar
            def _(act):
                act.wait_ge(ev["q_turned"], 1)
                nc.scalar.activation(qT[:], TR[:, 0:REP * R].rearrange("p (r b i) -> p b r i", r=REP, i=DEC), ACT.Copy)
                nc.scalar.activation(kT[:, :, W:NK], TR[:, REP * R:5 * R].rearrange("p (b i) -> p b i", i=DEC),
                                     ACT.Copy).then_inc(ev["qT"], 1)
                act.wait_ge(ev["shifted"], 1)
                for n in range(4):
                    nc.scalar.activation(pr[:, n, :], sc[:, n, :], ACT.Exp, bias=nm[:, n:n + 1], accum_out=rs[:, n:n + 1])
                nc.scalar.activation(es, sd, ACT.Exp).then_inc(ev["probs"], 1)
                act.wait_ge(ev["p_turned"], 1)
                nc.scalar.activation(ptb[:].rearrange("p n m -> p (n m)"), KB[:, 0:4, :].rearrange("p n m -> p (n m)"),
                                     ACT.Copy).then_inc(ev["ptb"], 1)
                nc.scalar.activation(ptn[:].rearrange("p n m -> p (n m)"),
                                     KB[0:DEC, 4:8, :].rearrange("p n m -> p (n m)"), ACT.Copy).then_inc(ev["ptn"], 1)

            @block.vector
            def _(dve):
                dve.wait_ge(ev["k_turned"], 1)
                nc.vector.tensor_copy(kT[:, :, 0:W], KB[:]).then_inc(ev["kT"], 1)
                dve.wait_ge(loads, 16 * 6)
                dve.wait_ge(ev["scored"], 1)
                for g in range(KV):
                    for hf in range(2):
                        n = 2 * g + hf
                        ins = nc.vector.tensor_tensor_reduce(
                            sc[:, n, :], SS[:, g, hf * NK:(hf + 1) * NK], mask[:], SCALE, sink[:, g:g + 1],
                            ALU.add, ALU.max, mx[:, n:n + 1])
                ins.then_inc(ev["maxed"], 1)
                dve.wait_ge(ev["maxed"], 1)
                nc.vector.tensor_scalar(nm, mx, -1.0, None, ALU.mult)
                nc.vector.tensor_tensor(sd.rearrange("p (g f) -> p g f", g=KV), bcast(sink[:], 2, 2),
                                        mx.rearrange("p (g f) -> p g f", g=KV), ALU.subtract).then_inc(ev["shifted"], 1)
                dve.wait_ge(ev["probs"], 1)
                nc.vector.tensor_tensor(den, rs, es, ALU.add).then_inc(ev["den"], 1)
                dve.wait_ge(ev["den"], 1)
                nc.vector.reciprocal(rden, den).then_inc(ev["rden"], 1)
                dve.wait_ge(ev["rden"], 1)
                dve.wait_ge(ev["weighed"], 1)
                nc.vector.tensor_tensor(oS[:], PO[:, 0, 0:4 * HD].rearrange("p (n d) -> p n d", d=HD),
                                        bcast(rden, HD, 2), ALU.mult).then_inc(ev["o_done"], 1)
                dve.wait_ge(back_in, 16 * NB * KV)
                nc.vector.tensor_tensor_reduce(at2[:], at[:], at[:], 1.0, 0.0, ALU.mult, ALU.add, ss).then_inc(ev["ss"], 1)
                dve.wait_ge(ev["ss"], 1)
                dve.wait_ge(ev["rstd"], 1)
                nc.vector.tensor_scalar(at2[:], at[:], rstd, None, ALU.mult).then_inc(ev["at2"], 1)
                dve.wait_ge(ev["a_turned"], 1)
                nc.vector.tensor_tensor(aT[:], TR[:, 0:4 * R].rearrange("p (k n) -> p k n", n=R), bcast(g_attn[:], R, 2),
                                        ALU.mult).then_inc(ev["aT"], 1)
                dve.wait_ge(ev["mixed"], 1)
                for b in range(2):
                    row = xr[:, 512 * b:512 * b + 512]
                    ins = nc.vector.tensor_tensor(row, PO[0:R, b, :], row, ALU.add)
                ins.then_inc(ev["x1"], 1)

            @block.tensor
            def _(pe):
                pe.wait_ge(qkv_in, 16)
                for r in range(5):
                    ins = nc.tensor.transpose(TR[:, r * R:(r + 1) * R], qkv[:, r * P:(r + 1) * P], ident[0:R, 0:R])
                ins.then_inc(ev["q_turned"], 1)
                pe.wait_ge(loads, 16 * 6)
                for b in range(NB):
                    ins = nc.tensor.transpose(KB[:, b, :], kc[:, b, :], ident[:])
                ins.then_inc(ev["k_turned"], 1)
                pe.wait_ge(ev["qT"], 1)
                pe.wait_ge(ev["kT"], 1)
                for g in range(KV):
                    for b in range(NB):
                        row = 32 * (b % 4)
                        ins = nc.tensor.matmul(SS[row:row + 32, g, (b // 4) * NK:(b // 4 + 1) * NK],
                                               qT[g * HD:(g + 1) * HD, b].rearrange("p r i -> p (r i)"),
                                               kT[g * HD:(g + 1) * HD, b, :], start=True, stop=True)
                ins.then_inc(ev["scored"], 1)
                pe.wait_ge(ev["probs"], 1)
                for n in range(4):
                    nc.tensor.transpose(KB[:, n, :], pr[:, n, 0:W], ident[:])
                for n in range(4):
                    ins = nc.tensor.transpose(KB[0:DEC, 4 + n, :], pr[:, n, W:NK], ident[:])
                ins.then_inc(ev["p_turned"], 1)
                pe.wait_ge(ev["ptb"], 1)
                pe.wait_ge(ev["ptn"], 1)
                for b in range(NB):
                    for g in range(KV):
                        n, row = 2 * g + b // 4, 32 * (b % 4)
                        out = PO[row:row + 32, 0, n * HD:(n + 1) * HD]
                        nc.tensor.matmul(out, ptb[:, n, row:row + 32], vc[:, b, g * HD:(g + 1) * HD], start=True, stop=False)
                        ins = nc.tensor.matmul(out, ptn[:, n, row:row + 32], vn[:, b, g * HD:(g + 1) * HD],
                                               start=False, stop=True)
                ins.then_inc(ev["weighed"], 1)
                pe.wait_ge(ev["at2"], 1)
                for j in range(AW // P):
                    ins = nc.tensor.transpose(TR[:, j * R:(j + 1) * R], at2[:, j * P:(j + 1) * P], ident[0:R, 0:R])
                ins.then_inc(ev["a_turned"], 1)
                pe.wait_ge(ev["aT"], 1)
                for b in range(2):
                    for j in range(AW // P):
                        ins = nc.tensor.matmul(PO[0:R, b, :], aT[:, j, :], w_top[:, j, 512 * b:512 * b + 512],
                                               start=(j == 0), stop=(j == AW // P - 1))
                ins.then_inc(ev["mixed"], 1)


class Shared:

    def __init__(self, c):
        self.w_top = c.sb("w_top", [P, AW // P, D])
        self.g_attn = c.sb("g_attn", [P, AW // P])
        self.ident = c.sb("ident", [P, P])
        self.half = c.sb("minus_half", [P, 1])


def run_ssm(nc, sems, a, s):
    with ExitStack() as ctx:
        c = Core(nc, ctx, sems)
        ident = c.sb("ident_c", [P, P])
        U2 = c.sb("U2", [P, L * SW])
        U2g = c.sb("U2g", [P, GRP * L * CH])
        Us = c.sb("Us", [NB, GRP, L, CH])
        XT = c.sb("XT", [P, GRP, NC])
        K16 = U2[0:CH, :].rearrange("p (g m) -> p g m", g=GRP)
        TOE = U2g[:].rearrange("p (g m) -> p g m", g=GRP)
        WBt = [c.sb(f"WBt_{x}", [P, PAIRS, P]) for x in "ri"]
        WB = [c.sb(f"WB_{x}", [P, PAIRS, P]) for x in "ri"]
        WC = [c.sb(f"WC_{x}", [P, PAIRS, (L + 1) * CH]) for x in "ri"]
        BU = [c.sb(f"BU_{x}", [P, PAIRS, NC]) for x in "ri"]
        G = [c.sb(f"G_{x}", [P, PAIRS, CK]) for x in "ri"]
        H = [c.sb(f"H_{x}", [P, PAIRS, NC + 1]) for x in "ri"]
        ROTt = WBt
        T1, T2 = (c.sb(f"T{i}", [P, PAIRS * (L + 1) * CH]) for i in (1, 2))
        lam = [c.sb(f"lam_{x}", [P, PAIRS]) for x in "ri"]
        lstep = c.sb("lstep", [P, PAIRS])
        Bm = [c.sb(f"Bm_{x}", [P, PAIRS, CH]) for x in "ri"]
        Cm = [c.sb(f"Cm_{x}", [P, PAIRS, CH]) for x in "ri"]
        BB = [c.sb(f"BB_{x}", [P, PAIRS, CH]) for x in "ri"]
        PW = [c.sb(f"PW_{x}", [P, L + 1, PAIRS]) for x in "ri"]
        PR = [c.sb(f"PR_{x}", [P, L, PAIRS]) for x in "ri"]
        h0 = [c.sb(f"h0_{x}", [P, PAIRS, NB]) for x in "ri"]
        HS = [c.sb(f"HS_{x}", [P, PAIRS, NB]) for x in "ri"]
        dsk = c.sb("dsk", [CH, GRP, CH])
        dd = c.sb("dd", [CH, GRP, CH])
        v = {n: c.sb(f"v_{n}", [P, PAIRS]) for n in
             "dt lrdt th mag mag8 k r1 r2 k2 sin cos den t t2 m1 zr zi ph k3 q1 q2 k4 us uc g1 g2".split()}
        tp1, tp2 = c.sb("tp1", [P, PAIRS * 64]), c.sb("tp2", [P, PAIRS * 64])
        PA = c.ps("PA", [P, 8, 512])
        ev = Once(c, "m")
        dv, ac, pl = c.steps("dve_steps"), c.steps("act_steps"), c.steps("pool_steps")
        loads, u_in, us_in, toe, stores = (c.sem(n) for n in ("loads_m", "u_in", "us_in", "toe_in", "stores_m"))
        copied = c.sem("bu_copied")
        y_copied = c.sem("y_copied")

        def tell(eng, name):
            eng.sem_inc(ev[name], 1)

        def mul(eng, st, dst, x, y, t1, t2, part, neg=False):
            if part == 0:
                eng.tensor_tensor(t1, x[0], y[0], ALU.mult)
                st.chain(eng, eng.tensor_tensor(t2, x[1], y[1], ALU.mult))
                st.chain(eng, eng.tensor_tensor(dst, t1, t2, ALU.subtract))
                return
            eng.tensor_tensor(t1, x[0], y[1], ALU.mult)
            st.chain(eng, eng.tensor_tensor(t2, x[1], y[0], ALU.mult))
            if neg:
                st.chain(eng, eng.scalar_tensor_tensor(dst, t1, -1.0, t2, ALU.mult, ALU.subtract))
            else:
                st.chain(eng, eng.tensor_tensor(dst, t1, t2, ALU.add))

        def reduce_angle(eng, st, r, k, x, quarter):
            st.chain(eng, eng.tensor_scalar(k, x, 1.0 / TWO_PI, 0.25 if quarter else 0.0, ALU.mult, ALU.add))
            st.chain(eng, eng.tensor_scalar(k, k, ROUND, None, ALU.add))
            st.chain(eng, eng.tensor_scalar(k, k, ROUND, None, ALU.subtract))
            st.chain(eng, eng.scalar_tensor_tensor(r, k, -PI_HI, x, ALU.mult, ALU.add))
            st.chain(eng, eng.scalar_tensor_tensor(r, k, -PI_LO, r, ALU.mult, ALU.add))
            if quarter:
                st.chain(eng, eng.tensor_scalar(r, r, float(np.float32(np.pi / 2)), None, ALU.add))
            st.chain(eng, eng.tensor_scalar(r, r, PI_MAX, -PI_MAX, ALU.min, ALU.max))

        with nc.Block() as block:

            @block.sync
            def _(sp):
                sp.dma_start(lstep[:], a["log_step"]).then_inc(loads, 16)
                for x, part in enumerate(("re", "im")):
                    sp.dma_start(lam[x][:], a[f"lam_{part}"]).then_inc(loads, 16)
                    sp.dma_start(Bm[x][:], a[f"b_{part}"]).then_inc(loads, 16)
                    sp.dma_start(Cm[x][:], a[f"c_{part}"]).then_inc(loads, 16)
                    sp.dma_start(h0[x][:], a[f"h0_{part}"]).then_inc(loads, 16)
                sp.dma_start(dsk[:].rearrange("p g c -> p (g c)"), a["d_skip"].to_broadcast([CH, SW])).then_inc(loads, 16)
                sp.dma_start(ident[:], a["ident"]).then_inc(loads, 16)
                sp.dma_start(U2[:], s["u"][0:SEQ, :].rearrange("(c j) n -> c (j n)", j=L)).then_inc(u_in, 16)
                for j in range(L):
                    src = s["u"][SEQ:SEQ + NS_ROWS, :].rearrange("(b j) (g n) -> j b g n", j=L, n=CH)
                    sp.dma_start(Us[:, :, j, :], src[j]).then_inc(us_in, 16)
                sp.wait_ge(ev["k16"], 1)
                sp.wait_ge(ev["toe_zero"], 1)
                for j in range(L):
                    sp.dma_start(TOE[j * CH:(j + 1) * CH, :, j * CH:], K16[:, :, 0:(L - j) * CH]).then_inc(toe, 16)
                sp.wait_ge(ev["h_prompt"], 1)
                sp.dma_start(a["ssm_re_prompt"], v["g1"][:]).then_inc(stores, 16)
                sp.dma_start(a["ssm_im_prompt"], v["g2"][:]).then_inc(stores, 16)
                sp.wait_ge(ev["h_sample"], 1)
                sp.dma_start(a["ssm_re_sample"], HS[0][:]).then_inc(stores, 16)
                sp.dma_start(a["ssm_im_sample"], HS[1][:]).then_inc(stores, 16)
                sp.wait_ge(y_copied, 8)
                sp.dma_start(s["y_ssm"][0:SEQ, :].rearrange("(c j) n -> c (j n)", j=L), U2[:]).then_inc(stores, 16)
                sp.wait_ge(y_copied, 16)
                sp.dma_start(s["y_ssm"][SEQ:SEQ + NS_ROWS, :].rearrange("(b j) n -> b (j n)", j=L),
                             Us[:].rearrange("b g j n -> b (g j n)")).then_inc(stores, 16)
                sp.wait_ge(stores, 16 * 6)

            @block.gpsimd
            def _(pool):
                pool.wait_ge(ev["unit"], 1)
                pool.wait_ge(ev["wb_turned"], 1)
                pool.tensor_copy(ROTt[0][:, :, 0:1].rearrange("p q o -> p (q o)"), v["uc"][:])
                pl.chain(pool, pool.tensor_copy(ROTt[1][:, :, 0:1].rearrange("p q o -> p (q o)"), v["us"][:]))
                n = 1
                while n < CK:
                    x = [bcast(ROTt[i][:, :, n - 1], n, 2) for i in range(2)]
                    y = [ROTt[i][:, :, 0:n] for i in range(2)]
                    t1, t2 = (t[:, 0:PAIRS * n].rearrange("p (q n) -> p q n", n=n) for t in (tp1, tp2))
                    mul(pool, pl, ROTt[0][:, :, n:2 * n], x, y, t1, t2, 0)
                    mul(pool, pl, ROTt[1][:, :, n:2 * n], x, y, t1, t2, 1)
                    n *= 2
                tell(pool, "rot")
                pool.wait_ge(ev["u_turned"], 8)
                pool.memset(U2g[:], 0.0).then_inc(ev["toe_zero"], 1)

            @block.scalar
            def _(act):
                def f(dst, src, func, **kw):
                    ac.chain(act, nc.scalar.activation(dst, src, func, **kw))

                act.wait_ge(loads, 16 * 11)
                f(v["dt"][:], lstep[:], ACT.Exp)
                tell(act, "dt")
                act.wait_ge(ev["angle"], 1)
                nc.scalar.activation(v["mag8"][:], v["lrdt"][:], ACT.Exp, scale=float(L))
                nc.scalar.activation(v["mag"][:], v["lrdt"][:], ACT.Exp).then_inc(ev["mag"], 1)
                nc.scalar.activation(v["sin"][:], v["r1"][:], ACT.Sin)
                nc.scalar.activation(v["cos"][:], v["r2"][:], ACT.Sin).then_inc(ev["sincos"], 1)
                act.wait_ge(ev["phase"], 1)
                nc.scalar.activation(v["us"][:], v["q1"][:], ACT.Sin)
                nc.scalar.activation(v["uc"][:], v["q2"][:], ACT.Sin).then_inc(ev["unit"], 1)
                act.wait_ge(u_in, 16)
                nc.scalar.activation(U2g[:].rearrange("p (g j n) -> p j g n", j=L, n=CH),
                                     U2[:].rearrange("p (j g n) -> p j g n", j=L, n=CH), ACT.Copy).then_inc(ev["u_grouped"], 1)
                for b in range(8):
                    act.wait_ge(ev["u_turned"], b + 1)
                    nc.scalar.activation(XT[:, 4 * b:4 * b + 4, 0:CK], PA[:, b, :].rearrange("p (g n) -> p g n", n=CK),
                                         ACT.Copy).then_inc(ev["xt"], 1)
                act.wait_ge(ev["us_turned"], 1)
                nc.scalar.activation(XT[:, :, CK:NC], PA[:, 0, 0:GRP * NB].rearrange("p (g n) -> p g n", n=NB),
                                     ACT.Copy).then_inc(ev["xt"], 1)
                for b in range(8):
                    act.wait_ge(ev["wb_part"], b + 1)
                    nc.scalar.activation(WB[b // 4][:, 4 * (b % 4):4 * (b % 4) + 4, :],
                                         PA[:, b, :].rearrange("p (q n) -> p q n", n=P), ACT.Copy).then_inc(ev["wb"], 1)
                act.wait_ge(ev["k_done"], 1)
                for b in range(8):
                    ins = nc.scalar.activation(
                        K16.rearrange("p (q s) m -> p s q m", s=2)[:, b // 4, 4 * (b % 4):4 * (b % 4) + 4, :],
                        PA[0:CH, b, :].rearrange("p (q n) -> p q n", n=P), ACT.Copy)
                ins.then_inc(ev["k_copied"], 1)
                for n in range(12):
                    x, q = n // 6, 3 * (n % 6)
                    w = min(3, PAIRS - q)
                    act.wait_ge(ev["bu_part"], n + 1)
                    nc.scalar.activation(BU[x][:, q:q + w, :], PA[:, n % 8, 0:w * NC].rearrange("p (q n) -> p q n", n=NC),
                                         ACT.Copy).then_inc(copied, 1)
                act.wait_ge(toe, 16 * L)
                for b in range(8):
                    act.wait_ge(ev["y_part"], b + 1)
                    out = U2[:].rearrange("p (j q s n) -> p s q j n", j=L, q=PAIRS, s=2)[:, b // 4, 4 * (b % 4):4 * (b % 4) + 4]
                    nc.scalar.activation(out, PA[:, b, :].rearrange("p (q j n) -> p q j n", q=4, j=L),
                                         ACT.Copy).then_inc(y_copied, 1)
                for b in range(8):
                    act.wait_ge(ev["ys_part"], b + 1)
                    out = Us[:].rearrange("b g j n -> b (g j n)").rearrange(
                        "p (j q s n) -> p s q j n", j=L, q=PAIRS, s=2)[:, b // 4, 4 * (b % 4):4 * (b % 4) + 4]
                    nc.scalar.activation(out, PA[0:NB, b, :].rearrange("p (q j n) -> p q j n", q=4, j=L),
                                         ACT.Copy).then_inc(y_copied, 1)

            @block.vector
            def _(dve):
                tt, ts = nc.vector.tensor_tensor, nc.vector.tensor_scalar

                def link(ins):
                    dv.chain(dve, ins)

                dve.wait_ge(loads, 16 * 11)
                dve.wait_ge(ev["dt"], 1)
                lr, li = lam[0][:], lam[1][:]
                tt(v["lrdt"][:], lr, v["dt"][:], ALU.mult)
                link(tt(v["th"][:], li, v["dt"][:], ALU.mult))
                reduce_angle(dve, dv, v["r1"][:], v["k"][:], v["th"][:], False)
                reduce_angle(dve, dv, v["r2"][:], v["k2"][:], v["th"][:], True)
                link(ts(v["ph"][:], v["r1"][:], float(L), None, ALU.mult))
                tell(dve, "angle")
                reduce_angle(dve, dv, v["q1"][:], v["k3"][:], v["ph"][:], False)
                reduce_angle(dve, dv, v["q2"][:], v["k4"][:], v["ph"][:], True)
                tell(dve, "phase")
                dve.wait_ge(ev["mag"], 1)
                dve.wait_ge(ev["sincos"], 1)
                nc.vector.memset(PW[0][:, 0, :], 1.0)
                nc.vector.memset(PW[1][:, 0, :], 0.0)
                tt(PW[0][:, 1, :], v["mag"][:], v["cos"][:], ALU.mult)
                link(tt(PW[1][:, 1, :], v["mag"][:], v["sin"][:], ALU.mult))
                ab = [PW[i][:, 1, :] for i in range(2)]
                for n in (1, 2, 4):
                    x = [bcast(PW[i][:, n, :], n, 1) for i in range(2)]
                    y = [PW[i][:, 1:n + 1, :] for i in range(2)]
                    t1, t2 = (t[:, 0:n * PAIRS].rearrange("p (n q) -> p n q", n=n) for t in (T1, T2))
                    mul(nc.vector, dv, PW[0][:, n + 1:2 * n + 1, :], x, y, t1, t2, 0)
                    mul(nc.vector, dv, PW[1][:, n + 1:2 * n + 1, :], x, y, t1, t2, 1)
                for i in range(2):
                    for j in range(L):
                        ins = nc.vector.tensor_copy(PR[i][:, j, :], PW[i][:, L - 1 - j, :])
                link(ins)
                tt(v["t"][:], lr, lr, ALU.mult)
                link(tt(v["t2"][:], li, li, ALU.mult))
                link(tt(v["den"][:], v["t"][:], v["t2"][:], ALU.add))
                link(nc.vector.reciprocal(v["den"][:], v["den"][:]))
                link(ts(v["m1"][:], ab[0], 1.0, None, ALU.subtract))
                tt(v["t"][:], v["m1"][:], lr, ALU.mult)
                link(tt(v["t2"][:], ab[1], li, ALU.mult))
                link(tt(v["zr"][:], v["t"][:], v["t2"][:], ALU.add))
                tt(v["t"][:], ab[1], lr, ALU.mult)
                link(tt(v["t2"][:], v["m1"][:], li, ALU.mult))
                link(tt(v["zi"][:], v["t"][:], v["t2"][:], ALU.subtract))
                tt(v["zr"][:], v["zr"][:], v["den"][:], ALU.mult)
                link(tt(v["zi"][:], v["zi"][:], v["den"][:], ALU.mult))
                z = [bcast(v["zr"][:], CH, 2), bcast(v["zi"][:], CH, 2)]
                t1, t2 = (t[:, 0:PAIRS * CH].rearrange("p (q n) -> p q n", n=CH) for t in (T1, T2))
                mul(nc.vector, dv, BB[0][:], z, [m[:] for m in Bm], t1, t2, 0)
                mul(nc.vector, dv, BB[1][:], z, [m[:] for m in Bm], t1, t2, 1)
                x = [bcast(PR[i][:].rearrange("p t q -> p q t"), CH, 3) for i in range(2)]
                y = [bcast(BB[i][:], L, 2) for i in range(2)]
                t1, t2 = (t[:, 0:PAIRS * P].rearrange("p (q t n) -> p q t n", t=L, n=CH) for t in (T1, T2))
                for i in range(2):
                    mul(nc.vector, dv, WBt[i][:].rearrange("p q (t n) -> p q t n", n=CH), x, y, t1, t2, i)
                    tell(dve, "wbt")
                x = [bcast(PW[i][:].rearrange("p t q -> p q t"), CH, 3) for i in range(2)]
                y = [bcast(Cm[i][:], L + 1, 2) for i in range(2)]
                t1, t2 = (t[:].rearrange("p (q t n) -> p q t n", t=L + 1, n=CH) for t in (T1, T2))
                mul(nc.vector, dv, WC[0][:].rearrange("p q (t n) -> p q t n", n=CH), x, y, t1, t2, 0)
                nc.vector.tensor_tensor(t1, x[0], y[1], ALU.mult)
                link(nc.vector.tensor_tensor(t2, x[1], y[0], ALU.mult))
                nc.vector.scalar_tensor_tensor(WC[1][:].rearrange("p q m -> p (q m)"), T1[:], -1.0, T2[:],
                                               ALU.mult, ALU.subtract).then_inc(ev["wc"], 1)
                for i in range(2):
                    nc.vector.memset(H[i][:, :, 0:1], 0.0)
                    ins = nc.vector.tensor_copy(H[i][:, :, CK + 1:NC + 1], h0[i][:])
                link(ins)
                link(tt(dd[:], dsk[:], bcast(ident[0:CH, 0:CH], GRP, 1), ALU.mult))
                dve.wait_ge(ev["k_copied"], 1)
                tt(K16[:, :, 0:CH], K16[:, :, 0:CH], dd[:], ALU.add).then_inc(ev["k16"], 1)
                dve.wait_ge(copied, 12)
                dve.wait_ge(ev["rot"], 1)
                dve.wait_ge(ev["wc"], 1)
                rot = [r[:] for r in ROTt]
                bu = [b[:, :, 0:CK] for b in BU]
                t1, t2 = (t[:, 0:PAIRS * CK].rearrange("p (q n) -> p q n", n=CK) for t in (T1, T2))
                tt(t1, rot[0], bu[0], ALU.mult)
                link(tt(t2, rot[1], bu[1], ALU.mult))
                link(tt(G[0][:], t1, t2, ALU.add))
                tt(t1, rot[0], bu[1], ALU.mult)
                link(tt(t2, rot[1], bu[0], ALU.mult))
                link(tt(G[1][:], t1, t2, ALU.subtract))
                for i in range(2):
                    for q in range(PAIRS):
                        ins = nc.vector.tensor_tensor_scan(G[i][:, q, :], v["mag8"][:, q:q + 1].to_broadcast([P, CK]),
                                                           G[i][:, q, :], 0.0, ALU.mult, ALU.add)
                link(ins)
                g = [x[:] for x in G]
                for i in range(2):
                    mul(nc.vector, dv, H[i][:, :, 1:CK + 1], rot, g, t1, t2, i)
                tell(dve, "h")
                nc.vector.tensor_copy(v["g1"][:], H[0][:, :, CK])
                nc.vector.tensor_copy(v["g2"][:], H[1][:, :, CK]).then_inc(ev["h_prompt"], 1)
                x = [bcast(PW[i][:, L, :], NB, 2) for i in range(2)]
                y = [h0[i][:] for i in range(2)]
                t1, t2 = (t[:, 0:PAIRS * NB].rearrange("p (q n) -> p q n", n=NB) for t in (T1, T2))
                for i in range(2):
                    mul(nc.vector, dv, HS[i][:], x, y, t1, t2, i)
                    link(tt(HS[i][:], HS[i][:], BU[i][:, :, CK:NC], ALU.add))
                tell(dve, "h_sample")

            @block.tensor
            def _(pe):
                pe.wait_ge(loads, 16 * 11)
                pe.wait_ge(ev["u_grouped"], 1)
                for g in range(GRP):
                    ins = nc.tensor.transpose(PA[:, g // 4, (g % 4) * P:(g % 4 + 1) * P], U2g[:, g * P:(g + 1) * P], ident[:])
                    if g % 4 == 3:
                        ins.then_inc(ev["u_turned"], 1)
                pe.wait_ge(us_in, 16 * L)
                pe.wait_ge(ev["xt"], 1)
                for g in range(GRP):
                    ins = nc.tensor.transpose(PA[:, 0, g * NB:(g + 1) * NB], Us[:, g].rearrange("b j n -> b (j n)"),
                                              ident[0:NB, 0:NB])
                ins.then_inc(ev["us_turned"], 1)
                pe.wait_ge(ev["xt"], 9)
                for b in range(8):
                    pe.wait_ge(ev["wbt"], b // 4 + 1)
                    for n in range(4):
                        q = 4 * (b % 4) + n
                        ins = nc.tensor.transpose(PA[:, b, n * P:(n + 1) * P], WBt[b // 4][:, q, :], ident[:])
                    ins.then_inc(ev["wb_part"], 1)
                pe.wait_ge(ev["wb"], 8)
                tell(pe, "wb_turned")
                pe.wait_ge(ev["wc"], 1)
                for q in range(PAIRS):
                    for h in range(2):
                        rows = slice(h * ST, (h + 1) * ST)
                        out = PA[0:CH, 4 * h + q // 4, (q % 4) * P:(q % 4 + 1) * P]
                        for i in range(2):
                            ins = nc.tensor.matmul(out, BB[i][rows, q, :], WC[i][rows, q, 0:P], start=(i == 0), stop=(i == 1))
                ins.then_inc(ev["k_done"], 1)
                pe.wait_ge(ev["k_copied"], 1)
                for n in range(12):
                    x, q0 = n // 6, 3 * (n % 6)
                    if n >= 8:
                        pe.wait_ge(copied, n - 7)
                    for q in range(q0, min(q0 + 3, PAIRS)):
                        for h in range(2):
                            rows = slice(h * ST, (h + 1) * ST)
                            ins = nc.tensor.matmul(PA[rows, n % 8, (q - q0) * NC:(q - q0 + 1) * NC],
                                                   WB[x][:, q, rows], XT[:, 2 * q + h, :], start=True, stop=True)
                    ins.then_inc(ev["bu_part"], 1)
                pe.wait_ge(copied, 12)
                pe.wait_ge(ev["h"], 1)
                pe.wait_ge(toe, 16 * L)

                def outputs(b, lo, hi, xlo, part):
                    h = b // 4
                    rows = slice(h * ST, (h + 1) * ST)
                    for n in range(4):
                        q = 4 * (b % 4) + n
                        out = PA[0:hi - lo, b, n * P:(n + 1) * P]
                        nc.tensor.matmul(out, XT[:, 2 * q + h, xlo:xlo + hi - lo], TOE[:, 2 * q + h, :], start=True, stop=False)
                        nc.tensor.matmul(out, H[0][rows, q, lo:hi], WC[0][rows, q, CH:], start=False, stop=False)
                        ins = nc.tensor.matmul(out, H[1][rows, q, lo:hi], WC[1][rows, q, CH:], start=False, stop=True)
                    ins.then_inc(part, 1)

                for b in range(8):
                    outputs(b, 0, CK, 0, ev["y_part"])
                for b in range(8):
                    pe.wait_ge(y_copied, b + 1)
                    outputs(b, CK + 1, NC + 1, CK, ev["ys_part"])


class PerTile:

    def __init__(self, sem):
        self.sem, self.n, self.per = sem, 0, None

    def chain(self, eng, t, ins, nop=False):
        self.n += 1
        ins.then_inc(self.sem, 1)
        eng.wait_ge(self.sem, self.n if self.per is None else t * self.per + self.n)
        if nop:
            eng.nop(nofuse=True)

    def tile_ends(self):
        assert self.per in (None, self.n), (self.per, self.n)
        self.per, self.n = self.n, 0


def retrieve_experts(nc, sems, a, s):
    with ExitStack() as ctx:
        c = Core(nc, ctx, sems)
        KS, NSLOT, UR, VR, DG = TOPK, EH * TOPK, 8, 4, 4
        HC = 2 * EH
        BLOCKS = ((0, 2, 16), (2, 4, 5), (4, 8, 3), (8, 16, 1))
        NCAND = sum((a1 - a0) * b for a0, a1, b in BLOCKS)
        LOWEST = float(np.finfo(np.float32).min)
        wq = c.sb("wq", [P, KD, EH * 2 * QH])
        keys = c.sb("keys", [QH, HC, KEYS])
        w_bot = c.sb("w_bot", [P, SW // P, D])
        w_glu = c.sb("w_glu", [P, SW // P, SW])
        b_glu = c.sb("b_glu", [P, SW])
        g_ffn = c.sb("g_ffn", [P, D])
        g_fin = c.sb("g_fin", [P, D])
        g_ssm = c.sb("g_ssm", [P, SW // P])
        ident = c.sb("ident_d", [P, P])
        place = c.sb("place", [P, NCAND])
        u_ring = c.sb("u_ring", [P, UR, D])
        v_ring = c.sb("v_ring", [P, VR, D])
        xr = c.sb("xr", [P, D])
        xn_next = c.sb("xn_next", [P, D])
        xn = c.sb("xn", [P, D])
        xo = c.sb("xo", [P, D])
        xnT = c.sb("xnT", [P, KD, P])
        qT = c.sb("qTe", [P, EH, P])
        S = c.sb("S", [P, EH, KEYS])
        y = c.sb("y", [P, SW])
        z = c.sb("z", [P, SW])
        yT = c.sb("yT", [P, SW // P, P])
        dg = c.sb("dg", [P, DG, P])
        top_v = c.sb("top_v", [P, EH, 2, KS])
        top_i = c.sb("top_i", [P, EH, 2, KS], U32)
        top_f = c.sb("top_f", [P, EH, 2, KS])
        left = c.sb("left", [P, KEYS])
        cand = c.sb("cand", [P, EH, NCAND])
        cid = c.sb("cid", [P, EH, NCAND])
        best = c.sb("best", [P, EH, KS])
        pos = c.sb("pos", [P, EH, KS], U32)
        pos_f = c.sb("pos_f", [P, EH, KS])
        idx_f = c.sb("idx_f", [P, EH, KS])
        idx_next = c.sb("idx_next", [P, NSLOT], U32)
        idx_u = c.sb("idx_u", [P, NSLOT], U32)
        idx_v = c.sb("idx_v", [P, NSLOT], U32)
        ex = c.sb("ex", [P, EH, KS])
        gate_next = c.sb("gate_next", [P, NSLOT])
        gate = c.sb("gate", [P, NSLOT])
        dot = c.sb("dot", [P, NSLOT])
        act_w = c.sb("act_w", [P, NSLOT])
        wgt = c.sb("wgt", [P, NSLOT])
        stat = c.sb("stat_e", [P, 16])
        nmax, esum = c.sb("nmax", [P, EH]), c.sb("esum", [P, EH])
        match = S[:].rearrange("p h n -> p (h n)")[:, 0:KS * NCAND].rearrange("p (k n) -> p k n", n=NCAND)
        squares = S[:].rearrange("p h n -> p (h n)")
        (ss_y, ms_y, sd_y, rs_y, ss_x, ms_x, sd_x, rs_x, ss_o, ms_o, sd_o, rs_o) = (stat[:, i:i + 1] for i in range(12))
        ACC = c.ps("ACC", [P, 2, 512])
        TQ = c.ps("TQ", [P, 2, 512])
        ZS = c.ps("ZS", [P, 2, 512])
        OP = c.ps("OP", [P, 2, 512])
        acc = ACC[:].rearrange("p b n -> p (b n)")

        weights = c.sem("weights_e")
        early = c.sem("weights_e1")
        rows_in = c.count("rows_in", 32)
        stored = c.sem("stored_e")
        k = {n: c.count(n) for n in (
            "y_gelu y_turned yT_done z_done zb_done gate_y sd_y_done yn_done yn_turned ynT_done bot_done xr_done "
            "sd_x_done xn_done xn_turned xnT_done q_a q_b q_c q_d qT_a qT_b qT_c qT_d s_a s_b S_a S_b topped_a topped_b "
            "idx_ready nmax_done ex_done gate_ready idx_taken idx_v_taken xn_taken acc_begun acc_taken "
            "ss_o_done ms_y_done ms_x_done ms_o_done sd_o_done out_ready out_stored").split()}
        u_in = [c.sem(f"u_in{i}") for i in range(UR)]
        v_in = [c.sem(f"v_in{i}") for i in range(VR)]
        dots = c.sem("dots_done")
        pv = c.sem("v_used")
        gelus, wgts, diags = c.sem("gelus"), c.sem("weights_done"), c.sem("diags_done")
        dch = PerTile(c.sem("dve_steps_e"))

        def ring_in(eng, sems, t, s_):
            n = len(sems)
            eng.wait_ge(sems[s_ % n], t * (16 * NSLOT // n) + 16 * (s_ // n + 1))

        with nc.Block() as block:

            @block.sync
            def _(sp):
                def rows(t):
                    k["acc_begun"].held(sp, t - 1)
                    k["yn_turned"].held(sp, t - 1)
                    rows_in.mark(sp.dma_start(y[:], s["y_ssm"][bass.ts(t, P), :]))
                    rows_in.mark(sp.dma_start(xr[:], s["x1"][bass.ts(t, P), :]))

                def out(t, n):
                    k["out_ready"].held(sp, t)
                    dst = a["y"][bass.ts(t, P), :] if n == P else a["y"][SEQ:SEQ + n, :]
                    sp.dma_start(dst, xo[0:n, :]).then_inc(stored, 16)
                    sp.wait_ge(stored, (t + 1) * 16)
                    sp.nop(nofuse=True)
                    sp.sem_inc(k["out_stored"].sem, 1)

                k["out_stored"].prime(sp)
                rows(0)
                sp.dma_start(ident[:], a["ident"]).then_inc(early, 16)
                sp.dma_start(w_glu[:], a["w_glu"].rearrange("(k p) n -> p k n", p=P)).then_inc(early, 16)
                sp.dma_start(b_glu[:], a["b_glu"].to_broadcast([P, SW])).then_inc(early, 16)
                sp.dma_start(g_ssm[:], a["g_ssm"]).then_inc(early, 16)
                sp.dma_start(w_bot[:], a["w_out"][AW:D, :].rearrange("(k p) n -> p k n", p=P)).then_inc(weights, 16)
                sp.dma_start(g_ffn[:], a["g_ffn"].to_broadcast([P, D])).then_inc(weights, 16)
                sp.dma_start(g_fin[:], a["g_final"].to_broadcast([P, D])).then_inc(weights, 16)
                sp.dma_start(place[:], a["place"].to_broadcast([P, NCAND])).then_inc(weights, 16)
                sp.dma_start(keys[:].rearrange("d c n -> d (c n)"), a["keys"]).then_inc(weights, 16)
                sp.dma_start(wq[:], a["w_query"].rearrange("(k p) n -> p k n", p=P)).then_inc(weights, 16)
                with sp.Fori(0, PT) as t:
                    rows(t + 1)
                    out(t, P)
                out(PT, NS_ROWS)

            @block.gpsimd
            def _(pool):
                def take_indices(t, n):
                    k["idx_ready"].held(pool, t)
                    k["idx_taken"].mark(pool.tensor_copy(idx_u[0:n, :], idx_next[0:n, :]))
                    k["idx_taken"].held(pool, t)

                def gather(ring, table, idx, sems, s_, n):
                    pool.indirect_dma_start(
                        out=ring[0:n, s_ % len(sems), :], out_offset=None, in_=a[table],
                        in_offset=bass.IndirectOffsetOnAxis(ap=idx[0:n, s_:s_ + 1], axis=0)).then_inc(sems[s_ % len(sems)], 16)

                def retrieve(t, n, tail):
                    for h in range(EH + 1):
                        for j in range(KS):
                            if h < EH:
                                s_ = KS * h + j
                                pool.wait_ge(dots, t * NSLOT + s_ + 1)
                                pool.nop(nofuse=True)
                                gather(u_ring, "u_table", idx_u, u_in, s_, n)
                            if (h, j) == (0, KS // 2):
                                pool.wait_ge(pv, t * NSLOT + VR)
                                pool.nop(nofuse=True)
                                k["idx_v_taken"].mark(pool.tensor_copy(idx_v[0:n, :], idx_u[0:n, :]))
                                k["idx_v_taken"].held(pool, t)
                            if h > 0:
                                s_ = KS * (h - 1) + j
                                pool.wait_ge(pv, t * NSLOT + s_ + 1)
                                pool.nop(nofuse=True)
                                gather(v_ring, "v_table", idx_v, v_in, s_, n)
                    if tail:
                        pool.wait_ge(dots, (t + 1) * NSLOT + UR)
                        pool.nop(nofuse=True)
                        take_indices(t + 1, P)

                k["idx_taken"].prime(pool)
                k["idx_v_taken"].prime(pool)
                take_indices(0, P)
                with pool.Fori(0, PT) as t:
                    retrieve(t, P, True)
                retrieve(PT, NS_ROWS, False)

            @block.scalar
            def _(act):
                A = nc.scalar.activation

                def flat(x):
                    return x.rearrange("p b n -> p (b n)")

                def prepare(t, h, j):
                    at = (h, j)
                    if at == (0, 3):
                        rows_in.of(act, t)
                        k["y_gelu"].mark(A(y[:], y[:], ACT.Gelu))
                    elif at == (0, 6):
                        k["y_turned"].of(act, t)
                        k["yT_done"].mark(A(flat(yT[:]), TQ[:, 0, :], ACT.Copy))
                    elif at == (0, 14):
                        k["zb_done"].of(act, t)
                        k["gate_y"].mark(A(z[:], z[:], ACT.Sigmoid))
                    elif at == (1, 6):
                        k["ms_y_done"].of(act, t)
                        k["sd_y_done"].mark(A(sd_y, ms_y, ACT.Sqrt))
                    elif at == (2, 9):
                        k["ms_x_done"].of(act, t)
                        k["sd_x_done"].mark(A(sd_x, ms_x, ACT.Sqrt))
                    elif at == (3, 2):
                        k["xn_turned"].of(act, t)
                        A(flat(xnT[:, 0:4, :]), TQ[:, 0, :], ACT.Copy)
                        k["xnT_done"].mark(A(flat(xnT[:, 4:8, :]), TQ[:, 1, :], ACT.Copy))
                    elif at in ((3, 8), (3, 12), (5, 4), (5, 8)):
                        n = "abcd"[((3, 8), (3, 12), (5, 4), (5, 8)).index(at)]
                        b = n in "bd"
                        k[f"q_{n}"].of(act, t)
                        k[f"qT_{n}"].mark(A(flat(qT[:, 4 * b:4 * b + 4, :]), TQ[:, int(b), :], ACT.Copy))
                    elif at in ((3, 15), (5, 11)):
                        n = "ab"[at == (5, 11)]
                        k[f"s_{n}"].of(act, t)
                        if n == "b":
                            k["topped_a"].of(act, t)
                        A(flat(S[:, 0:4, :]), ZS[:, 0, :], ACT.Copy)
                        k[f"S_{n}"].mark(A(flat(S[:, 4:8, :]), ZS[:, 1, :], ACT.Copy))
                    elif at == (7, 3):
                        k["nmax_done"].of(act, t)
                        for e in range(EH):
                            ins = A(ex[:, e, :], best[:, e, :], ACT.Exp, bias=nmax[:, e:e + 1], accum_out=esum[:, e:e + 1])
                        k["ex_done"].mark(ins)

                def take_rows(t, n):
                    k["gate_ready"].of(act, t)
                    act.wait_ge(dots, t * NSLOT + UR)
                    if not isinstance(t, int) or t > 0:
                        act.wait_ge(wgts, t * EH)
                    A(xn[0:n, :], xn_next[0:n, :], ACT.Copy)
                    k["xn_taken"].mark(A(gate[0:n, :], gate_next[0:n, :], ACT.Copy))

                def retrieve(t, n, prep):
                    for h in range(EH + 1):
                        for j in range(KS):
                            if h > 0:
                                s_ = KS * (h - 1) + j
                                if j == 0:
                                    act.wait_ge(wgts, t * EH + h)
                                act.wait_ge(pv, t * NSLOT + s_ + 1)
                                A(dg[0:n, s_ % DG, 0:n], ident[0:n, 0:n], ACT.Copy,
                                  scale=wgt[0:n, s_:s_ + 1]).then_inc(diags, 1)
                            if prep and h < EH:
                                prepare(t + 1, h, j)
                        if h < EH:
                            act.wait_ge(dots, t * NSLOT + KS * (h + 1) + UR)
                            cols = slice(KS * h, KS * (h + 1))
                            A(act_w[0:n, cols], dot[0:n, cols], ACT.Gelu).then_inc(gelus, 1)
                    if prep:
                        take_rows(t + 1, P)
                    k["ms_o_done"].of(act, t)
                    k["sd_o_done"].mark(A(sd_o[0:n], ms_o[0:n], ACT.Sqrt))

                for n in ("y_gelu yT_done gate_y sd_y_done sd_x_done xnT_done qT_a qT_b qT_c qT_d S_a S_b ex_done "
                          "xn_taken sd_o_done").split():
                    k[n].prime(act)
                act.wait_ge(early, 64)
                for h in range(EH):
                    for j in range(KS):
                        prepare(0, h, j)
                take_rows(0, P)
                with act.Fori(0, PT) as t:
                    retrieve(t, P, True)
                retrieve(PT, NS_ROWS, False)

            @block.vector
            def _(dve):
                V = nc.vector

                def rstd(t, ss, ms, sd, rs, width, mid, done, n=P):
                    k[mid].mark(V.tensor_scalar(ms[0:n], ss[0:n], 1.0 / width, EPS, ALU.mult, ALU.add))
                    k[done].of(dve, t)
                    dch_(t, V.reciprocal(rs[0:n], sd[0:n]))

                def dch_(t, ins, nop=False):
                    dch.chain(dve, t, ins, nop)

                def best16(t, vals, where, src, tmp):
                    dch_(t, V.max(vals[:, 0:8], src), True)
                    V.max_index(where[:, 0:8], vals[:, 0:8], src)
                    dch_(t, V.match_replace(tmp, vals[:, 0:8], src, LOWEST), True)
                    dch_(t, V.max(vals[:, 8:16], tmp), True)
                    dch_(t, V.max_index(where[:, 8:16], vals[:, 8:16], tmp), True)

                def pairwise(src, dst, op):
                    n = 0
                    for a0, a1, w in BLOCKS:
                        m = a1 - a0
                        x = bcast(src[:, :, 0, a0:a1], w, 3)
                        yy = bcast(src[:, :, 1, 0:w], m, 2)
                        ins = V.tensor_tensor(dst[:, :, n:n + m * w].rearrange("p h (m w) -> p h m w", w=w), x, yy, op)
                        n += m * w
                    return ins

                def prepare(t, h, j):
                    at = (h, j)
                    if at == (0, 13):
                        k["z_done"].of(dve, t)
                        k["zb_done"].mark(V.tensor_tensor(z[:], ZS[:, 0, :], b_glu[:], ALU.add))
                    elif at == (1, 3):
                        k["gate_y"].of(dve, t)
                        dch_(t, V.tensor_tensor(y[:], y[:], z[:], ALU.mult))
                        dch_(t, V.tensor_tensor_reduce(z[:], y[:], y[:], 1.0, 0.0, ALU.mult, ALU.add, ss_y))
                        k["ms_y_done"].mark(V.tensor_scalar(ms_y, ss_y, 1.0 / SW, EPS, ALU.mult, ALU.add))
                    elif at == (1, 9):
                        k["sd_y_done"].of(dve, t)
                        dch_(t, V.reciprocal(rs_y, sd_y))
                        k["yn_done"].mark(V.tensor_scalar(y[:], y[:], rs_y, None, ALU.mult))
                    elif at == (1, 13):
                        k["yn_turned"].of(dve, t)
                        k["ynT_done"].mark(V.tensor_tensor(yT[:], TQ[:, 0, :].rearrange("p (k n) -> p k n", n=P),
                                                           bcast(g_ssm[:], P, 2), ALU.mult))
                    elif at == (2, 6):
                        k["bot_done"].of(dve, t)
                        k["xn_taken"].of(dve, t - 1)
                        V.tensor_tensor(xr[:, 0:512], OP[:, 0, :], xr[:, 0:512], ALU.add)
                        dch_(t, V.tensor_tensor(xr[:, 512:D], OP[:, 1, :], xr[:, 512:D], ALU.add))
                        k["xr_done"].mark(V.tensor_tensor_reduce(xn_next[:], xr[:], xr[:], 1.0, 0.0, ALU.mult, ALU.add, ss_x))
                        k["xr_done"].of(dve, t)
                        k["ms_x_done"].mark(V.tensor_scalar(ms_x, ss_x, 1.0 / D, EPS, ALU.mult, ALU.add))
                    elif at == (2, 12):
                        k["sd_x_done"].of(dve, t)
                        dch_(t, V.reciprocal(rs_x, sd_x))
                        k["xn_done"].mark(V.scalar_tensor_tensor(xn_next[:], xr[:], rs_x, g_ffn[:], ALU.mult, ALU.mult))
                    elif h in (4, 6) and j % 2 == 1:
                        n, i = "ab"[h == 6], j // 2
                        e = 4 * (h == 6) + i // 2
                        if i == 0:
                            k[f"S_{n}"].held(dve, t)
                        best16(t, top_v[:, e, i % 2, :], top_i[:, e, i % 2, :], S[:, i, :], left[:])
                        if i == 7:
                            dve.sem_inc(k[f"topped_{n}"].sem, 1)
                    elif at == (7, 1):
                        dch_(t, V.tensor_copy(top_f[:], top_i[:]))
                        dch_(t, V.tensor_scalar(top_f[:, :, 0, :], top_f[:, :, 0, :], float(KEYS), None, ALU.mult))
                        pairwise(top_v, cand, ALU.add)
                        dch_(t, pairwise(top_f, cid, ALU.add), True)
                        for e in range(EH):
                            best16(t, best[:, e, :], pos[:, e, :], cand[:, e, :], left[:, 0:NCAND])
                        V.tensor_copy(pos_f[:], pos[:])
                        k["nmax_done"].mark(V.tensor_scalar(nmax[:], best[:, :, 0:1].rearrange("p h o -> p (h o)"), -1.0, None, ALU.mult))
                        k["nmax_done"].of(dve, t)
                    elif h == 7 and 4 <= j < 4 + EH:
                        e = j - 4
                        dch_(t, V.tensor_tensor(match, bcast(place[:], KS, 1), bcast(pos_f[:, e, :], NCAND, 2), ALU.is_equal))
                        dch_(t, V.tensor_tensor(match, match, bcast(cid[:, e, :], KS, 1), ALU.mult))
                        dch_(t, V.tensor_reduce(idx_f[:, e, :], match, AX.X, ALU.add))
                    elif at == (7, 13):
                        k["idx_taken"].of(dve, t - 1)
                        k["xn_taken"].of(dve, t - 1)
                        k["idx_ready"].mark(V.tensor_copy(idx_next[:], idx_f[:].rearrange("p h k -> p (h k)")))
                        k["ex_done"].of(dve, t)
                        dch_(t, V.reciprocal(esum[:], esum[:]))
                        k["gate_ready"].mark(V.tensor_tensor(gate_next[:].rearrange("p (h k) -> p h k", k=KS), ex[:],
                                                             bcast(esum[:], KS, 2), ALU.mult))

                def weigh(t, h, n):
                    cols = slice(KS * h, KS * (h + 1))
                    dve.wait_ge(gelus, t * EH + h + 1)
                    V.tensor_tensor(wgt[0:n, cols], act_w[0:n, cols], gate[0:n, cols], ALU.mult).then_inc(wgts, 1)

                def retrieve(t, n, prep):
                    k["xn_taken"].of(dve, t)
                    for h in range(EH):
                        for j in range(KS):
                            s_ = KS * h + j
                            ring_in(dve, u_in, t, s_)
                            row = u_ring[0:n, s_ % UR, :]
                            V.tensor_tensor_reduce(row, row, xn[0:n, :], 1.0, 0.0, ALU.mult, ALU.add,
                                                   dot[0:n, s_:s_ + 1]).then_inc(dots, 1)
                            if j == 0 and h > 0:
                                weigh(t, h - 1, n)
                            if prep:
                                prepare(t + 1, h, j)
                    weigh(t, EH - 1, n)
                    k["out_stored"].of(dve, t - 1)
                    dve.wait_ge(pv, t * NSLOT + NSLOT + VR)
                    k["acc_taken"].mark(V.tensor_copy(xo[0:n, :], acc[0:n, :]))
                    k["acc_taken"].of(dve, t)
                    k["ss_o_done"].mark(V.tensor_tensor_reduce(squares[0:n, :], xo[0:n, :], xo[0:n, :], 1.0, 0.0,
                                                               ALU.mult, ALU.add, ss_o[0:n]))
                    k["ss_o_done"].of(dve, t)
                    k["ms_o_done"].mark(V.tensor_scalar(ms_o[0:n], ss_o[0:n], 1.0 / D, EPS, ALU.mult, ALU.add))
                    k["sd_o_done"].of(dve, t)
                    dch_(t + 1, V.reciprocal(rs_o[0:n], sd_o[0:n]))
                    k["out_ready"].mark(V.scalar_tensor_tensor(xo[0:n, :], xo[0:n, :], rs_o[0:n], g_fin[0:n, :],
                                                               ALU.mult, ALU.mult))

                for n in ("zb_done yn_done ynT_done xr_done xn_done topped_a topped_b idx_ready nmax_done gate_ready "
                          "acc_taken ss_o_done ms_y_done ms_x_done ms_o_done out_ready").split():
                    k[n].prime(dve)
                dve.sem_inc(dots, UR)
                dve.wait_ge(early, 64)
                dve.wait_ge(weights, 16 * 6)
                for h in range(EH):
                    for j in range(KS):
                        prepare(0, h, j)
                dch_(0, V.memset(rs_o, 1.0))
                dch.tile_ends()
                with dve.Fori(0, PT) as t:
                    retrieve(t, P, True)
                dch.tile_ends()
                retrieve(PT, NS_ROWS, False)

            @block.tensor
            def _(pe):
                def prepare(t, h, j):
                    at = (h, j)
                    if at == (0, 4):
                        k["y_gelu"].of(pe, t)
                        k["xnT_done"].of(pe, t - 1)
                        for n in range(SW // P):
                            ins = nc.tensor.transpose(TQ[:, 0, n * P:(n + 1) * P], y[:, n * P:(n + 1) * P], ident[:])
                        k["y_turned"].mark(ins)
                    elif at == (0, 9):
                        k["yT_done"].of(pe, t)
                        k["S_b"].of(pe, t - 1)
                        for n in range(SW // P):
                            ins = nc.tensor.matmul(ZS[:, 0, :], yT[:, n, :], w_glu[:, n, :], start=(n == 0), stop=(n == SW // P - 1))
                        k["z_done"].mark(ins)
                    elif at == (1, 11):
                        k["yn_done"].of(pe, t)
                        for n in range(SW // P):
                            ins = nc.tensor.transpose(TQ[:, 0, n * P:(n + 1) * P], y[:, n * P:(n + 1) * P], ident[:])
                        k["yn_turned"].mark(ins)
                    elif at in ((2, 1), (2, 3)):
                        b = int(at == (2, 3))
                        k["ynT_done"].of(pe, t)
                        k["xr_done"].of(pe, t - 1)
                        for n in range(SW // P):
                            ins = nc.tensor.matmul(OP[:, b, :], yT[:, n, :], w_bot[:, n, 512 * b:512 * b + 512],
                                                   start=(n == 0), stop=(n == SW // P - 1))
                        if b:
                            k["bot_done"].mark(ins)
                    elif at == (2, 15):
                        k["xn_done"].of(pe, t)
                        for n in range(KD):
                            ins = nc.tensor.transpose(TQ[:, n // 4, (n % 4) * P:(n % 4 + 1) * P],
                                                      xn_next[:, n * P:(n + 1) * P], ident[:])
                        k["xn_turned"].mark(ins)
                    elif (h == 3 and 3 <= j < 11) or (h == 5 and 0 <= j < 8):
                        i = j - 3 if h == 3 else j
                        if i == 0:
                            k["xnT_done"].of(pe, t)
                            k["qT_b"].of(pe, t if h == 5 else t - 1)
                            k["s_a"].of(pe, t if h == 5 else t - 1)
                        hc = i + 8 * (h == 5)
                        for n in range(KD):
                            ins = nc.tensor.matmul(TQ[:, i // 4, (i % 4) * P:(i % 4 + 1) * P],
                                                   wq[:, n, hc * QH:(hc + 1) * QH], xnT[:, n, :],
                                                   start=(n == 0), stop=(n == KD - 1))
                        if i % 4 == 3:
                            k["q_" + "abcd"[2 * (h == 5) + i // 4]].mark(ins)
                    elif at in ((3, 13), (5, 10)):
                        n = "ab"[h == 5]
                        k["qT_" + "bd"[h == 5]].of(pe, t)
                        if n == "b":
                            k["S_a"].of(pe, t)
                        for i in range(EH):
                            ins = nc.tensor.matmul(ZS[:, i // 4, (i % 4) * P:(i % 4 + 1) * P], qT[:, i, :],
                                                   keys[:, i + 8 * (h == 5), :], start=True, stop=True)
                        k[f"s_{n}"].mark(ins)

                def begin(t, n):
                    k["xr_done"].of(pe, t)
                    k["acc_taken"].of(pe, t - 1)
                    for b in range(2):
                        ins = nc.tensor.matmul(ACC[0:n, b, :], ident[0:n, 0:n], xr[0:n, 512 * b:512 * b + 512],
                                               start=True, stop=False)
                    k["acc_begun"].mark(ins)

                def retrieve(t, n, prep):
                    begin(t, n)
                    for h in range(EH + 1):
                        for j in range(KS):
                            if h > 0:
                                s_ = KS * (h - 1) + j
                                pe.wait_ge(diags, t * NSLOT + s_ + 1)
                                ring_in(pe, v_in, t, s_)
                                for b in range(2):
                                    ins = nc.tensor.matmul(ACC[0:n, b, :], dg[0:n, s_ % DG, 0:n],
                                                           v_ring[0:n, s_ % VR, 512 * b:512 * b + 512],
                                                           start=False, stop=(s_ == NSLOT - 1))
                                ins.then_inc(pv, 1)
                            if prep and h < EH:
                                prepare(t + 1, h, j)

                for n in ("y_turned z_done yn_turned bot_done xn_turned q_a q_b q_c q_d s_a s_b acc_begun").split():
                    k[n].prime(pe)
                pe.sem_inc(pv, VR)
                pe.wait_ge(early, 64)
                pe.wait_ge(weights, 16 * 6)
                for h in range(EH):
                    for j in range(KS):
                        prepare(0, h, j)
                with pe.Fori(0, PT) as t:
                    retrieve(t, P, True)
                retrieve(PT, NS_ROWS, False)


def hybrid_layer(nc, a, s):
    sems = []

    def phase_ends():
        nc.clear_and_free_semaphores(sems)
        sems.clear()
        nc.all_engine_barrier()

    with ExitStack() as ctx:
        shared = Shared(Core(nc, ctx, sems))
        mix_tokens(nc, sems, a, s, shared)
        mix_samples(nc, sems, a, s, shared)
    phase_ends()
    run_ssm(nc, sems, a, s)
    phase_ends()
    retrieve_experts(nc, sems, a, s)


def host_layout(x):
    f = {n: np.ascontiguousarray(np.asarray(v)) for n, v in x.items()}
    rows = np.zeros((ROWS_PAD, D), np.float32)
    rows[:SEQ] = f["x_prompt"].reshape(SEQ, D)
    rows[SEQ:SEQ + NS_ROWS] = f["x_sample"].reshape(NS_ROWS, D)
    pos = np.zeros(ROWS_PAD, np.float32)
    pos[:SEQ] = np.arange(SEQ)
    pos[SEQ:SEQ + NS_ROWS] = np.tile(PAST + np.arange(DEC), NB)
    inv = np.float32(500000.0) ** (-np.arange(HALF, dtype=np.float32) * np.float32(2.0) / np.float32(ROT))
    ang = pos[:, None] * inv[None, :].astype(np.float32)
    rope = np.concatenate([np.cos(ang), np.sin(ang)], axis=1).astype(np.float32)
    q, key = np.arange(P)[:, None], np.arange(W)[None, :]
    off = np.float32(NEG / SCALE)
    mask = np.zeros((ROWS_PAD, 2 * W), np.float32)
    for t in range(PT):
        own = np.where(key <= q, 0, off)
        before = np.where((key > q) & (t > 0), 0, off)
        mask[t * P:(t + 1) * P] = np.concatenate([own, before] if t % 2 == 0 else [before, own], axis=1)
    i, key = (np.arange(P) % DEC)[:, None], np.arange(W + DEC)[None, :]
    mask_s = np.where((key > i) & (key <= W + i), 0, off).astype(np.float32)

    def pairs(v):
        v = v.reshape(PAIRS, 2, ST, *v.shape[2:])
        return np.ascontiguousarray(np.moveaxis(v, 0, 2).reshape(2 * ST, PAIRS, *v.shape[3:]))

    cols = np.concatenate([np.arange(AW).reshape(KV, REP, HD).transpose(1, 0, 2).ravel(), np.arange(AW, IN_W)])
    out = {
        "x": rows, "rope": rope, "mask": mask, "mask_s": mask_s,
        "ident": np.eye(P, dtype=np.float32), "minus_half": np.full((P, 1), -0.5, np.float32),
        "w_in": f["w_in"][0][:, cols], "b_in": f["b_in"].reshape(1, IN_W)[:, cols],
        "g_mix": np.ascontiguousarray(f["norm_mix"].reshape(KD, P).T),
        "g_attn": np.ascontiguousarray(f["norm_attn_out"].reshape(AW // P, P).T),
        "g_ssm": np.ascontiguousarray(f["norm_ssm_out"].reshape(SW // P, P).T),
        "g_ffn": f["norm_ffn"].reshape(1, D), "g_final": f["norm_final"].reshape(1, D),
        "sink": f["attn_sinks"].reshape(1, HEADS),
        "sink_s": np.ascontiguousarray(np.broadcast_to(
            f["attn_sinks"].reshape(KV, 1, REP, 1), (KV, 4, REP, DEC)).reshape(KV, P).T),
        "w_out": f["w_out"][0], "w_glu": f["ssm_w_glu"][0], "b_glu": f["ssm_b_glu"].reshape(1, SW),
        "cache_k": f["cache_k"].reshape(NB, W, KV * HD), "cache_v": f["cache_v"].reshape(NB, W, KV * HD),
        "h0_re": pairs(np.moveaxis(f["state_ssm_re"][0], 0, 2)), "h0_im": pairs(np.moveaxis(f["state_ssm_im"][0], 0, 2)),
        "lam_re": pairs(f["ssm_lam_re"][0]), "lam_im": pairs(f["ssm_lam_im"][0]),
        "log_step": pairs(np.broadcast_to(f["ssm_log_step"][0][:, None], (GRP, ST))),
        "b_re": pairs(f["ssm_b_re"][0]), "b_im": pairs(f["ssm_b_im"][0]),
        "c_re": pairs(np.swapaxes(f["ssm_c_re"][0], 1, 2)), "c_im": pairs(np.swapaxes(f["ssm_c_im"][0], 1, 2)),
        "d_skip": f["ssm_d"].reshape(1, SW),
        "w_query": f["peer_w_query"][0],
        "keys": np.ascontiguousarray(np.transpose(f["peer_sub_keys"][0], (3, 0, 1, 2)).reshape(QH, EH * 2 * KEYS)),
        "place": np.arange(62, dtype=np.float32).reshape(1, 62),
        "u_table": f["peer_u"][0], "v_table": f["peer_v"][0],
    }
    return {n: np.ascontiguousarray(v) for n, v in out.items()}


OUTPUTS = {
    "y": (SEQ + NS_ROWS, D), "new_k_prompt": (W, KV * HD), "new_v_prompt": (W, KV * HD),
    "ssm_re_prompt": (P, PAIRS), "ssm_im_prompt": (P, PAIRS),
    "new_k_sample": (NB, W, KV * HD), "new_v_sample": (NB, W, KV * HD),
    "ssm_re_sample": (P, PAIRS, NB), "ssm_im_sample": (P, PAIRS, NB),
}
SCRATCH = {
    "u": (ROWS_PAD, SW), "x1": (ROWS_PAD, D), "pj": (NS_ROWS, U_COL), "x_s": (NS_ROWS, D),
    "attn_s": (P, 4 * HD), "y_ssm": (ROWS_PAD, SW),
}


def kernel(**inputs):
    import concourse.bacc as bacc
    from concourse.bass_utils import run_bass_kernel_spmd

    nc = bacc.Bacc("TRN2", target_bir_lowering=False, num_devices=1)
    laid = host_layout(inputs)
    a = {n: nc.dram_tensor(f"in_{n}", v.shape, mybir.dt.from_np(v.dtype), kind="ExternalInput").ap()
         for n, v in laid.items()}
    a |= {n: nc.dram_tensor(f"out_{n}", shape, F32, kind="ExternalOutput").ap() for n, shape in OUTPUTS.items()}
    s = {n: nc.dram_tensor(f"scratch_{n}", shape, F32, kind="Internal").ap() for n, shape in SCRATCH.items()}
    hybrid_layer(nc, a, s)
    r = run_bass_kernel_spmd(nc, [{f"in_{n}": v for n, v in laid.items()}], core_ids=[0]).results[0]
    got = {n: np.asarray(r[f"out_{n}"]) for n in OUTPUTS}

    def groups(v):
        v = np.moveaxis(v.reshape(2, ST, PAIRS, *v.shape[2:]), 2, 0)
        return v.reshape(GRP, ST, *v.shape[3:])

    def state(n, sample):
        v = groups(got[n])
        return np.moveaxis(v, 2, 0)[None] if sample else v[None, None]

    window = (1, 1, W, KV, HD)
    windows = (1, NB, W, KV, HD)
    return (got["y"][:SEQ].reshape(1, SEQ, D), got["y"][SEQ:].reshape(NB, DEC, D),
            got["new_k_prompt"].reshape(window), got["new_v_prompt"].reshape(window),
            state("ssm_re_prompt", False), state("ssm_im_prompt", False),
            got["new_k_sample"].reshape(windows), got["new_v_sample"].reshape(windows),
            state("ssm_re_sample", True), state("ssm_im_sample", True))
```

```python
from contextlib import ExitStack

import concourse.bass as bass
import numpy as np
from concourse import mybir

F32 = mybir.dt.float32
U32 = mybir.dt.uint32
ALU = mybir.AluOpType
ACT = mybir.ActivationFunctionType
AX = mybir.AxisListType

P = 128
D = 1024
KD = D // P
SEQ, NB, DEC = 1024, 8, 8
NS_ROWS = NB * DEC
PT = SEQ // P
ROWS_PAD = (PT + 1) * P
assert 2 * NS_ROWS == P
PAST = 2048
HEADS, KV, REP, HD = 8, 2, 4, 64
AW = HEADS * HD
W = 128
ROT = HD // 4
HALF = ROT // 2
SW = D - AW
GRP, CH, ST = 32, 16, 64
assert PT % 2 == 0
PAIRS = GRP // 2
L = 8
CK = SEQ // L
NC = CK + NB
IN_W = AW + 2 * KV * HD + SW
U_COL = AW + 2 * KV * HD
EH, KEYS, TOPK, QH = 8, 128, 16, 128
EPS = 1e-5
NEG = float(np.float32(-1e30))
SCALE = HD ** -0.5
TWO_PI = 2 * np.pi
PI_HI = 6.28125
PI_LO = TWO_PI - PI_HI
ROUND = 1.5 * 2.0 ** 23
PI_MAX = 3.1415925


class Count:

    def __init__(self, sem, step=1):
        self.sem, self.step = sem, step
        self.first = 2 if step == 1 else 1

    def prime(self, eng):
        assert self.step == 1
        eng.sem_inc(self.sem, 1)

    def mark(self, ins):
        ins.then_inc(self.sem, 16 if self.step >= 16 else 1)

    def of(self, eng, t):
        if isinstance(t, int) and t + self.first <= 0:
            return
        eng.wait_ge(self.sem, (t + self.first) * self.step)

    def held(self, eng, t):
        self.of(eng, t)
        eng.nop(nofuse=True)


class Steps:

    def __init__(self, sem):
        self.sem, self.n = sem, 0

    def mark(self, ins):
        self.n += 1
        ins.then_inc(self.sem, 1)
        return self.n

    def chain(self, eng, ins):
        self.mark(ins)
        eng.wait_ge(self.sem, self.n)


class Core:

    def __init__(self, nc, ctx, sems):
        self.nc, self.ctx, self.sems = nc, ctx, sems

    def sb(self, name, shape, dt=F32):
        return self.ctx.enter_context(self.nc.sbuf_tensor(name, shape, dt))

    def ps(self, name, shape):
        return self.ctx.enter_context(self.nc.psum_tensor(name, shape, F32))

    def sem(self, name):
        self.sems.append(self.nc.alloc_semaphore(name=name))
        return self.sems[-1]

    def count(self, name, step=1):
        return Count(self.sem(name), step)

    def steps(self, name):
        return Steps(self.sem(name))


def bcast(ap, n, dim):
    shape = list(ap.shape)
    return ap.unsqueeze(dim).to_broadcast(shape[:dim] + [n] + shape[dim:])


def mix_tokens(nc, sems, a, s, shared):
    with ExitStack() as ctx:
        c = Core(nc, ctx, sems)
        w_in = c.sb("w_in", [P, KD, IN_W])
        w_top, g_attn, ident, half = shared.w_top, shared.g_attn, shared.ident, shared.half
        b_in = c.sb("b_in", [P, IN_W])
        g_mix = c.sb("g_mix", [P, KD])
        sink = c.sb("sink", [P, HEADS])
        xt = c.sb("xt", [P, 2, D])
        rope = c.sb("rope", [P, 2, 2 * HALF])
        mask = c.sb("mask", [P, 2, 2 * W])
        xs = c.sb("xs", [P, D])
        xT = c.sb("xT", [P, KD, P])
        pj = c.sb("pj", [P, 2, IN_W])
        rt = c.sb("rt", [P, 4, HEADS + KV, HALF])
        qT = c.sb("qT", [P, REP, P])
        kT = c.sb("kT", [P, 2, P])
        vb = c.sb("vb", [P, 2, P])
        sc = c.sb("sc", [P, HEADS, 2 * W])
        pr = c.sb("pr", [P, HEADS, 2 * W])
        ptr = c.sb("ptr", [P, 2 * HEADS, P])
        at = c.sb("at", [P, AW])
        at2 = c.sb("at2", [P, AW])
        aT = c.sb("aT", [P, AW // P, P])
        small = c.sb("small_a", [P, 8, HEADS])
        stat = c.sb("stat_a", [P, 8])
        mx, nm, sd, es, rs, den, rden = (small[:, i, :] for i in range(7))
        ssx, msx, rsx, ssa, msa, rsa = (stat[:, i:i + 1] for i in range(6))

        PJ = c.ps("PJ", [P, 3, 512])
        SC = c.ps("SC", [P, 4, 2, 2 * W])
        X = c.ps("X", [P, 512])
        QK = SC[:, 2:4, :, :].rearrange("p b c n -> p (b c n)")
        SCf = SC[:, :, :, :].rearrange("p b c n -> p (b c n)")

        weights = c.sem("weights_in")
        kept = c.sem("kv_out")
        zeroed = c.sem("zeroed_a")
        tile_in = c.count("tile_in", 48)
        u_out = c.count("u_out", 16)
        x1_out = c.count("x1_out", 16)
        names = ("ssx_done rsx_done xs_done x_turned xT_done projected pj_done roped v_kept qk_turned "
                 "qkT_done scored maxed shifted probs_done p_turned ptr_act ptr_dve weighed at_done "
                 "ssa_done rsa_done at2_done a_turned aT_done mixed x1_done msx_done msa_done rope_mul "
                 "den_done rden_done").split()
        k = {n: c.count(n) for n in names}
        N_W = 8

        def load(eng, t, p):
            tile_in.mark(eng.dma_start(xt[:, p, :], a["x"][bass.ts(t, P), :]))
            tile_in.mark(eng.dma_start(rope[:, p, :], a["rope"][bass.ts(t, P), :]))
            tile_in.mark(eng.dma_start(mask[:, p, :], a["mask"][bass.ts(t, P), :]))

        with nc.Block() as block:

            @block.sync
            def _(sp):
                def prologue():
                    load(sp, 0, 0)
                    sp.dma_start(w_in[:], a["w_in"].rearrange("(k p) n -> p k n", p=P)).then_inc(weights, 16)
                    sp.dma_start(b_in[:], a["b_in"].to_broadcast([P, IN_W])).then_inc(weights, 16)
                    sp.dma_start(g_mix[:], a["g_mix"]).then_inc(weights, 16)
                    sp.dma_start(g_attn[:], a["g_attn"]).then_inc(weights, 16)
                    sp.dma_start(sink[:], a["sink"].to_broadcast([P, HEADS])).then_inc(weights, 16)
                    sp.dma_start(ident[:], a["ident"]).then_inc(weights, 16)
                    sp.dma_start(w_top[:], a["w_out"][0:AW, :].rearrange("(k p) n -> p k n", p=P)).then_inc(weights, 16)
                    sp.dma_start(half[:], a["minus_half"]).then_inc(weights, 16)

                def step(t, p):
                    load(sp, t + 1, 1 - p)
                    k["pj_done"].held(sp, t + 1)
                    u_out.mark(sp.dma_start(s["u"][bass.ts(t + 1, P), :], pj[:, 1 - p, U_COL:]))
                    k["x1_done"].held(sp, t)
                    x1_out.mark(sp.dma_start(s["x1"][bass.ts(t, P), :], xt[:, p, :]))
                    u_out.held(sp, t + 1)
                    x1_out.held(sp, t)

                prologue()
                k["pj_done"].held(sp, 0)
                u_out.mark(sp.dma_start(s["u"][0:P, :], pj[:, 0, U_COL:]))
                u_out.held(sp, 0)
                with sp.Fori(0, PT // 2) as i:
                    for p in range(2):
                        step(i * 2 + p, p)
                k["roped"].held(sp, PT)
                sp.dma_start(a["new_k_prompt"], pj[:, 1, AW:AW + KV * HD]).then_inc(kept, 16)
                sp.dma_start(a["new_v_prompt"], pj[:, 1, AW + KV * HD:U_COL]).then_inc(kept, 16)
                sp.dma_start(s["pj"], pj[0:NS_ROWS, 0, 0:U_COL]).then_inc(kept, 16)
                sp.dma_start(s["x_s"], xt[0:NS_ROWS, 0, :]).then_inc(kept, 16)
                sp.wait_ge(kept, 16 * 4)

            @block.gpsimd
            def _(pool):
                for n in ("roped", "rsx_done", "msx_done", "v_kept", "rsa_done", "msa_done", "rope_mul"):
                    k[n].prime(pool)

                def rstd(t, src, ms, out, width, ready, mid, done):
                    ready.held(pool, t)
                    mid.mark(pool.tensor_scalar(ms, src, 1.0 / width, EPS, ALU.mult, ALU.add))
                    mid.held(pool, t)
                    done.mark(pool.tensor_tensor(out, ms, half[:], ALU.pow))

                def rotate(t, p):
                    heads = pj[:, p, 0:AW + KV * HD].rearrange("p (h d) -> p h d", d=HD)
                    x1, x2 = heads[:, :, 0:HALF], heads[:, :, HALF:ROT]
                    cos = bcast(rope[:, p, 0:HALF], HEADS + KV, 1)
                    sin = bcast(rope[:, p, HALF:], HEADS + KV, 1)
                    k["pj_done"].held(pool, t)
                    k["roped"].held(pool, t - 1)
                    pool.tensor_tensor(rt[:, 0], x1, cos, ALU.mult)
                    pool.tensor_tensor(rt[:, 1], x2, sin, ALU.mult)
                    pool.tensor_tensor(rt[:, 2], x2, cos, ALU.mult)
                    k["rope_mul"].mark(pool.tensor_tensor(rt[:, 3], x1, sin, ALU.mult))
                    k["rope_mul"].held(pool, t)
                    pool.tensor_tensor(x1, rt[:, 0], rt[:, 1], ALU.subtract)
                    k["roped"].mark(pool.tensor_tensor(x2, rt[:, 2], rt[:, 3], ALU.add))

                def step(t, p):
                    k["weighed"].held(pool, t - 1)
                    k["v_kept"].mark(pool.tensor_copy(vb[:, p, :], pj[:, p, AW + KV * HD:U_COL]))
                    rstd(t + 1, ssx, msx, rsx, D, k["ssx_done"], k["msx_done"], k["rsx_done"])
                    rotate(t + 1, 1 - p)
                    rstd(t, ssa, msa, rsa, AW, k["ssa_done"], k["msa_done"], k["rsa_done"])

                pool.memset(kT[:, 1, :], 0.0).then_inc(zeroed, 1)
                pool.memset(vb[:, 1, :], 0.0).then_inc(zeroed, 1)
                pool.wait_ge(weights, 16 * N_W)
                rstd(0, ssx, msx, rsx, D, k["ssx_done"], k["msx_done"], k["rsx_done"])
                rotate(0, 0)
                with pool.Fori(0, PT // 2) as i:
                    for p in range(2):
                        step(i * 2 + p, p)

            @block.scalar
            def _(act):
                for n in ("ssx_done", "qkT_done", "probs_done", "ptr_act"):
                    k[n].prime(act)

                def squares(t, p):
                    tile_in.of(act, t)
                    k["x_turned"].of(act, t - 1)
                    k["ssx_done"].mark(nc.scalar.activation(xs[:], xt[:, p, :], ACT.Square, accum_out=ssx))

                def step(t, p):
                    k["qk_turned"].of(act, t)
                    k["scored"].of(act, t - 1)
                    act.wait_ge(zeroed, 2)
                    nc.scalar.activation(qT[:].rearrange("p r n -> p (r n)"), QK[:, 0:512], ACT.Copy)
                    k["qkT_done"].mark(nc.scalar.activation(kT[:, p, :], QK[:, 512:512 + P], ACT.Copy))
                    squares(t + 1, 1 - p)
                    k["shifted"].of(act, t)
                    k["p_turned"].of(act, t - 1)
                    k["den_done"].of(act, t - 1)
                    for h in range(HEADS):
                        nc.scalar.activation(pr[:, h, :], sc[:, h, :], ACT.Exp, bias=nm[:, h:h + 1],
                                             accum_out=rs[:, h:h + 1])
                    k["probs_done"].mark(nc.scalar.activation(es, sd, ACT.Exp))
                    k["p_turned"].of(act, t)
                    k["weighed"].of(act, t - 1)
                    nc.scalar.activation(ptr[:, 0:4, :].rearrange("p a n -> p (a n)"), SCf[:, 0:512], ACT.Copy)
                    k["ptr_act"].mark(nc.scalar.activation(
                        ptr[:, 4:8, :].rearrange("p a n -> p (a n)"), SCf[:, 512:1024], ACT.Copy))

                squares(0, 0)
                with act.Fori(0, PT // 2) as i:
                    for p in range(2):
                        step(i * 2 + p, p)

            @block.vector
            def _(dve):
                for n in ("xs_done", "xT_done", "pj_done", "maxed", "shifted", "ptr_dve", "at_done", "ssa_done",
                          "at2_done", "aT_done", "x1_done", "den_done", "rden_done"):
                    k[n].prime(dve)

                def project(t, p):
                    k["rsx_done"].of(dve, t)
                    k["ssx_done"].of(dve, t)
                    k["xs_done"].mark(nc.vector.tensor_scalar(xs[:], xt[:, p, :], rsx, None, ALU.mult))
                    k["x_turned"].of(dve, t)
                    k["projected"].of(dve, t - 1)
                    for b in range(2):
                        ins = nc.vector.tensor_tensor(
                            xT[:, 4 * b:4 * b + 4, :], PJ[:, b, :].rearrange("p (k n) -> p k n", n=P),
                            bcast(g_mix[:, 4 * b:4 * b + 4], P, 2), ALU.mult)
                    k["xT_done"].mark(ins)
                    k["projected"].of(dve, t)
                    tile_in.of(dve, t)
                    k["v_kept"].of(dve, t - 2)
                    for b, (lo, hi) in enumerate(((0, 512), (512, U_COL), (U_COL, IN_W))):
                        ins = nc.vector.tensor_tensor(pj[:, p, lo:hi], PJ[:, b, 0:hi - lo], b_in[:, lo:hi], ALU.add)
                    k["pj_done"].mark(ins)

                def step(t, p):
                    k["scored"].of(dve, t)
                    k["probs_done"].of(dve, t - 1)
                    tile_in.held(dve, t)
                    for h in range(HEADS):
                        ins = nc.vector.tensor_tensor_reduce(
                            sc[:, h, :], SC[:, h // 2, h % 2, :], mask[:, p, :], SCALE, sink[:, h:h + 1],
                            ALU.add, ALU.max, mx[:, h:h + 1])
                    k["maxed"].mark(ins)
                    k["maxed"].of(dve, t)
                    nc.vector.tensor_scalar(nm, mx, -1.0, None, ALU.mult)
                    k["shifted"].mark(nc.vector.tensor_tensor(sd, sink[:], mx, ALU.subtract))
                    project(t + 1, 1 - p)
                    k["probs_done"].of(dve, t)
                    k["at_done"].of(dve, t - 1)
                    k["den_done"].mark(nc.vector.tensor_tensor(den, rs, es, ALU.add))
                    k["den_done"].of(dve, t)
                    k["rden_done"].mark(nc.vector.reciprocal(rden, den))
                    k["p_turned"].of(dve, t)
                    k["weighed"].of(dve, t - 1)
                    nc.vector.tensor_copy(ptr[:, 8:12, :].rearrange("p a n -> p (a n)"), SCf[:, 1024:1536])
                    k["ptr_dve"].mark(nc.vector.tensor_copy(
                        ptr[:, 12:16, :].rearrange("p a n -> p (a n)"), SCf[:, 1536:2048]))
                    k["weighed"].of(dve, t)
                    k["rden_done"].of(dve, t)
                    k["at2_done"].of(dve, t - 1)
                    k["at_done"].mark(nc.vector.tensor_tensor(
                        at[:].rearrange("p (h d) -> p h d", d=HD), X[:].rearrange("p (h d) -> p h d", d=HD),
                        bcast(rden, HD, 2), ALU.mult))
                    k["at_done"].of(dve, t)
                    k["a_turned"].of(dve, t - 1)
                    k["ssa_done"].mark(nc.vector.tensor_tensor_reduce(at2[:], at[:], at[:], 1.0, 0.0,
                                                                      ALU.mult, ALU.add, ssa))
                    k["ssa_done"].of(dve, t)
                    k["rsa_done"].of(dve, t)
                    k["at2_done"].mark(nc.vector.tensor_scalar(at2[:], at[:], rsa, None, ALU.mult))
                    k["a_turned"].of(dve, t)
                    k["aT_done"].mark(nc.vector.tensor_tensor(
                        aT[:], X[:].rearrange("p (k n) -> p k n", n=P), bcast(g_attn[:], P, 2), ALU.mult))
                    k["mixed"].of(dve, t)
                    for b in range(2):
                        half_row = xt[:, p, 512 * b:512 * b + 512]
                        ins = nc.vector.tensor_tensor(half_row, PJ[:, b, :], half_row, ALU.add)
                    k["x1_done"].mark(ins)

                dve.wait_ge(weights, 16 * N_W)
                project(0, 0)
                with dve.Fori(0, PT // 2) as i:
                    for p in range(2):
                        step(i * 2 + p, p)

            @block.tensor
            def _(pe):
                for n in ("x_turned", "projected", "qk_turned", "scored", "p_turned", "weighed", "a_turned", "mixed"):
                    k[n].prime(pe)

                def project(t):
                    k["xs_done"].of(pe, t)
                    k["x1_done"].of(pe, t - 2)
                    k["pj_done"].of(pe, t - 1)
                    for j in range(KD):
                        ins = nc.tensor.transpose(PJ[:, j // 4, (j % 4) * P:(j % 4 + 1) * P],
                                                  xs[:, j * P:(j + 1) * P], ident[:])
                    k["x_turned"].mark(ins)
                    k["xT_done"].of(pe, t)
                    for b, (lo, hi) in enumerate(((0, 512), (512, U_COL), (U_COL, IN_W))):
                        for j in range(KD):
                            ins = nc.tensor.matmul(PJ[:, b, 0:hi - lo], xT[:, j, :], w_in[:, j, lo:hi],
                                                   start=(j == 0), stop=(j == KD - 1))
                    k["projected"].mark(ins)

                def step(t, p):
                    k["roped"].of(pe, t)
                    k["ptr_act"].of(pe, t - 1)
                    k["ptr_dve"].of(pe, t - 1)
                    for r in range(REP):
                        nc.tensor.transpose(QK[:, r * P:(r + 1) * P], pj[:, p, r * P:(r + 1) * P], ident[:])
                    k["qk_turned"].mark(nc.tensor.transpose(
                        QK[:, 512:512 + P], pj[:, p, AW:AW + KV * HD], ident[:]))
                    k["qkT_done"].of(pe, t)
                    for h in range(HEADS):
                        g, r = divmod(h, REP)
                        ins = nc.tensor.matmul(SC[:, h // 2, h % 2, :], qT[g * HD:(g + 1) * HD, r, :],
                                               kT[g * HD:(g + 1) * HD, :, :].rearrange("p a n -> p (a n)"),
                                               start=True, stop=True)
                    k["scored"].mark(ins)
                    project(t + 1)
                    k["probs_done"].of(pe, t)
                    k["maxed"].of(pe, t)
                    for h in range(HEADS):
                        for w in range(2):
                            n = 2 * h + w
                            ins = nc.tensor.transpose(SCf[:, n * P:(n + 1) * P], pr[:, h, w * W:(w + 1) * W], ident[:])
                    k["p_turned"].mark(ins)
                    k["ptr_act"].of(pe, t)
                    k["ptr_dve"].of(pe, t)
                    k["v_kept"].of(pe, t)
                    k["aT_done"].of(pe, t - 1)
                    for h in range(HEADS):
                        g = h // REP
                        for w in range(2):
                            ins = nc.tensor.matmul(X[:, h * HD:(h + 1) * HD], ptr[:, 2 * h + w, :],
                                                   vb[:, w, g * HD:(g + 1) * HD], start=(w == 0), stop=(w == 1))
                    k["weighed"].mark(ins)
                    k["at2_done"].of(pe, t)
                    for j in range(AW // P):
                        ins = nc.tensor.transpose(X[:, j * P:(j + 1) * P], at2[:, j * P:(j + 1) * P], ident[:])
                    k["a_turned"].mark(ins)
                    k["aT_done"].of(pe, t)
                    k["pj_done"].of(pe, t + 1)
                    for b in range(2):
                        for j in range(AW // P):
                            ins = nc.tensor.matmul(PJ[:, b, :], aT[:, j, :], w_top[:, j, 512 * b:512 * b + 512],
                                                   start=(j == 0), stop=(j == AW // P - 1))
                    k["mixed"].mark(ins)

                pe.wait_ge(weights, 16 * N_W)
                project(0)
                with pe.Fori(0, PT // 2) as i:
                    for p in range(2):
                        step(i * 2 + p, p)


class Once:

    def __init__(self, core, phase):
        self.core, self.phase, self.sems = core, phase, {}

    def __getitem__(self, name):
        if name not in self.sems:
            self.sems[name] = self.core.sem(f"{self.phase}_{name}")
        return self.sems[name]


def mix_samples(nc, sems, a, s, shared):
    with ExitStack() as ctx:
        c = Core(nc, ctx, sems)
        w_top, g_attn, ident, half = shared.w_top, shared.g_attn, shared.ident, shared.half
        R, NK = NS_ROWS, W + DEC
        qkv = c.sb("qkv_s", [R, U_COL])
        xr = c.sb("xr_s", [R, D])
        kc = c.sb("kc", [P, NB, P])
        vc = c.sb("vc", [P, NB, P])
        vn = c.sb("vn", [DEC, NB, P])
        mask = c.sb("mask_s", [P, NK])
        sink = c.sb("sink_s", [P, KV])
        qT = c.sb("qT_s", [P, NB, REP, DEC])
        kT = c.sb("kT_s", [P, NB, NK])
        sc = c.sb("sc_s", [P, 4, NK])
        pr = c.sb("pr_s", [P, 4, NK])
        ptb = c.sb("ptb", [P, 4, P])
        ptn = c.sb("ptn", [DEC, 4, P])
        small = c.sb("small_s", [P, 8, 4])
        stat = c.sb("stat_s", [P, 4])
        oS = c.sb("o_s", [P, 4, HD])
        at = c.sb("at_s", [R, AW])
        at2 = c.sb("at2_s", [R, AW])
        aT = c.sb("aT_s", [P, AW // P, R])
        mx, nm, sd, es, rs, den, rden = (small[:, i, :] for i in range(7))
        ss, ms, rstd = (stat[0:R, i:i + 1] for i in range(3))
        TR = c.ps("TR", [P, 512])
        KB = c.ps("KB", [P, NB, P])
        SS = c.ps("SS", [P, KV, 512])
        PO = c.ps("PO", [P, 2, 512])
        ev = Once(c, "s")
        loads, qkv_in, back_in, stores = c.sem("loads_s"), c.sem("qkv_in"), c.sem("back_in"), c.sem("stores_s")

        with nc.Block() as block:

            @block.sync
            def _(sp):
                sp.dma_start(qkv[:], s["pj"]).then_inc(qkv_in, 16)
                sp.dma_start(kc[:], a["cache_k"].rearrange("b j n -> j b n")).then_inc(loads, 16)
                sp.dma_start(vc[:], a["cache_v"].rearrange("b j n -> j b n")).then_inc(loads, 16)
                sp.dma_start(vn[:], s["pj"][:, AW + KV * HD:U_COL].rearrange("(b i) n -> i b n", i=DEC)).then_inc(loads, 16)
                sp.dma_start(mask[:], a["mask_s"]).then_inc(loads, 16)
                sp.dma_start(sink[:], a["sink_s"]).then_inc(loads, 16)
                sp.dma_start(xr[:], s["x_s"]).then_inc(loads, 16)
                for n, lo in (("k", AW), ("v", AW + KV * HD)):
                    out = a[f"new_{n}_sample"]
                    sp.dma_start(out[:, 0:W - DEC, :], a[f"cache_{n}"][:, DEC:W, :]).then_inc(stores, 16)
                    sp.dma_start(out[:, W - DEC:W, :], s["pj"][:, lo:lo + KV * HD].rearrange("(b i) n -> b i n", i=DEC)).then_inc(stores, 16)
                sp.wait_ge(ev["o_done"], 1)
                sp.dma_start(s["attn_s"], oS[:].rearrange("p n d -> p (n d)")).then_inc(ev["o_out"], 16)
                sp.wait_ge(ev["o_out"], 16)
                for b in range(NB):
                    for g in range(KV):
                        src = s["attn_s"][32 * (b % 4):32 * (b % 4) + 32, (2 * g + b // 4) * HD:(2 * g + b // 4 + 1) * HD]
                        sp.dma_start(at[b * DEC:(b + 1) * DEC, g * 256:(g + 1) * 256].rearrange("i (r d) -> i r d", d=HD),
                                     src.rearrange("(r i) d -> i r d", i=DEC)).then_inc(back_in, 16)
                sp.wait_ge(ev["x1"], 1)
                for lo in (SEQ, SEQ + R):
                    sp.dma_start(s["x1"][lo:lo + R, :], xr[:]).then_inc(stores, 16)
                sp.wait_ge(stores, 16 * 6)

            @block.gpsimd
            def _(pool):
                pool.wait_ge(ev["ss"], 1)
                pool.tensor_scalar(ms, ss, 1.0 / AW, EPS, ALU.mult, ALU.add).then_inc(ev["ms"], 1)
                pool.wait_ge(ev["ms"], 1)
                pool.tensor_tensor(rstd, ms, half[0:R, :], ALU.pow).then_inc(ev["rstd"], 1)

            @block.scalar
            def _(act):
                act.wait_ge(ev["q_turned"], 1)
                nc.scalar.activation(qT[:], TR[:, 0:REP * R].rearrange("p (r b i) -> p b r i", r=REP, i=DEC), ACT.Copy)
                nc.scalar.activation(kT[:, :, W:NK], TR[:, REP * R:5 * R].rearrange("p (b i) -> p b i", i=DEC),
                                     ACT.Copy).then_inc(ev["qT"], 1)
                act.wait_ge(ev["shifted"], 1)
                for n in range(4):
                    nc.scalar.activation(pr[:, n, :], sc[:, n, :], ACT.Exp, bias=nm[:, n:n + 1], accum_out=rs[:, n:n + 1])
                nc.scalar.activation(es, sd, ACT.Exp).then_inc(ev["probs"], 1)
                act.wait_ge(ev["p_turned"], 1)
                nc.scalar.activation(ptb[:].rearrange("p n m -> p (n m)"), KB[:, 0:4, :].rearrange("p n m -> p (n m)"),
                                     ACT.Copy).then_inc(ev["ptb"], 1)
                nc.scalar.activation(ptn[:].rearrange("p n m -> p (n m)"),
                                     KB[0:DEC, 4:8, :].rearrange("p n m -> p (n m)"), ACT.Copy).then_inc(ev["ptn"], 1)

            @block.vector
            def _(dve):
                dve.wait_ge(ev["k_turned"], 1)
                nc.vector.tensor_copy(kT[:, :, 0:W], KB[:]).then_inc(ev["kT"], 1)
                dve.wait_ge(loads, 16 * 6)
                dve.wait_ge(ev["scored"], 1)
                for g in range(KV):
                    for hf in range(2):
                        n = 2 * g + hf
                        ins = nc.vector.tensor_tensor_reduce(
                            sc[:, n, :], SS[:, g, hf * NK:(hf + 1) * NK], mask[:], SCALE, sink[:, g:g + 1],
                            ALU.add, ALU.max, mx[:, n:n + 1])
                ins.then_inc(ev["maxed"], 1)
                dve.wait_ge(ev["maxed"], 1)
                nc.vector.tensor_scalar(nm, mx, -1.0, None, ALU.mult)
                nc.vector.tensor_tensor(sd.rearrange("p (g f) -> p g f", g=KV), bcast(sink[:], 2, 2),
                                        mx.rearrange("p (g f) -> p g f", g=KV), ALU.subtract).then_inc(ev["shifted"], 1)
                dve.wait_ge(ev["probs"], 1)
                nc.vector.tensor_tensor(den, rs, es, ALU.add).then_inc(ev["den"], 1)
                dve.wait_ge(ev["den"], 1)
                nc.vector.reciprocal(rden, den).then_inc(ev["rden"], 1)
                dve.wait_ge(ev["rden"], 1)
                dve.wait_ge(ev["weighed"], 1)
                nc.vector.tensor_tensor(oS[:], PO[:, 0, 0:4 * HD].rearrange("p (n d) -> p n d", d=HD),
                                        bcast(rden, HD, 2), ALU.mult).then_inc(ev["o_done"], 1)
                dve.wait_ge(back_in, 16 * NB * KV)
                nc.vector.tensor_tensor_reduce(at2[:], at[:], at[:], 1.0, 0.0, ALU.mult, ALU.add, ss).then_inc(ev["ss"], 1)
                dve.wait_ge(ev["ss"], 1)
                dve.wait_ge(ev["rstd"], 1)
                nc.vector.tensor_scalar(at2[:], at[:], rstd, None, ALU.mult).then_inc(ev["at2"], 1)
                dve.wait_ge(ev["a_turned"], 1)
                nc.vector.tensor_tensor(aT[:], TR[:, 0:4 * R].rearrange("p (k n) -> p k n", n=R), bcast(g_attn[:], R, 2),
                                        ALU.mult).then_inc(ev["aT"], 1)
                dve.wait_ge(ev["mixed"], 1)
                for b in range(2):
                    row = xr[:, 512 * b:512 * b + 512]
                    ins = nc.vector.tensor_tensor(row, PO[0:R, b, :], row, ALU.add)
                ins.then_inc(ev["x1"], 1)

            @block.tensor
            def _(pe):
                pe.wait_ge(qkv_in, 16)
                for r in range(5):
                    ins = nc.tensor.transpose(TR[:, r * R:(r + 1) * R], qkv[:, r * P:(r + 1) * P], ident[0:R, 0:R])
                ins.then_inc(ev["q_turned"], 1)
                pe.wait_ge(loads, 16 * 6)
                for b in range(NB):
                    ins = nc.tensor.transpose(KB[:, b, :], kc[:, b, :], ident[:])
                ins.then_inc(ev["k_turned"], 1)
                pe.wait_ge(ev["qT"], 1)
                pe.wait_ge(ev["kT"], 1)
                for g in range(KV):
                    for b in range(NB):
                        row = 32 * (b % 4)
                        ins = nc.tensor.matmul(SS[row:row + 32, g, (b // 4) * NK:(b // 4 + 1) * NK],
                                               qT[g * HD:(g + 1) * HD, b].rearrange("p r i -> p (r i)"),
                                               kT[g * HD:(g + 1) * HD, b, :], start=True, stop=True)
                ins.then_inc(ev["scored"], 1)
                pe.wait_ge(ev["probs"], 1)
                for n in range(4):
                    nc.tensor.transpose(KB[:, n, :], pr[:, n, 0:W], ident[:])
                for n in range(4):
                    ins = nc.tensor.transpose(KB[0:DEC, 4 + n, :], pr[:, n, W:NK], ident[:])
                ins.then_inc(ev["p_turned"], 1)
                pe.wait_ge(ev["ptb"], 1)
                pe.wait_ge(ev["ptn"], 1)
                for b in range(NB):
                    for g in range(KV):
                        n, row = 2 * g + b // 4, 32 * (b % 4)
                        out = PO[row:row + 32, 0, n * HD:(n + 1) * HD]
                        nc.tensor.matmul(out, ptb[:, n, row:row + 32], vc[:, b, g * HD:(g + 1) * HD], start=True, stop=False)
                        ins = nc.tensor.matmul(out, ptn[:, n, row:row + 32], vn[:, b, g * HD:(g + 1) * HD],
                                               start=False, stop=True)
                ins.then_inc(ev["weighed"], 1)
                pe.wait_ge(ev["at2"], 1)
                for j in range(AW // P):
                    ins = nc.tensor.transpose(TR[:, j * R:(j + 1) * R], at2[:, j * P:(j + 1) * P], ident[0:R, 0:R])
                ins.then_inc(ev["a_turned"], 1)
                pe.wait_ge(ev["aT"], 1)
                for b in range(2):
                    for j in range(AW // P):
                        ins = nc.tensor.matmul(PO[0:R, b, :], aT[:, j, :], w_top[:, j, 512 * b:512 * b + 512],
                                               start=(j == 0), stop=(j == AW // P - 1))
                ins.then_inc(ev["mixed"], 1)


class Shared:

    def __init__(self, c):
        self.w_top = c.sb("w_top", [P, AW // P, D])
        self.g_attn = c.sb("g_attn", [P, AW // P])
        self.ident = c.sb("ident", [P, P])
        self.half = c.sb("minus_half", [P, 1])


def run_ssm(nc, sems, a, s):
    with ExitStack() as ctx:
        c = Core(nc, ctx, sems)
        ident = c.sb("ident_c", [P, P])
        U2 = c.sb("U2", [P, L * SW])
        U2g = c.sb("U2g", [P, GRP * L * CH])
        Us = c.sb("Us", [NB, GRP, L, CH])
        XT = c.sb("XT", [P, GRP, NC])
        K16 = U2[0:CH, :].rearrange("p (g m) -> p g m", g=GRP)
        TOE = U2g[:].rearrange("p (g m) -> p g m", g=GRP)
        WBt = [c.sb(f"WBt_{x}", [P, PAIRS, P]) for x in "ri"]
        WB = [c.sb(f"WB_{x}", [P, PAIRS, P]) for x in "ri"]
        WC = [c.sb(f"WC_{x}", [P, PAIRS, (L + 1) * CH]) for x in "ri"]
        BU = [c.sb(f"BU_{x}", [P, PAIRS, NC]) for x in "ri"]
        G = [c.sb(f"G_{x}", [P, PAIRS, CK]) for x in "ri"]
        H = [c.sb(f"H_{x}", [P, PAIRS, NC + 1]) for x in "ri"]
        ROTt = WBt
        T1, T2 = (c.sb(f"T{i}", [P, PAIRS * (L + 1) * CH]) for i in (1, 2))
        lam = [c.sb(f"lam_{x}", [P, PAIRS]) for x in "ri"]
        lstep = c.sb("lstep", [P, PAIRS])
        Bm = [c.sb(f"Bm_{x}", [P, PAIRS, CH]) for x in "ri"]
        Cm = [c.sb(f"Cm_{x}", [P, PAIRS, CH]) for x in "ri"]
        BB = [c.sb(f"BB_{x}", [P, PAIRS, CH]) for x in "ri"]
        PW = [c.sb(f"PW_{x}", [P, L + 1, PAIRS]) for x in "ri"]
        PR = [c.sb(f"PR_{x}", [P, L, PAIRS]) for x in "ri"]
        h0 = [c.sb(f"h0_{x}", [P, PAIRS, NB]) for x in "ri"]
        HS = [c.sb(f"HS_{x}", [P, PAIRS, NB]) for x in "ri"]
        dsk = c.sb("dsk", [CH, GRP, CH])
        dd = c.sb("dd", [CH, GRP, CH])
        v = {n: c.sb(f"v_{n}", [P, PAIRS]) for n in
             "dt lrdt th mag mag8 k r1 r2 k2 sin cos den t t2 m1 zr zi ph k3 q1 q2 k4 us uc g1 g2".split()}
        tp1, tp2 = c.sb("tp1", [P, PAIRS * 64]), c.sb("tp2", [P, PAIRS * 64])
        PA = c.ps("PA", [P, 8, 512])
        ev = Once(c, "m")
        dv, ac, pl = c.steps("dve_steps"), c.steps("act_steps"), c.steps("pool_steps")
        loads, u_in, us_in, toe, stores = (c.sem(n) for n in ("loads_m", "u_in", "us_in", "toe_in", "stores_m"))
        copied = c.sem("bu_copied")
        y_copied = c.sem("y_copied")

        def tell(eng, name):
            eng.sem_inc(ev[name], 1)

        def mul(eng, st, dst, x, y, t1, t2, part, neg=False):
            if part == 0:
                eng.tensor_tensor(t1, x[0], y[0], ALU.mult)
                st.chain(eng, eng.tensor_tensor(t2, x[1], y[1], ALU.mult))
                st.chain(eng, eng.tensor_tensor(dst, t1, t2, ALU.subtract))
                return
            eng.tensor_tensor(t1, x[0], y[1], ALU.mult)
            st.chain(eng, eng.tensor_tensor(t2, x[1], y[0], ALU.mult))
            if neg:
                st.chain(eng, eng.scalar_tensor_tensor(dst, t1, -1.0, t2, ALU.mult, ALU.subtract))
            else:
                st.chain(eng, eng.tensor_tensor(dst, t1, t2, ALU.add))

        def reduce_angle(eng, st, r, k, x, quarter):
            st.chain(eng, eng.tensor_scalar(k, x, 1.0 / TWO_PI, 0.25 if quarter else 0.0, ALU.mult, ALU.add))
            st.chain(eng, eng.tensor_scalar(k, k, ROUND, None, ALU.add))
            st.chain(eng, eng.tensor_scalar(k, k, ROUND, None, ALU.subtract))
            st.chain(eng, eng.scalar_tensor_tensor(r, k, -PI_HI, x, ALU.mult, ALU.add))
            st.chain(eng, eng.scalar_tensor_tensor(r, k, -PI_LO, r, ALU.mult, ALU.add))
            if quarter:
                st.chain(eng, eng.tensor_scalar(r, r, float(np.float32(np.pi / 2)), None, ALU.add))
            st.chain(eng, eng.tensor_scalar(r, r, PI_MAX, -PI_MAX, ALU.min, ALU.max))

        with nc.Block() as block:

            @block.sync
            def _(sp):
                sp.dma_start(lstep[:], a["log_step"]).then_inc(loads, 16)
                for x, part in enumerate(("re", "im")):
                    sp.dma_start(lam[x][:], a[f"lam_{part}"]).then_inc(loads, 16)
                    sp.dma_start(Bm[x][:], a[f"b_{part}"]).then_inc(loads, 16)
                    sp.dma_start(Cm[x][:], a[f"c_{part}"]).then_inc(loads, 16)
                    sp.dma_start(h0[x][:], a[f"h0_{part}"]).then_inc(loads, 16)
                sp.dma_start(dsk[:].rearrange("p g c -> p (g c)"), a["d_skip"].to_broadcast([CH, SW])).then_inc(loads, 16)
                sp.dma_start(ident[:], a["ident"]).then_inc(loads, 16)
                sp.dma_start(U2[:], s["u"][0:SEQ, :].rearrange("(c j) n -> c (j n)", j=L)).then_inc(u_in, 16)
                for j in range(L):
                    src = s["u"][SEQ:SEQ + NS_ROWS, :].rearrange("(b j) (g n) -> j b g n", j=L, n=CH)
                    sp.dma_start(Us[:, :, j, :], src[j]).then_inc(us_in, 16)
                sp.wait_ge(ev["k16"], 1)
                sp.wait_ge(ev["toe_zero"], 1)
                for j in range(L):
                    sp.dma_start(TOE[j * CH:(j + 1) * CH, :, j * CH:], K16[:, :, 0:(L - j) * CH]).then_inc(toe, 16)
                sp.wait_ge(ev["h_prompt"], 1)
                sp.dma_start(a["ssm_re_prompt"], v["g1"][:]).then_inc(stores, 16)
                sp.dma_start(a["ssm_im_prompt"], v["g2"][:]).then_inc(stores, 16)
                sp.wait_ge(ev["h_sample"], 1)
                sp.dma_start(a["ssm_re_sample"], HS[0][:]).then_inc(stores, 16)
                sp.dma_start(a["ssm_im_sample"], HS[1][:]).then_inc(stores, 16)
                sp.wait_ge(y_copied, 8)
                sp.dma_start(s["y_ssm"][0:SEQ, :].rearrange("(c j) n -> c (j n)", j=L), U2[:]).then_inc(stores, 16)
                sp.wait_ge(y_copied, 16)
                for lo in (SEQ, SEQ + NS_ROWS):
                    sp.dma_start(s["y_ssm"][lo:lo + NS_ROWS, :].rearrange("(b j) n -> b (j n)", j=L),
                                 Us[:].rearrange("b g j n -> b (g j n)")).then_inc(stores, 16)
                sp.wait_ge(stores, 16 * 7)

            @block.gpsimd
            def _(pool):
                pool.wait_ge(ev["unit"], 1)
                pool.wait_ge(ev["wb_turned"], 1)
                pool.tensor_copy(ROTt[0][:, :, 0:1].rearrange("p q o -> p (q o)"), v["uc"][:])
                pl.chain(pool, pool.tensor_copy(ROTt[1][:, :, 0:1].rearrange("p q o -> p (q o)"), v["us"][:]))
                n = 1
                while n < CK:
                    x = [bcast(ROTt[i][:, :, n - 1], n, 2) for i in range(2)]
                    y = [ROTt[i][:, :, 0:n] for i in range(2)]
                    t1, t2 = (t[:, 0:PAIRS * n].rearrange("p (q n) -> p q n", n=n) for t in (tp1, tp2))
                    mul(pool, pl, ROTt[0][:, :, n:2 * n], x, y, t1, t2, 0)
                    mul(pool, pl, ROTt[1][:, :, n:2 * n], x, y, t1, t2, 1)
                    n *= 2
                tell(pool, "rot")
                pool.wait_ge(ev["u_turned"], 8)
                pool.memset(U2g[:], 0.0).then_inc(ev["toe_zero"], 1)

            @block.scalar
            def _(act):
                def f(dst, src, func, **kw):
                    ac.chain(act, nc.scalar.activation(dst, src, func, **kw))

                act.wait_ge(loads, 16 * 11)
                f(v["dt"][:], lstep[:], ACT.Exp)
                tell(act, "dt")
                act.wait_ge(ev["angle"], 1)
                nc.scalar.activation(v["mag8"][:], v["lrdt"][:], ACT.Exp, scale=float(L))
                nc.scalar.activation(v["mag"][:], v["lrdt"][:], ACT.Exp).then_inc(ev["mag"], 1)
                nc.scalar.activation(v["sin"][:], v["r1"][:], ACT.Sin)
                nc.scalar.activation(v["cos"][:], v["r2"][:], ACT.Sin).then_inc(ev["sincos"], 1)
                act.wait_ge(ev["phase"], 1)
                nc.scalar.activation(v["us"][:], v["q1"][:], ACT.Sin)
                nc.scalar.activation(v["uc"][:], v["q2"][:], ACT.Sin).then_inc(ev["unit"], 1)
                act.wait_ge(u_in, 16)
                nc.scalar.activation(U2g[:].rearrange("p (g j n) -> p j g n", j=L, n=CH),
                                     U2[:].rearrange("p (j g n) -> p j g n", j=L, n=CH), ACT.Copy).then_inc(ev["u_grouped"], 1)
                for b in range(8):
                    act.wait_ge(ev["u_turned"], b + 1)
                    nc.scalar.activation(XT[:, 4 * b:4 * b + 4, 0:CK], PA[:, b, :].rearrange("p (g n) -> p g n", n=CK),
                                         ACT.Copy).then_inc(ev["xt"], 1)
                act.wait_ge(ev["us_turned"], 1)
                nc.scalar.activation(XT[:, :, CK:NC], PA[:, 0, 0:GRP * NB].rearrange("p (g n) -> p g n", n=NB),
                                     ACT.Copy).then_inc(ev["xt"], 1)
                for b in range(8):
                    act.wait_ge(ev["wb_part"], b + 1)
                    nc.scalar.activation(WB[b // 4][:, 4 * (b % 4):4 * (b % 4) + 4, :],
                                         PA[:, b, :].rearrange("p (q n) -> p q n", n=P), ACT.Copy).then_inc(ev["wb"], 1)
                act.wait_ge(ev["k_done"], 1)
                for b in range(8):
                    ins = nc.scalar.activation(
                        K16.rearrange("p (q s) m -> p s q m", s=2)[:, b // 4, 4 * (b % 4):4 * (b % 4) + 4, :],
                        PA[0:CH, b, :].rearrange("p (q n) -> p q n", n=P), ACT.Copy)
                ins.then_inc(ev["k_copied"], 1)
                for n in range(12):
                    x, q = n // 6, 3 * (n % 6)
                    w = min(3, PAIRS - q)
                    act.wait_ge(ev["bu_part"], n + 1)
                    nc.scalar.activation(BU[x][:, q:q + w, :], PA[:, n % 8, 0:w * NC].rearrange("p (q n) -> p q n", n=NC),
                                         ACT.Copy).then_inc(copied, 1)
                act.wait_ge(toe, 16 * L)
                for b in range(8):
                    act.wait_ge(ev["y_part"], b + 1)
                    out = U2[:].rearrange("p (j q s n) -> p s q j n", j=L, q=PAIRS, s=2)[:, b // 4, 4 * (b % 4):4 * (b % 4) + 4]
                    nc.scalar.activation(out, PA[:, b, :].rearrange("p (q j n) -> p q j n", q=4, j=L),
                                         ACT.Copy).then_inc(y_copied, 1)
                for b in range(8):
                    act.wait_ge(ev["ys_part"], b + 1)
                    out = Us[:].rearrange("b g j n -> b (g j n)").rearrange(
                        "p (j q s n) -> p s q j n", j=L, q=PAIRS, s=2)[:, b // 4, 4 * (b % 4):4 * (b % 4) + 4]
                    nc.scalar.activation(out, PA[0:NB, b, :].rearrange("p (q j n) -> p q j n", q=4, j=L),
                                         ACT.Copy).then_inc(y_copied, 1)

            @block.vector
            def _(dve):
                tt, ts = nc.vector.tensor_tensor, nc.vector.tensor_scalar

                def link(ins):
                    dv.chain(dve, ins)

                dve.wait_ge(loads, 16 * 11)
                dve.wait_ge(ev["dt"], 1)
                lr, li = lam[0][:], lam[1][:]
                tt(v["lrdt"][:], lr, v["dt"][:], ALU.mult)
                link(tt(v["th"][:], li, v["dt"][:], ALU.mult))
                reduce_angle(dve, dv, v["r1"][:], v["k"][:], v["th"][:], False)
                reduce_angle(dve, dv, v["r2"][:], v["k2"][:], v["th"][:], True)
                link(ts(v["ph"][:], v["r1"][:], float(L), None, ALU.mult))
                tell(dve, "angle")
                reduce_angle(dve, dv, v["q1"][:], v["k3"][:], v["ph"][:], False)
                reduce_angle(dve, dv, v["q2"][:], v["k4"][:], v["ph"][:], True)
                tell(dve, "phase")
                dve.wait_ge(ev["mag"], 1)
                dve.wait_ge(ev["sincos"], 1)
                nc.vector.memset(PW[0][:, 0, :], 1.0)
                nc.vector.memset(PW[1][:, 0, :], 0.0)
                tt(PW[0][:, 1, :], v["mag"][:], v["cos"][:], ALU.mult)
                link(tt(PW[1][:, 1, :], v["mag"][:], v["sin"][:], ALU.mult))
                ab = [PW[i][:, 1, :] for i in range(2)]
                for n in (1, 2, 4):
                    x = [bcast(PW[i][:, n, :], n, 1) for i in range(2)]
                    y = [PW[i][:, 1:n + 1, :] for i in range(2)]
                    t1, t2 = (t[:, 0:n * PAIRS].rearrange("p (n q) -> p n q", n=n) for t in (T1, T2))
                    mul(nc.vector, dv, PW[0][:, n + 1:2 * n + 1, :], x, y, t1, t2, 0)
                    mul(nc.vector, dv, PW[1][:, n + 1:2 * n + 1, :], x, y, t1, t2, 1)
                for i in range(2):
                    for j in range(L):
                        ins = nc.vector.tensor_copy(PR[i][:, j, :], PW[i][:, L - 1 - j, :])
                link(ins)
                tt(v["t"][:], lr, lr, ALU.mult)
                link(tt(v["t2"][:], li, li, ALU.mult))
                link(tt(v["den"][:], v["t"][:], v["t2"][:], ALU.add))
                link(nc.vector.reciprocal(v["den"][:], v["den"][:]))
                link(ts(v["m1"][:], ab[0], 1.0, None, ALU.subtract))
                tt(v["t"][:], v["m1"][:], lr, ALU.mult)
                link(tt(v["t2"][:], ab[1], li, ALU.mult))
                link(tt(v["zr"][:], v["t"][:], v["t2"][:], ALU.add))
                tt(v["t"][:], ab[1], lr, ALU.mult)
                link(tt(v["t2"][:], v["m1"][:], li, ALU.mult))
                link(tt(v["zi"][:], v["t"][:], v["t2"][:], ALU.subtract))
                tt(v["zr"][:], v["zr"][:], v["den"][:], ALU.mult)
                link(tt(v["zi"][:], v["zi"][:], v["den"][:], ALU.mult))
                z = [bcast(v["zr"][:], CH, 2), bcast(v["zi"][:], CH, 2)]
                t1, t2 = (t[:, 0:PAIRS * CH].rearrange("p (q n) -> p q n", n=CH) for t in (T1, T2))
                mul(nc.vector, dv, BB[0][:], z, [m[:] for m in Bm], t1, t2, 0)
                mul(nc.vector, dv, BB[1][:], z, [m[:] for m in Bm], t1, t2, 1)
                x = [bcast(PR[i][:].rearrange("p t q -> p q t"), CH, 3) for i in range(2)]
                y = [bcast(BB[i][:], L, 2) for i in range(2)]
                t1, t2 = (t[:, 0:PAIRS * P].rearrange("p (q t n) -> p q t n", t=L, n=CH) for t in (T1, T2))
                for i in range(2):
                    mul(nc.vector, dv, WBt[i][:].rearrange("p q (t n) -> p q t n", n=CH), x, y, t1, t2, i)
                    tell(dve, "wbt")
                x = [bcast(PW[i][:].rearrange("p t q -> p q t"), CH, 3) for i in range(2)]
                y = [bcast(Cm[i][:], L + 1, 2) for i in range(2)]
                t1, t2 = (t[:].rearrange("p (q t n) -> p q t n", t=L + 1, n=CH) for t in (T1, T2))
                mul(nc.vector, dv, WC[0][:].rearrange("p q (t n) -> p q t n", n=CH), x, y, t1, t2, 0)
                nc.vector.tensor_tensor(t1, x[0], y[1], ALU.mult)
                link(nc.vector.tensor_tensor(t2, x[1], y[0], ALU.mult))
                nc.vector.scalar_tensor_tensor(WC[1][:].rearrange("p q m -> p (q m)"), T1[:], -1.0, T2[:],
                                               ALU.mult, ALU.subtract).then_inc(ev["wc"], 1)
                for i in range(2):
                    nc.vector.memset(H[i][:, :, 0:1], 0.0)
                    ins = nc.vector.tensor_copy(H[i][:, :, CK + 1:NC + 1], h0[i][:])
                link(ins)
                link(tt(dd[:], dsk[:], bcast(ident[0:CH, 0:CH], GRP, 1), ALU.mult))
                dve.wait_ge(ev["k_copied"], 1)
                tt(K16[:, :, 0:CH], K16[:, :, 0:CH], dd[:], ALU.add).then_inc(ev["k16"], 1)
                dve.wait_ge(copied, 12)
                dve.wait_ge(ev["rot"], 1)
                dve.wait_ge(ev["wc"], 1)
                rot = [r[:] for r in ROTt]
                bu = [b[:, :, 0:CK] for b in BU]
                t1, t2 = (t[:, 0:PAIRS * CK].rearrange("p (q n) -> p q n", n=CK) for t in (T1, T2))
                tt(t1, rot[0], bu[0], ALU.mult)
                link(tt(t2, rot[1], bu[1], ALU.mult))
                link(tt(G[0][:], t1, t2, ALU.add))
                tt(t1, rot[0], bu[1], ALU.mult)
                link(tt(t2, rot[1], bu[0], ALU.mult))
                link(tt(G[1][:], t1, t2, ALU.subtract))
                for i in range(2):
                    for q in range(PAIRS):
                        ins = nc.vector.tensor_tensor_scan(G[i][:, q, :], v["mag8"][:, q:q + 1].to_broadcast([P, CK]),
                                                           G[i][:, q, :], 0.0, ALU.mult, ALU.add)
                link(ins)
                g = [x[:] for x in G]
                for i in range(2):
                    mul(nc.vector, dv, H[i][:, :, 1:CK + 1], rot, g, t1, t2, i)
                tell(dve, "h")
                nc.vector.tensor_copy(v["g1"][:], H[0][:, :, CK])
                nc.vector.tensor_copy(v["g2"][:], H[1][:, :, CK]).then_inc(ev["h_prompt"], 1)
                x = [bcast(PW[i][:, L, :], NB, 2) for i in range(2)]
                y = [h0[i][:] for i in range(2)]
                t1, t2 = (t[:, 0:PAIRS * NB].rearrange("p (q n) -> p q n", n=NB) for t in (T1, T2))
                for i in range(2):
                    mul(nc.vector, dv, HS[i][:], x, y, t1, t2, i)
                    link(tt(HS[i][:], HS[i][:], BU[i][:, :, CK:NC], ALU.add))
                tell(dve, "h_sample")

            @block.tensor
            def _(pe):
                pe.wait_ge(loads, 16 * 11)
                pe.wait_ge(ev["u_grouped"], 1)
                for g in range(GRP):
                    ins = nc.tensor.transpose(PA[:, g // 4, (g % 4) * P:(g % 4 + 1) * P], U2g[:, g * P:(g + 1) * P], ident[:])
                    if g % 4 == 3:
                        ins.then_inc(ev["u_turned"], 1)
                pe.wait_ge(us_in, 16 * L)
                pe.wait_ge(ev["xt"], 1)
                for g in range(GRP):
                    ins = nc.tensor.transpose(PA[:, 0, g * NB:(g + 1) * NB], Us[:, g].rearrange("b j n -> b (j n)"),
                                              ident[0:NB, 0:NB])
                ins.then_inc(ev["us_turned"], 1)
                pe.wait_ge(ev["xt"], 9)
                for b in range(8):
                    pe.wait_ge(ev["wbt"], b // 4 + 1)
                    for n in range(4):
                        q = 4 * (b % 4) + n
                        ins = nc.tensor.transpose(PA[:, b, n * P:(n + 1) * P], WBt[b // 4][:, q, :], ident[:])
                    ins.then_inc(ev["wb_part"], 1)
                pe.wait_ge(ev["wb"], 8)
                tell(pe, "wb_turned")
                pe.wait_ge(ev["wc"], 1)
                for q in range(PAIRS):
                    for h in range(2):
                        rows = slice(h * ST, (h + 1) * ST)
                        out = PA[0:CH, 4 * h + q // 4, (q % 4) * P:(q % 4 + 1) * P]
                        for i in range(2):
                            ins = nc.tensor.matmul(out, BB[i][rows, q, :], WC[i][rows, q, 0:P], start=(i == 0), stop=(i == 1))
                ins.then_inc(ev["k_done"], 1)
                pe.wait_ge(ev["k_copied"], 1)
                for n in range(12):
                    x, q0 = n // 6, 3 * (n % 6)
                    if n >= 8:
                        pe.wait_ge(copied, n - 7)
                    for q in range(q0, min(q0 + 3, PAIRS)):
                        for h in range(2):
                            rows = slice(h * ST, (h + 1) * ST)
                            ins = nc.tensor.matmul(PA[rows, n % 8, (q - q0) * NC:(q - q0 + 1) * NC],
                                                   WB[x][:, q, rows], XT[:, 2 * q + h, :], start=True, stop=True)
                    ins.then_inc(ev["bu_part"], 1)
                pe.wait_ge(copied, 12)
                pe.wait_ge(ev["h"], 1)
                pe.wait_ge(toe, 16 * L)

                def outputs(b, lo, hi, xlo, part):
                    h = b // 4
                    rows = slice(h * ST, (h + 1) * ST)
                    for n in range(4):
                        q = 4 * (b % 4) + n
                        out = PA[0:hi - lo, b, n * P:(n + 1) * P]
                        nc.tensor.matmul(out, XT[:, 2 * q + h, xlo:xlo + hi - lo], TOE[:, 2 * q + h, :], start=True, stop=False)
                        nc.tensor.matmul(out, H[0][rows, q, lo:hi], WC[0][rows, q, CH:], start=False, stop=False)
                        ins = nc.tensor.matmul(out, H[1][rows, q, lo:hi], WC[1][rows, q, CH:], start=False, stop=True)
                    ins.then_inc(part, 1)

                for b in range(8):
                    outputs(b, 0, CK, 0, ev["y_part"])
                for b in range(8):
                    pe.wait_ge(y_copied, b + 1)
                    outputs(b, CK + 1, NC + 1, CK, ev["ys_part"])


class PerTile:

    def __init__(self, sem, per):
        self.sem, self.n, self.base, self.per = sem, 0, 0, per

    def chain(self, eng, t, ins, nop=False):
        self.n += 1
        ins.then_inc(self.sem, 1)
        eng.wait_ge(self.sem, self.n if t is None else self.base + t * self.per + self.n)
        if nop:
            eng.nop(nofuse=True)

    def loop_begins(self):
        self.base, self.n = self.n, 0

    def turn_ends(self):
        assert self.n == self.per, (self.n, self.per)
        self.n = 0


def retrieve_experts(nc, sems, a, s):
    with ExitStack() as ctx:
        c = Core(nc, ctx, sems)
        KS, NSLOT, UR, VR, DG = TOPK, EH * TOPK, 8, 4, 4
        DVE_STEPS = 130
        HC = 2 * EH
        BLOCKS = ((0, 2, 16), (2, 4, 5), (4, 8, 3), (8, 16, 1))
        NCAND = sum((a1 - a0) * b for a0, a1, b in BLOCKS)
        LOWEST = float(np.finfo(np.float32).min)
        wq = c.sb("wq", [P, KD, EH * 2 * QH])
        keys = c.sb("keys", [QH, HC, KEYS])
        w_bot = c.sb("w_bot", [P, SW // P, D])
        w_glu = c.sb("w_glu", [P, SW // P, SW])
        b_glu = c.sb("b_glu", [P, SW])
        g_ffn = c.sb("g_ffn", [P, D])
        g_fin = c.sb("g_fin", [P, D])
        g_ssm = c.sb("g_ssm", [P, SW // P])
        ident = c.sb("ident_d", [P, P])
        fold = c.sb("fold", [P, P])
        place = c.sb("place", [P, NCAND])
        u_ring = c.sb("u_ring", [P, UR, D])
        v_ring = c.sb("v_ring", [P, VR, D])
        xr = c.sb("xr", [P, D])
        xn_next = c.sb("xn_next", [P, D])
        xn = c.sb("xn", [P, D])
        xo = c.sb("xo", [P, D])
        xnT = c.sb("xnT", [P, KD, P])
        qT = c.sb("qTe", [P, EH, P])
        S = c.sb("S", [P, EH, KEYS])
        y = c.sb("y", [P, SW])
        z = c.sb("z", [P, SW])
        yT = c.sb("yT", [P, SW // P, P])
        dg = c.sb("dg", [P, DG, P])
        top_v = c.sb("top_v", [P, EH, 2, KS])
        top_i = c.sb("top_i", [P, EH, 2, KS], U32)
        top_f = c.sb("top_f", [P, EH, 2, KS])
        left = c.sb("left", [P, KEYS])
        cand = c.sb("cand", [P, EH, NCAND])
        cid = c.sb("cid", [P, EH, NCAND])
        best = c.sb("best", [P, EH, KS])
        pos = c.sb("pos", [P, EH, KS], U32)
        pos_f = c.sb("pos_f", [P, EH, KS])
        idx_f = c.sb("idx_f", [P, EH, KS])
        idx_next = c.sb("idx_next", [P, NSLOT], U32)
        idx = c.sb("idx", [P, NSLOT], U32)
        idx_first = c.sb("idx_first", [P, KS], U32)
        idx_last = c.sb("idx_last", [P, KS], U32)
        ex = c.sb("ex", [P, EH, KS])
        gate_next = c.sb("gate_next", [P, NSLOT])
        gate = c.sb("gate", [P, NSLOT])
        dot = c.sb("dot", [P, NSLOT])
        act_w = c.sb("act_w", [P, NSLOT])
        wgt = c.sb("wgt", [P, NSLOT])
        stat = c.sb("stat_e", [P, 16])
        nmax, esum = c.sb("nmax", [P, EH]), c.sb("esum", [P, EH])
        match = S[:].rearrange("p h n -> p (h n)")[:, 0:KS * NCAND].rearrange("p (k n) -> p k n", n=NCAND)
        squares = S[:].rearrange("p h n -> p (h n)")
        (ss_y, ms_y, sd_y, rs_y, ss_x, ms_x, sd_x, rs_x, ss_o, ms_o, sd_o, rs_o) = (stat[:, i:i + 1] for i in range(12))
        ACC = c.ps("ACC", [P, 2, 512])
        TQ = c.ps("TQ", [P, 2, 512])
        ZS = c.ps("ZS", [P, 2, 512])
        OP = c.ps("OP", [P, 2, 512])
        acc = ACC[:].rearrange("p b n -> p (b n)")

        weights = c.sem("weights_e")
        early = c.sem("weights_e1")
        y_in, xr_in = c.count("y_in", 16), c.count("xr_in", 16)
        stored = c.sem("stored_e")
        k = {n: c.count(n) for n in (
            "y_gelu y_turned yT_done z_done zb_done gate_y sd_y_done yn_done yn_turned ynT_done bot_done xr_done "
            "sd_x_done xn_done xn_turned xnT_done q_a q_b q_c q_d qT_a qT_b qT_c qT_d s_a s_b S_a S_b topped_a topped_b "
            "idx_ready nmax_done ex_done gate_ready idx_taken first_taken last_taken xn_taken gate_taken acc_begun acc_taken "
            "ss_o_done ms_y_done ms_x_done ms_o_done sd_o_done out_ready out_stored").split()}
        u_in = [c.sem(f"u_in{i}") for i in range(UR)]
        v_in = [c.sem(f"v_in{i}") for i in range(VR)]
        dots = c.sem("dots_done")
        pv = c.sem("v_used")
        gelus, wgts, diags = c.sem("gelus"), c.sem("weights_done"), c.sem("diags_done")
        dch = PerTile(c.sem("dve_steps_e"), DVE_STEPS)

        def ring_in(eng, sems, t, s_):
            n = len(sems)
            eng.wait_ge(sems[s_ % n], t * (16 * NSLOT // n) + 16 * (s_ // n + 1))

        def blocks(turn, t):
            if turn == "samples":
                return [(h, (t, h) if h < EH // 2 else None, None) for h in range(1, EH // 2 + 1)]
            return ([(h, (t, h), (t + 1, h)) for h in range(1, EH)]
                    + [(EH, (t + 1, 0), (t + 2, 0) if turn == "steady" else None)])

        with nc.Block() as block:

            @block.sync
            def _(sp):
                def load_y(t):
                    k["yn_turned"].held(sp, t - 1)
                    y_in.mark(sp.dma_start(y[:], s["y_ssm"][bass.ts(t, P), :]))

                def load_xr(t):
                    k["acc_begun"].held(sp, t - 1)
                    xr_in.mark(sp.dma_start(xr[:], s["x1"][bass.ts(t, P), :]))

                def out(t, n):
                    k["out_ready"].held(sp, t)
                    dst = a["y"][bass.ts(t, P), :] if n == P else a["y"][SEQ:SEQ + n, :]
                    sp.dma_start(dst, xo[0:n, :]).then_inc(stored, 16)
                    sp.wait_ge(stored, (t + 1) * 16)
                    sp.nop(nofuse=True)
                    sp.sem_inc(k["out_stored"].sem, 1)

                k["out_stored"].prime(sp)
                load_y(0)
                load_xr(0)
                sp.dma_start(ident[:], a["ident"]).then_inc(early, 16)
                sp.dma_start(w_glu[:], a["w_glu"].rearrange("(k p) n -> p k n", p=P)).then_inc(early, 16)
                sp.dma_start(b_glu[:], a["b_glu"].to_broadcast([P, SW])).then_inc(early, 16)
                sp.dma_start(g_ssm[:], a["g_ssm"]).then_inc(early, 16)
                sp.dma_start(w_bot[:], a["w_out"][AW:D, :].rearrange("(k p) n -> p k n", p=P)).then_inc(weights, 16)
                sp.dma_start(fold[:], a["fold"]).then_inc(weights, 16)
                sp.dma_start(g_ffn[:], a["g_ffn"].to_broadcast([P, D])).then_inc(weights, 16)
                sp.dma_start(g_fin[:], a["g_final"].to_broadcast([P, D])).then_inc(weights, 16)
                sp.dma_start(place[:], a["place"].to_broadcast([P, NCAND])).then_inc(weights, 16)
                sp.dma_start(keys[:].rearrange("d c n -> d (c n)"), a["keys"]).then_inc(weights, 16)
                sp.dma_start(wq[:], a["w_query"].rearrange("(k p) n -> p k n", p=P)).then_inc(weights, 16)
                load_y(1)
                with sp.Fori(0, PT - 1) as t:
                    load_xr(t + 1)
                    load_y(t + 2)
                    out(t, P)
                load_xr(PT)
                out(PT - 1, P)
                out(PT, NS_ROWS)

            @block.gpsimd
            def _(pool):
                def gather(ring, table, which, col, sems, s_):
                    pool.indirect_dma_start(
                        out=ring[:, s_ % len(sems), :], out_offset=None, in_=a[table],
                        in_offset=bass.IndirectOffsetOnAxis(ap=which[:, col:col + 1], axis=0)
                        ).then_inc(sems[s_ % len(sems)], 16)

                def gather_u(t, h, j):
                    s_ = KS * h + j
                    pool.wait_ge(dots, t * NSLOT + s_ + 1)
                    pool.nop(nofuse=True)
                    gather(u_ring, "u_table", *((idx_first, j) if h == 0 else (idx, s_)), u_in, s_)

                def gather_v(t, h, j):
                    s_ = KS * h + j
                    pool.wait_ge(pv, t * NSLOT + s_ + 1)
                    pool.nop(nofuse=True)
                    gather(v_ring, "v_table", *((idx_last, j) if h == EH - 1 else (idx, s_)), v_in, s_)

                def retrieve(turn, t):
                    k["idx_taken"].held(pool, t)
                    for h, u, _ in blocks(turn, t):
                        if h == EH:
                            k["last_taken"].held(pool, t)
                            k["first_taken"].held(pool, t + 1)
                        for j in range(KS):
                            if u:
                                gather_u(*u, j)
                            gather_v(t, h - 1, j)

                k["first_taken"].held(pool, 0)
                for j in range(KS):
                    gather_u(0, 0, j)
                with pool.Fori(0, PT - 1) as t:
                    retrieve("steady", t)
                retrieve("eighth", PT - 1)
                retrieve("samples", PT)

            @block.scalar
            def _(act):
                A = nc.scalar.activation

                def flat(x):
                    return x.rearrange("p b n -> p (b n)")

                def prepare(t, h, j):
                    at = (h, j)
                    if at == (0, 3):
                        y_in.of(act, t)
                        k["y_gelu"].mark(A(y[:], y[:], ACT.Gelu))
                    elif at == (0, 6):
                        k["y_turned"].of(act, t)
                        k["yT_done"].mark(A(flat(yT[:]), TQ[:, 0, :], ACT.Copy))
                    elif at == (0, 14):
                        k["zb_done"].of(act, t)
                        k["gate_y"].mark(A(z[:], z[:], ACT.Sigmoid))
                    elif at == (1, 6):
                        k["ms_y_done"].of(act, t)
                        k["sd_y_done"].mark(A(sd_y, ms_y, ACT.Sqrt))
                    elif at == (2, 9):
                        k["ms_x_done"].of(act, t)
                        k["sd_x_done"].mark(A(sd_x, ms_x, ACT.Sqrt))
                    elif at == (3, 2):
                        k["xn_turned"].of(act, t)
                        A(flat(xnT[:, 0:4, :]), TQ[:, 0, :], ACT.Copy)
                        k["xnT_done"].mark(A(flat(xnT[:, 4:8, :]), TQ[:, 1, :], ACT.Copy))
                    elif at in ((3, 8), (3, 12), (4, 4), (4, 8)):
                        n = "abcd"[((3, 8), (3, 12), (4, 4), (4, 8)).index(at)]
                        b = n in "bd"
                        k[f"q_{n}"].of(act, t)
                        k[f"qT_{n}"].mark(A(flat(qT[:, 4 * b:4 * b + 4, :]), TQ[:, int(b), :], ACT.Copy))
                    elif at in ((3, 15), (5, 0)):
                        n = "ab"[at == (5, 0)]
                        k[f"s_{n}"].of(act, t)
                        if n == "b":
                            k["topped_a"].of(act, t)
                        A(flat(S[:, 0:4, :]), ZS[:, 0, :], ACT.Copy)
                        k[f"S_{n}"].mark(A(flat(S[:, 4:8, :]), ZS[:, 1, :], ACT.Copy))
                    elif at == (6, 12):
                        k["nmax_done"].of(act, t)
                        for e in range(EH):
                            ins = A(ex[:, e, :], best[:, e, :], ACT.Exp, bias=nmax[:, e:e + 1], accum_out=esum[:, e:e + 1])
                        k["ex_done"].mark(ins)

                def take_rows(t):
                    k["xn_done"].of(act, t)
                    act.wait_ge(dots, t * NSLOT + UR)
                    k["xn_taken"].mark(A(xn[:], xn_next[:], ACT.Copy))

                def take_gates(t, halves):
                    k["gate_ready"].of(act, t)
                    if not isinstance(t, int) or t > 0:
                        act.wait_ge(wgts, t * EH)
                    for lo, hi, up in ((0, NS_ROWS, NSLOT // 2), (NS_ROWS, P, NSLOT)) if halves else ((0, P, NSLOT),):
                        n = NSLOT // 2 if halves else NSLOT
                        ins = A(gate[lo:hi, 0:n], gate_next[lo:hi, up - n:up], ACT.Copy)
                    k["gate_taken"].mark(ins)

                def activate(t, h):
                    act.wait_ge(dots, t * NSLOT + KS * (h + 1) + UR)
                    cols = slice(KS * h, KS * (h + 1))
                    A(act_w[:, cols], dot[:, cols], ACT.Gelu).then_inc(gelus, 1)

                def root_out(t, n):
                    k["ms_o_done"].of(act, t)
                    k["sd_o_done"].mark(A(sd_o[0:n], ms_o[0:n], ACT.Sqrt))

                def retrieve(turn, t):
                    diag = fold if turn == "samples" else ident
                    for h, u, prep in blocks(turn, t):
                        for j in range(KS):
                            s_ = KS * (h - 1) + j
                            if j == 0:
                                act.wait_ge(wgts, t * EH + h)
                            act.wait_ge(pv, t * NSLOT + s_ + 1)
                            A(dg[:, s_ % DG, :], diag[:], ACT.Copy, scale=wgt[:, s_:s_ + 1]).then_inc(diags, 1)
                            if (h, j) == (EH, KS // 2):
                                take_gates(t + 1, turn == "eighth")
                            if prep:
                                prepare(*prep, j)
                        if u and u[1] == EH - 1:
                            take_rows(t + 1)
                        if u:
                            activate(*u)
                    root_out(t, NS_ROWS if turn == "samples" else P)

                for n in ("y_gelu yT_done gate_y sd_y_done sd_x_done xnT_done qT_a qT_b qT_c qT_d S_a S_b ex_done "
                          "xn_taken gate_taken sd_o_done").split():
                    k[n].prime(act)
                act.wait_ge(early, 64)
                for h in range(EH):
                    for j in range(KS):
                        prepare(0, h, j)
                take_rows(0)
                take_gates(0, False)
                for j in range(KS):
                    prepare(1, 0, j)
                activate(0, 0)
                with act.Fori(0, PT - 1) as t:
                    retrieve("steady", t)
                retrieve("eighth", PT - 1)
                retrieve("samples", PT)

            @block.vector
            def _(dve):
                V = nc.vector

                turn_now = [None]

                def dch_(ins, nop=False):
                    dch.chain(dve, turn_now[0], ins, nop)

                def best16(vals, where, src, tmp):
                    dch_(V.max(vals[:, 0:8], src), True)
                    V.max_index(where[:, 0:8], vals[:, 0:8], src)
                    dch_(V.match_replace(tmp, vals[:, 0:8], src, LOWEST), True)
                    dch_(V.max(vals[:, 8:16], tmp), True)
                    dch_(V.max_index(where[:, 8:16], vals[:, 8:16], tmp), True)

                def pairwise(src, dst, op):
                    n = 0
                    for a0, a1, w in BLOCKS:
                        m = a1 - a0
                        x = bcast(src[:, :, 0, a0:a1], w, 3)
                        yy = bcast(src[:, :, 1, 0:w], m, 2)
                        ins = V.tensor_tensor(dst[:, :, n:n + m * w].rearrange("p h (m w) -> p h m w", w=w), x, yy, op)
                        n += m * w
                    return ins

                def prepare(t, h, j):
                    at = (h, j)
                    if at == (0, 13):
                        k["z_done"].of(dve, t)
                        k["zb_done"].mark(V.tensor_tensor(z[:], ZS[:, 0, :], b_glu[:], ALU.add))
                    elif at == (1, 3):
                        k["gate_y"].of(dve, t)
                        dch_(V.tensor_tensor(y[:], y[:], z[:], ALU.mult))
                        dch_(V.tensor_tensor_reduce(z[:], y[:], y[:], 1.0, 0.0, ALU.mult, ALU.add, ss_y))
                        k["ms_y_done"].mark(V.tensor_scalar(ms_y, ss_y, 1.0 / SW, EPS, ALU.mult, ALU.add))
                    elif at == (1, 9):
                        k["sd_y_done"].of(dve, t)
                        dch_(V.reciprocal(rs_y, sd_y))
                        k["yn_done"].mark(V.tensor_scalar(y[:], y[:], rs_y, None, ALU.mult))
                    elif at == (1, 13):
                        k["yn_turned"].of(dve, t)
                        k["ynT_done"].mark(V.tensor_tensor(yT[:], TQ[:, 0, :].rearrange("p (k n) -> p k n", n=P),
                                                           bcast(g_ssm[:], P, 2), ALU.mult))
                    elif at == (2, 6):
                        k["bot_done"].of(dve, t)
                        xr_in.of(dve, t)
                        k["xn_taken"].of(dve, t - 1)
                        V.tensor_tensor(xr[:, 0:512], OP[:, 0, :], xr[:, 0:512], ALU.add)
                        dch_(V.tensor_tensor(xr[:, 512:D], OP[:, 1, :], xr[:, 512:D], ALU.add))
                        k["xr_done"].mark(V.tensor_tensor_reduce(xn_next[:], xr[:], xr[:], 1.0, 0.0, ALU.mult, ALU.add, ss_x))
                        k["xr_done"].of(dve, t)
                        k["ms_x_done"].mark(V.tensor_scalar(ms_x, ss_x, 1.0 / D, EPS, ALU.mult, ALU.add))
                    elif at == (2, 12):
                        k["sd_x_done"].of(dve, t)
                        dch_(V.reciprocal(rs_x, sd_x))
                        k["xn_done"].mark(V.scalar_tensor_tensor(xn_next[:], xr[:], rs_x, g_ffn[:], ALU.mult, ALU.mult))
                    elif h in (4, 5) and j % 2 == 1:
                        n, i = "ab"[h == 5], j // 2
                        e = 4 * (h == 5) + i // 2
                        if i == 0:
                            k[f"S_{n}"].held(dve, t)
                        best16(top_v[:, e, i % 2, :], top_i[:, e, i % 2, :], S[:, i, :], left[:])
                        if i == 7:
                            dve.sem_inc(k[f"topped_{n}"].sem, 1)
                    elif at == (6, 1):
                        dch_(V.tensor_copy(top_f[:], top_i[:]))
                        dch_(V.tensor_scalar(top_f[:, :, 0, :], top_f[:, :, 0, :], float(KEYS), None, ALU.mult))
                        pairwise(top_v, cand, ALU.add)
                        dch_(pairwise(top_f, cid, ALU.add), True)
                    elif h == 6 and 2 <= j < 2 + EH:
                        e = j - 2
                        best16(best[:, e, :], pos[:, e, :], cand[:, e, :], left[:, 0:NCAND])
                    elif at == (6, 10):
                        V.tensor_copy(pos_f[:], pos[:])
                        k["nmax_done"].mark(V.tensor_scalar(nmax[:], best[:, :, 0:1].rearrange("p h o -> p (h o)"), -1.0, None, ALU.mult))
                        k["nmax_done"].of(dve, t)
                    elif at == (6, 14) or (h == 7 and j <= 12 and j % 2 == 0):
                        e = 0 if h == 6 else 1 + j // 2
                        dch_(V.tensor_tensor(match, bcast(place[:], KS, 1), bcast(pos_f[:, e, :], NCAND, 2), ALU.is_equal))
                        dch_(V.tensor_tensor(match, match, bcast(cid[:, e, :], KS, 1), ALU.mult))
                        dch_(V.tensor_reduce(idx_f[:, e, :], match, AX.X, ALU.add))
                    elif at == (7, 13):
                        k["idx_taken"].of(dve, t - 1)
                        k["gate_taken"].of(dve, t - 1)
                        k["idx_ready"].mark(V.tensor_copy(idx_next[:], idx_f[:].rearrange("p h k -> p (h k)")))
                        k["idx_ready"].of(dve, t)
                        k["ex_done"].of(dve, t)
                        dch_(V.reciprocal(esum[:], esum[:]))
                        k["gate_ready"].mark(V.tensor_tensor(gate_next[:].rearrange("p (h k) -> p h k", k=KS), ex[:],
                                                             bcast(esum[:], KS, 2), ALU.mult))

                def take(t, mark, dst, h0, n, halves, src=idx_next):
                    for lo, hi, up in ((0, NS_ROWS, 0), (NS_ROWS, P, EH // 2)) if halves else ((0, P, 0),):
                        cols = slice(KS * (h0 + up), KS * (h0 + up + n))
                        ins = V.tensor_copy(dst[lo:hi, 0:KS * n], src[lo:hi, cols])
                    mark.mark(ins)

                def take_first(t, halves):
                    k["idx_ready"].of(dve, t)
                    take(t, k["first_taken"], idx_first, 0, 1, halves)

                def take_rest(t, halves):
                    take(t, k["idx_taken"], idx, 0, EH // 2 if halves else EH, halves)

                def take_last(t):
                    k["idx_taken"].of(dve, t)
                    take(t, k["last_taken"], idx_last, EH - 1, 1, False, src=idx)

                def product(t, h, j):
                    s_ = KS * h + j
                    if s_ == 0:
                        k["xn_taken"].held(dve, t)
                    ring_in(dve, u_in, t, s_)
                    row = u_ring[:, s_ % UR, :]
                    V.tensor_tensor_reduce(row, row, xn[:], 1.0, 0.0, ALU.mult, ALU.add, dot[:, s_:s_ + 1]).then_inc(dots, 1)

                def weigh(t, h):
                    cols = slice(KS * h, KS * (h + 1))
                    dve.wait_ge(gelus, t * EH + h + 1)
                    V.tensor_tensor(wgt[:, cols], act_w[:, cols], gate[:, cols], ALU.mult).then_inc(wgts, 1)

                def sum_out(t, n, used):
                    k["out_stored"].of(dve, t - 1)
                    dve.wait_ge(pv, used + VR)
                    k["acc_taken"].mark(V.tensor_copy(xo[0:n, :], acc[0:n, :]))
                    k["acc_taken"].of(dve, t)
                    k["ss_o_done"].mark(V.tensor_tensor_reduce(squares[0:n, :], xo[0:n, :], xo[0:n, :], 1.0, 0.0,
                                                               ALU.mult, ALU.add, ss_o[0:n]))
                    k["ss_o_done"].of(dve, t)
                    k["ms_o_done"].mark(V.tensor_scalar(ms_o[0:n], ss_o[0:n], 1.0 / D, EPS, ALU.mult, ALU.add))

                def norm_out(t, n):
                    k["sd_o_done"].of(dve, t)
                    dch_(V.reciprocal(rs_o[0:n], sd_o[0:n]))
                    k["out_ready"].mark(V.scalar_tensor_tensor(xo[0:n, :], xo[0:n, :], rs_o[0:n], g_fin[0:n, :],
                                                               ALU.mult, ALU.mult))

                def retrieve(turn, t):
                    turn_now[0] = t
                    for h, u, prep in blocks(turn, t):
                        for j in range(KS):
                            if u:
                                product(*u, j)
                            if j == 0:
                                weigh(t, h - 1)
                            if (h, j) == (2, 0) and turn != "samples":
                                take_last(t)
                            if prep:
                                prepare(*prep, j)
                            if (h, j) == (EH - 1, KS - 1) and turn != "samples":
                                take_first(t + 1, turn == "eighth")
                            if (h, j) == (EH, KS // 2):
                                dve.wait_ge(pv, t * NSLOT + NSLOT - KS + VR)
                                take_rest(t + 1, turn == "eighth")
                    n, slots = (NS_ROWS, NSLOT // 2) if turn == "samples" else (P, NSLOT)
                    sum_out(t, n, t * NSLOT + slots)
                    norm_out(t, n)

                for n in ("zb_done yn_done ynT_done xr_done xn_done topped_a topped_b first_taken last_taken idx_taken idx_ready nmax_done gate_ready "
                          "acc_taken ss_o_done ms_y_done ms_x_done ms_o_done out_ready").split():
                    k[n].prime(dve)
                dve.sem_inc(dots, UR)
                dve.wait_ge(early, 64)
                dve.wait_ge(weights, 16 * 7)
                for h in range(EH):
                    for j in range(KS):
                        prepare(0, h, j)
                take_first(0, False)
                take_rest(0, False)
                for j in range(KS):
                    product(0, 0, j)
                    prepare(1, 0, j)
                dch.loop_begins()
                with dve.Fori(0, PT - 1) as t:
                    retrieve("steady", t)
                dch.turn_ends()
                retrieve("eighth", PT - 1)
                dch.turn_ends()
                retrieve("samples", PT)

            @block.tensor
            def _(pe):
                def prepare(t, h, j):
                    at = (h, j)
                    if at == (0, 4):
                        k["y_gelu"].of(pe, t)
                        k["xnT_done"].of(pe, t - 1)
                        for n in range(SW // P):
                            ins = nc.tensor.transpose(TQ[:, 0, n * P:(n + 1) * P], y[:, n * P:(n + 1) * P], ident[:])
                        k["y_turned"].mark(ins)
                    elif at == (0, 9):
                        k["yT_done"].of(pe, t)
                        k["S_b"].of(pe, t - 1)
                        for n in range(SW // P):
                            ins = nc.tensor.matmul(ZS[:, 0, :], yT[:, n, :], w_glu[:, n, :], start=(n == 0), stop=(n == SW // P - 1))
                        k["z_done"].mark(ins)
                    elif at == (1, 11):
                        k["yn_done"].of(pe, t)
                        for n in range(SW // P):
                            ins = nc.tensor.transpose(TQ[:, 0, n * P:(n + 1) * P], y[:, n * P:(n + 1) * P], ident[:])
                        k["yn_turned"].mark(ins)
                    elif at in ((2, 1), (2, 3)):
                        b = int(at == (2, 3))
                        k["ynT_done"].of(pe, t)
                        k["xr_done"].of(pe, t - 1)
                        for n in range(SW // P):
                            ins = nc.tensor.matmul(OP[:, b, :], yT[:, n, :], w_bot[:, n, 512 * b:512 * b + 512],
                                                   start=(n == 0), stop=(n == SW // P - 1))
                        if b:
                            k["bot_done"].mark(ins)
                    elif at == (2, 15):
                        k["xn_done"].of(pe, t)
                        for n in range(KD):
                            ins = nc.tensor.transpose(TQ[:, n // 4, (n % 4) * P:(n % 4 + 1) * P],
                                                      xn_next[:, n * P:(n + 1) * P], ident[:])
                        k["xn_turned"].mark(ins)
                    elif (h == 3 and 3 <= j < 11) or (h == 4 and j < 8):
                        i = j - 3 if h == 3 else j
                        if i == 0:
                            k["xnT_done"].of(pe, t)
                            k["qT_b"].of(pe, t if h == 4 else t - 1)
                            k["s_a"].of(pe, t if h == 4 else t - 1)
                        hc = i + 8 * (h == 4)
                        for n in range(KD):
                            ins = nc.tensor.matmul(TQ[:, i // 4, (i % 4) * P:(i % 4 + 1) * P],
                                                   wq[:, n, hc * QH:(hc + 1) * QH], xnT[:, n, :],
                                                   start=(n == 0), stop=(n == KD - 1))
                        if i % 4 == 3:
                            k["q_" + "abcd"[2 * (h == 4) + i // 4]].mark(ins)
                    elif at in ((3, 13), (4, 10)):
                        n = "ab"[h == 4]
                        k["qT_" + "bd"[h == 4]].of(pe, t)
                        if n == "b":
                            k["S_a"].of(pe, t)
                        for i in range(EH):
                            ins = nc.tensor.matmul(ZS[:, i // 4, (i % 4) * P:(i % 4 + 1) * P], qT[:, i, :],
                                                   keys[:, i + 8 * (h == 4), :], start=True, stop=True)
                        k[f"s_{n}"].mark(ins)

                def begin(t):
                    k["xr_done"].of(pe, t)
                    k["acc_taken"].of(pe, t - 1)
                    for b in range(2):
                        ins = nc.tensor.matmul(ACC[:, b, :], ident[:], xr[:, 512 * b:512 * b + 512],
                                               start=True, stop=False)
                    k["acc_begun"].mark(ins)

                def add_v(t, s_, last):
                    pe.wait_ge(diags, t * NSLOT + s_ + 1)
                    ring_in(pe, v_in, t, s_)
                    for b in range(2):
                        ins = nc.tensor.matmul(ACC[:, b, :], dg[:, s_ % DG, :], v_ring[:, s_ % VR, 512 * b:512 * b + 512],
                                               start=False, stop=last)
                    ins.then_inc(pv, 1)

                def retrieve(turn, t):
                    begin(t)
                    last = (NSLOT // 2 if turn == "samples" else NSLOT) - 1
                    for h, u, prep in blocks(turn, t):
                        for j in range(KS):
                            s_ = KS * (h - 1) + j
                            add_v(t, s_, s_ == last)
                            if prep:
                                prepare(*prep, j)

                for n in ("y_turned z_done yn_turned bot_done xn_turned q_a q_b q_c q_d s_a s_b acc_begun").split():
                    k[n].prime(pe)
                pe.sem_inc(pv, VR)
                pe.wait_ge(early, 64)
                pe.wait_ge(weights, 16 * 7)
                for h in range(EH):
                    for j in range(KS):
                        prepare(0, h, j)
                for j in range(KS):
                    prepare(1, 0, j)
                with pe.Fori(0, PT - 1) as t:
                    retrieve("steady", t)
                retrieve("eighth", PT - 1)
                retrieve("samples", PT)


def hybrid_layer(nc, a, s):
    sems = []

    def phase_ends():
        nc.clear_and_free_semaphores(sems)
        sems.clear()
        nc.all_engine_barrier()

    with ExitStack() as ctx:
        shared = Shared(Core(nc, ctx, sems))
        mix_tokens(nc, sems, a, s, shared)
        mix_samples(nc, sems, a, s, shared)
    phase_ends()
    run_ssm(nc, sems, a, s)
    phase_ends()
    retrieve_experts(nc, sems, a, s)


def host_layout(x):
    f = {n: np.ascontiguousarray(np.asarray(v)) for n, v in x.items()}
    rows = np.zeros((ROWS_PAD, D), np.float32)
    rows[:SEQ] = f["x_prompt"].reshape(SEQ, D)
    rows[SEQ:SEQ + NS_ROWS] = f["x_sample"].reshape(NS_ROWS, D)
    pos = np.zeros(ROWS_PAD, np.float32)
    pos[:SEQ] = np.arange(SEQ)
    pos[SEQ:SEQ + NS_ROWS] = np.tile(PAST + np.arange(DEC), NB)
    inv = np.float32(500000.0) ** (-np.arange(HALF, dtype=np.float32) * np.float32(2.0) / np.float32(ROT))
    ang = pos[:, None] * inv[None, :].astype(np.float32)
    rope = np.concatenate([np.cos(ang), np.sin(ang)], axis=1).astype(np.float32)
    q, key = np.arange(P)[:, None], np.arange(W)[None, :]
    off = np.float32(NEG / SCALE)
    mask = np.zeros((ROWS_PAD, 2 * W), np.float32)
    for t in range(PT):
        own = np.where(key <= q, 0, off)
        before = np.where((key > q) & (t > 0), 0, off)
        mask[t * P:(t + 1) * P] = np.concatenate([own, before] if t % 2 == 0 else [before, own], axis=1)
    i, key = (np.arange(P) % DEC)[:, None], np.arange(W + DEC)[None, :]
    mask_s = np.where((key > i) & (key <= W + i), 0, off).astype(np.float32)

    def pairs(v):
        v = v.reshape(PAIRS, 2, ST, *v.shape[2:])
        return np.ascontiguousarray(np.moveaxis(v, 0, 2).reshape(2 * ST, PAIRS, *v.shape[3:]))

    cols = np.concatenate([np.arange(AW).reshape(KV, REP, HD).transpose(1, 0, 2).ravel(), np.arange(AW, IN_W)])
    out = {
        "x": rows, "rope": rope, "mask": mask, "mask_s": mask_s,
        "ident": np.eye(P, dtype=np.float32), "fold": np.tile(np.eye(P // 2, P, dtype=np.float32), (2, 1)),
        "minus_half": np.full((P, 1), -0.5, np.float32),
        "w_in": f["w_in"][0][:, cols], "b_in": f["b_in"].reshape(1, IN_W)[:, cols],
        "g_mix": np.ascontiguousarray(f["norm_mix"].reshape(KD, P).T),
        "g_attn": np.ascontiguousarray(f["norm_attn_out"].reshape(AW // P, P).T),
        "g_ssm": np.ascontiguousarray(f["norm_ssm_out"].reshape(SW // P, P).T),
        "g_ffn": f["norm_ffn"].reshape(1, D), "g_final": f["norm_final"].reshape(1, D),
        "sink": f["attn_sinks"].reshape(1, HEADS),
        "sink_s": np.ascontiguousarray(np.broadcast_to(
            f["attn_sinks"].reshape(KV, 1, REP, 1), (KV, 4, REP, DEC)).reshape(KV, P).T),
        "w_out": f["w_out"][0], "w_glu": f["ssm_w_glu"][0], "b_glu": f["ssm_b_glu"].reshape(1, SW),
        "cache_k": f["cache_k"].reshape(NB, W, KV * HD), "cache_v": f["cache_v"].reshape(NB, W, KV * HD),
        "h0_re": pairs(np.moveaxis(f["state_ssm_re"][0], 0, 2)), "h0_im": pairs(np.moveaxis(f["state_ssm_im"][0], 0, 2)),
        "lam_re": pairs(f["ssm_lam_re"][0]), "lam_im": pairs(f["ssm_lam_im"][0]),
        "log_step": pairs(np.broadcast_to(f["ssm_log_step"][0][:, None], (GRP, ST))),
        "b_re": pairs(f["ssm_b_re"][0]), "b_im": pairs(f["ssm_b_im"][0]),
        "c_re": pairs(np.swapaxes(f["ssm_c_re"][0], 1, 2)), "c_im": pairs(np.swapaxes(f["ssm_c_im"][0], 1, 2)),
        "d_skip": f["ssm_d"].reshape(1, SW),
        "w_query": f["peer_w_query"][0],
        "keys": np.ascontiguousarray(np.transpose(f["peer_sub_keys"][0], (3, 0, 1, 2)).reshape(QH, EH * 2 * KEYS)),
        "place": np.arange(62, dtype=np.float32).reshape(1, 62),
        "u_table": f["peer_u"][0], "v_table": f["peer_v"][0],
    }
    return {n: np.ascontiguousarray(v) for n, v in out.items()}


OUTPUTS = {
    "y": (SEQ + NS_ROWS, D), "new_k_prompt": (W, KV * HD), "new_v_prompt": (W, KV * HD),
    "ssm_re_prompt": (P, PAIRS), "ssm_im_prompt": (P, PAIRS),
    "new_k_sample": (NB, W, KV * HD), "new_v_sample": (NB, W, KV * HD),
    "ssm_re_sample": (P, PAIRS, NB), "ssm_im_sample": (P, PAIRS, NB),
}
SCRATCH = {
    "u": (ROWS_PAD, SW), "x1": (ROWS_PAD, D), "pj": (NS_ROWS, U_COL), "x_s": (NS_ROWS, D),
    "attn_s": (P, 4 * HD), "y_ssm": (ROWS_PAD, SW),
}


def kernel(**inputs):
    import concourse.bacc as bacc
    from concourse.bass_utils import run_bass_kernel_spmd

    nc = bacc.Bacc("TRN2", target_bir_lowering=False, num_devices=1)
    laid = host_layout(inputs)
    a = {n: nc.dram_tensor(f"in_{n}", v.shape, mybir.dt.from_np(v.dtype), kind="ExternalInput").ap()
         for n, v in laid.items()}
    a |= {n: nc.dram_tensor(f"out_{n}", shape, F32, kind="ExternalOutput").ap() for n, shape in OUTPUTS.items()}
    s = {n: nc.dram_tensor(f"scratch_{n}", shape, F32, kind="Internal").ap() for n, shape in SCRATCH.items()}
    hybrid_layer(nc, a, s)
    r = run_bass_kernel_spmd(nc, [{f"in_{n}": v for n, v in laid.items()}], core_ids=[0]).results[0]
    got = {n: np.asarray(r[f"out_{n}"]) for n in OUTPUTS}

    def groups(v):
        v = np.moveaxis(v.reshape(2, ST, PAIRS, *v.shape[2:]), 2, 0)
        return v.reshape(GRP, ST, *v.shape[3:])

    def state(n, sample):
        v = groups(got[n])
        return np.moveaxis(v, 2, 0)[None] if sample else v[None, None]

    window = (1, 1, W, KV, HD)
    windows = (1, NB, W, KV, HD)
    return (got["y"][:SEQ].reshape(1, SEQ, D), got["y"][SEQ:].reshape(NB, DEC, D),
            got["new_k_prompt"].reshape(window), got["new_v_prompt"].reshape(window),
            state("ssm_re_prompt", False), state("ssm_im_prompt", False),
            got["new_k_sample"].reshape(windows), got["new_v_sample"].reshape(windows),
            state("ssm_re_sample", True), state("ssm_im_sample", True))
```

```python
from contextlib import ExitStack

import concourse.bass as bass
import numpy as np
from concourse import mybir

F32 = mybir.dt.float32
U32 = mybir.dt.uint32
ALU = mybir.AluOpType
ACT = mybir.ActivationFunctionType
AX = mybir.AxisListType

P = 128
D = 1024
KD = D // P
SEQ, NB, DEC = 1024, 8, 8
NS_ROWS = NB * DEC
PT = SEQ // P
ROWS_PAD = (PT + 1) * P
assert 2 * NS_ROWS == P
PAST = 2048
HEADS, KV, REP, HD = 8, 2, 4, 64
AW = HEADS * HD
W = 128
ROT = HD // 4
HALF = ROT // 2
SW = D - AW
GRP, CH, ST = 32, 16, 64
assert PT % 2 == 0
PAIRS = GRP // 2
L = 8
CK = SEQ // L
NC = CK + NB
IN_W = AW + 2 * KV * HD + SW
U_COL = AW + 2 * KV * HD
EH, KEYS, TOPK, QH = 8, 128, 16, 128
EPS = 1e-5
NEG = float(np.float32(-1e30))
SCALE = HD ** -0.5
TWO_PI = 2 * np.pi
PI_HI = 6.28125
PI_LO = TWO_PI - PI_HI
ROUND = 1.5 * 2.0 ** 23
PI_MAX = 3.1415925


class Count:

    def __init__(self, sem, step=1):
        self.sem, self.step = sem, step
        self.first = 2 if step == 1 else 1

    def prime(self, eng):
        assert self.step == 1
        eng.sem_inc(self.sem, 1)

    def mark(self, ins):
        ins.then_inc(self.sem, 16 if self.step >= 16 else 1)

    def of(self, eng, t):
        if isinstance(t, int) and t + self.first <= 0:
            return
        eng.wait_ge(self.sem, (t + self.first) * self.step)

    def held(self, eng, t):
        self.of(eng, t)
        eng.nop(nofuse=True)


class Steps:

    def __init__(self, sem):
        self.sem, self.n = sem, 0

    def mark(self, ins):
        self.n += 1
        ins.then_inc(self.sem, 1)
        return self.n

    def chain(self, eng, ins):
        self.mark(ins)
        eng.wait_ge(self.sem, self.n)


class Core:

    def __init__(self, nc, ctx, sems):
        self.nc, self.ctx, self.sems = nc, ctx, sems

    def sb(self, name, shape, dt=F32):
        return self.ctx.enter_context(self.nc.sbuf_tensor(name, shape, dt))

    def ps(self, name, shape):
        return self.ctx.enter_context(self.nc.psum_tensor(name, shape, F32))

    def sem(self, name):
        self.sems.append(self.nc.alloc_semaphore(name=name))
        return self.sems[-1]

    def count(self, name, step=1):
        return Count(self.sem(name), step)

    def steps(self, name):
        return Steps(self.sem(name))


def bcast(ap, n, dim):
    shape = list(ap.shape)
    return ap.unsqueeze(dim).to_broadcast(shape[:dim] + [n] + shape[dim:])


def mix_tokens(nc, sems, a, s, shared, par):
    with ExitStack() as ctx:
        c = Core(nc, ctx, sems)
        w_in = c.sb("w_in", [P, KD, IN_W])
        w_top, g_attn, ident, half = shared.w_top, shared.g_attn, shared.ident, shared.half
        b_in = c.sb("b_in", [P, IN_W])
        g_mix = c.sb("g_mix", [P, KD])
        sink = c.sb("sink", [P, HEADS])
        xt = c.sb("xt", [P, 2, D])
        xk = c.sb("xk", [P, 2, D])
        rope = c.sb("rope", [P, 2, 2 * HALF])
        mask = c.sb("mask", [P, 2, 2 * W])
        xs = c.sb("xs", [P, D])
        xT = c.sb("xT", [P, KD, P])
        pj = c.sb("pj", [P, 2, IN_W])
        rt = c.sb("rt", [P, 4, HEADS + KV, HALF])
        qT = c.sb("qT", [P, REP, P])
        kT = c.sb("kT", [P, 2, P])
        vb = c.sb("vb", [P, 2, P])
        sc = c.sb("sc", [P, HEADS, 2 * W])
        pr = c.sb("pr", [P, HEADS, 2 * W])
        ptr = c.sb("ptr", [P, 2 * HEADS, P])
        at = c.sb("at", [P, AW])
        at2 = c.sb("at2", [P, AW])
        aT = c.sb("aT", [P, AW // P, P])
        small = c.sb("small_a", [P, 8, HEADS])
        stat = c.sb("stat_a", [P, 8])
        mx, nm, sd, es, rs, den, rden = (small[:, i, :] for i in range(7))
        ssx, msx, rsx, ssa, msa, rsa = (stat[:, i:i + 1] for i in range(6))

        PJ = c.ps("PJ", [P, 3, 512])
        SC = c.ps("SC", [P, 4, 2, 2 * W])
        X = c.ps("X", [P, 512])
        QK = SC[:, 2:4, :, :].rearrange("p b c n -> p (b c n)")
        SCf = SC[:, :, :, :].rearrange("p b c n -> p (b c n)")

        weights, late = c.sem("weights_in"), c.sem("late_in")
        w_in_in = [c.sem(f"w_in_in{b}") for b in range(3)]
        kept = c.sem("kv_out")
        zeroed = c.sem("zeroed_a")
        x_in = [c.sem("x_in_even"), c.sem("x_in_odd")]
        tables_in, xk_in = c.count("tables_in", 32), c.count("xk_in", 16)
        u_out = c.count("u_out", 16)
        x1_out = c.count("x1_out", 16)
        names = ("ssx_done rsx_done xs_done x_turned xT_done projected pj_done roped v_kept qk_turned "
                 "qkT_done scored maxed shifted probs_done p_turned ptr_act ptr_dve weighed at_done "
                 "ssa_done rsa_done at2_done a_turned aT_done mixed x1_done msx_done msa_done rope_mul "
                 "den_done rden_done").split()
        k = {n: c.count(n) for n in names}
        N_W = 4
        W_COLS = ((0, 512), (512, U_COL), (U_COL, IN_W))

        def x_is_in(eng, t, p):
            eng.wait_ge(x_in[p], (t - p + 2) * 8)

        def steps(eng, step):
            step(0, 0, first=True)
            with eng.Fori(0, PT // 2 - 1) as i:
                step(i * 2 + 1, 1)
                step(i * 2 + 2, 0)
            step(PT - 1, 1, last=True)

        with nc.Block() as block:

            @block.sync
            def _(sp):
                def load_x(t, p):
                    k["xs_done"].held(sp, t - 2)
                    sp.dma_start(xt[:, p, :], a["x"][bass.ts(t, P), :]).then_inc(x_in[p], 16)

                def load_tables(t, p):
                    k["maxed"].held(sp, t - 2)
                    tables_in.held(sp, t - 1)
                    tables_in.mark(sp.dma_start(rope[:, p, :], a["rope"][bass.ts(t, P), :]))
                    tables_in.mark(sp.dma_start(mask[:, p, :], a["mask"][bass.ts(t, P), :]))

                def load_residual(t, p):
                    xk_in.held(sp, t - 1)
                    xk_in.mark(sp.dma_start(xk[:, p, :], a["x"][bass.ts(t, P), :]))

                def store_x1(t, p):
                    k["x1_done"].held(sp, t)
                    x1_out.mark(sp.dma_start(s["x1"][bass.ts(t, P), :], xk[:, p, :]))

                def store_u(t, p):
                    k["pj_done"].held(sp, t)
                    u_out.held(sp, t - 1)
                    u_out.mark(sp.dma_start(s["u"][bass.ts(t, P), :], pj[:, p, U_COL:]))

                def step(t, p, first=False, last=False):
                    if not last:
                        load_x(t + 2, p)
                    load_tables(t + 1, 1 - p)
                    if not first:
                        store_x1(t - 1, 1 - p)
                        x1_out.held(sp, t - 1)
                    if not last:
                        load_residual(t + 1, 1 - p)
                    store_u(t + 1, 1 - p)

                load_x(0, 0)
                load_x(1, 1)
                sp.dma_start(ident[:], a["ident"]).then_inc(weights, 16)
                sp.dma_start(g_mix[:], a["g_mix"]).then_inc(weights, 16)
                sp.dma_start(half[:], a["minus_half"]).then_inc(weights, 16)
                sp.dma_start(b_in[:], a["b_in"].to_broadcast([P, IN_W])).then_inc(weights, 16)
                w_rows = a["w_in"].rearrange("(k p) n -> p k n", p=P)
                for b in (2, 0, 1):
                    lo, hi = W_COLS[b]
                    sp.dma_start(w_in[:, :, lo:hi], w_rows[:, :, lo:hi]).then_inc(w_in_in[b], 16)
                    if b == 2:
                        par.load(sp, a)
                load_tables(0, 0)
                sp.dma_start(sink[:], a["sink"].to_broadcast([P, HEADS])).then_inc(late, 16)
                sp.dma_start(g_attn[:], a["g_attn"]).then_inc(late, 16)
                sp.dma_start(w_top[:], a["w_out"][0:AW, :].rearrange("(k p) n -> p k n", p=P)).then_inc(late, 16)
                load_residual(0, 0)
                store_u(0, 0)
                sp.dma_start(shared.kc[:], a["cache_k"].rearrange("b j n -> j b n")).then_inc(shared.caches_in, 16)
                sp.dma_start(shared.vc[:], a["cache_v"].rearrange("b j n -> j b n")).then_inc(shared.caches_in, 16)
                sp.dma_start(shared.mask_s[:], a["mask_s"]).then_inc(shared.caches_in, 16)
                sp.dma_start(shared.sink_s[:], a["sink_s"]).then_inc(shared.caches_in, 16)
                steps(sp, step)
                k["roped"].held(sp, PT)
                sp.dma_start(a["new_k_prompt"], pj[:, 1, AW:AW + KV * HD]).then_inc(kept, 16)
                sp.dma_start(a["new_v_prompt"], pj[:, 1, AW + KV * HD:U_COL]).then_inc(kept, 16)
                sp.dma_start(s["pj"], pj[0:NS_ROWS, 0, 0:U_COL]).then_inc(kept, 16)
                store_x1(PT - 1, 1)
                sp.wait_ge(kept, 16 * 3)
                x1_out.held(sp, PT - 1)
                u_out.held(sp, PT)

            @block.gpsimd
            def _(pool):
                for n in ("roped", "rsx_done", "msx_done", "v_kept", "rsa_done", "msa_done", "rope_mul"):
                    k[n].prime(pool)

                def rstd(t, src, ms, out, width, ready, mid, done):
                    ready.held(pool, t)
                    mid.mark(pool.tensor_scalar(ms, src, 1.0 / width, EPS, ALU.mult, ALU.add))
                    mid.held(pool, t)
                    done.mark(pool.tensor_tensor(out, ms, half[:], ALU.pow))

                def rstd_x(t):
                    k["xs_done"].held(pool, t - 1)
                    rstd(t, ssx, msx, rsx, D, k["ssx_done"], k["msx_done"], k["rsx_done"])

                def rstd_a(t):
                    rstd(t, ssa, msa, rsa, AW, k["ssa_done"], k["msa_done"], k["rsa_done"])

                def rotate(t, p):
                    heads = pj[:, p, 0:AW + KV * HD].rearrange("p (h d) -> p h d", d=HD)
                    x1, x2 = heads[:, :, 0:HALF], heads[:, :, HALF:ROT]
                    cos = bcast(rope[:, p, 0:HALF], HEADS + KV, 1)
                    sin = bcast(rope[:, p, HALF:], HEADS + KV, 1)
                    tables_in.held(pool, t)
                    k["pj_done"].held(pool, t)
                    k["roped"].held(pool, t - 1)
                    pool.tensor_tensor(rt[:, 0], x1, cos, ALU.mult)
                    pool.tensor_tensor(rt[:, 1], x2, sin, ALU.mult)
                    pool.tensor_tensor(rt[:, 2], x2, cos, ALU.mult)
                    k["rope_mul"].mark(pool.tensor_tensor(rt[:, 3], x1, sin, ALU.mult))
                    k["rope_mul"].held(pool, t)
                    pool.tensor_tensor(x1, rt[:, 0], rt[:, 1], ALU.subtract)
                    k["roped"].mark(pool.tensor_tensor(x2, rt[:, 2], rt[:, 3], ALU.add))

                def step(t, p, first=False, last=False):
                    if not first:
                        rstd_a(t - 1)
                    k["weighed"].held(pool, t - 1)
                    k["v_kept"].mark(pool.tensor_copy(vb[:, p, :], pj[:, p, AW + KV * HD:U_COL]))
                    if not last:
                        rstd_x(t + 2)
                    rotate(t + 1, 1 - p)

                pool.memset(kT[:, 1, :], 0.0).then_inc(zeroed, 1)
                pool.memset(vb[:, 1, :], 0.0).then_inc(zeroed, 1)
                pool.wait_ge(weights, 16 * N_W)
                rstd_x(0)
                rstd_x(1)
                rotate(0, 0)
                steps(pool, step)
                rstd_a(PT - 1)

            @block.scalar
            def _(act):
                for n in ("ssx_done", "qkT_done", "probs_done", "ptr_act"):
                    k[n].prime(act)

                def squares(t, p):
                    x_is_in(act, t, p)
                    k["x_turned"].of(act, t - 1)
                    k["msx_done"].of(act, t - 1)
                    k["ssx_done"].mark(nc.scalar.activation(xs[:], xt[:, p, :], ACT.Square, accum_out=ssx))

                def step(t, p, first=False, last=False):
                    k["qk_turned"].of(act, t)
                    k["scored"].of(act, t - 1)
                    if first:
                        act.wait_ge(zeroed, 2)
                    nc.scalar.activation(qT[:].rearrange("p r n -> p (r n)"), QK[:, 0:512], ACT.Copy)
                    k["qkT_done"].mark(nc.scalar.activation(kT[:, p, :], QK[:, 512:512 + P], ACT.Copy))
                    k["shifted"].of(act, t)
                    k["p_turned"].of(act, t - 1)
                    k["den_done"].of(act, t - 1)
                    for h in range(HEADS):
                        nc.scalar.activation(pr[:, h, :], sc[:, h, :], ACT.Exp, bias=nm[:, h:h + 1],
                                             accum_out=rs[:, h:h + 1])
                    k["probs_done"].mark(nc.scalar.activation(es, sd, ACT.Exp))
                    if not last:
                        squares(t + 2, p)
                    k["p_turned"].of(act, t)
                    k["weighed"].of(act, t - 1)
                    nc.scalar.activation(ptr[:, 0:4, :].rearrange("p a n -> p (a n)"), SCf[:, 0:512], ACT.Copy)
                    k["ptr_act"].mark(nc.scalar.activation(
                        ptr[:, 4:8, :].rearrange("p a n -> p (a n)"), SCf[:, 512:1024], ACT.Copy))

                squares(0, 0)
                squares(1, 1)
                par.on_scalar(nc, act)
                steps(act, step)

            @block.vector
            def _(dve):
                for n in ("xs_done", "xT_done", "pj_done", "maxed", "shifted", "ptr_dve", "at_done", "ssa_done",
                          "at2_done", "aT_done", "x1_done", "den_done", "rden_done"):
                    k[n].prime(dve)

                def normalise(t, p):
                    k["rsx_done"].of(dve, t)
                    k["ssx_done"].of(dve, t)
                    x_is_in(dve, t, p)
                    k["xs_done"].mark(nc.vector.tensor_scalar(xs[:], xt[:, p, :], rsx, None, ALU.mult))

                def take_columns(t):
                    k["x_turned"].of(dve, t)
                    k["projected"].of(dve, t - 1)
                    for b in range(2):
                        ins = nc.vector.tensor_tensor(
                            xT[:, 4 * b:4 * b + 4, :], PJ[:, b, :].rearrange("p (k n) -> p k n", n=P),
                            bcast(g_mix[:, 4 * b:4 * b + 4], P, 2), ALU.mult)
                    k["xT_done"].mark(ins)

                def take_projection(t, p):
                    k["projected"].of(dve, t)
                    u_out.of(dve, t - 2)
                    k["v_kept"].of(dve, t - 2)
                    for b, (lo, hi) in enumerate(W_COLS):
                        ins = nc.vector.tensor_tensor(pj[:, p, lo:hi], PJ[:, b, 0:hi - lo], b_in[:, lo:hi], ALU.add)
                    k["pj_done"].mark(ins)

                def divide(t):
                    k["weighed"].of(dve, t)
                    k["rden_done"].of(dve, t)
                    k["at2_done"].of(dve, t - 1)
                    k["at_done"].mark(nc.vector.tensor_tensor(
                        at[:].rearrange("p (h d) -> p h d", d=HD), X[:].rearrange("p (h d) -> p h d", d=HD),
                        bcast(rden, HD, 2), ALU.mult))
                    k["at_done"].of(dve, t)
                    k["a_turned"].of(dve, t - 1)
                    k["ssa_done"].mark(nc.vector.tensor_tensor_reduce(at2[:], at[:], at[:], 1.0, 0.0,
                                                                      ALU.mult, ALU.add, ssa))

                def normalise_out(t):
                    k["ssa_done"].of(dve, t)
                    k["rsa_done"].of(dve, t)
                    k["at2_done"].mark(nc.vector.tensor_scalar(at2[:], at[:], rsa, None, ALU.mult))

                def take_out_columns(t):
                    k["a_turned"].of(dve, t)
                    k["mixed"].of(dve, t - 1)
                    k["aT_done"].mark(nc.vector.tensor_tensor(
                        aT[:], X[:].rearrange("p (k n) -> p k n", n=P), bcast(g_attn[:], P, 2), ALU.mult))

                def add_residual(t, p):
                    k["mixed"].of(dve, t)
                    xk_in.of(dve, t)
                    for b in range(2):
                        half_row = xk[:, p, 512 * b:512 * b + 512]
                        ins = nc.vector.tensor_tensor(half_row, PJ[:, b, :], half_row, ALU.add)
                    k["x1_done"].mark(ins)

                def step(t, p, first=False, last=False):
                    if not first:
                        divide(t - 1)
                    normalise(t + 1, 1 - p)
                    if not first:
                        normalise_out(t - 1)
                    take_columns(t + 1)
                    if not first:
                        take_out_columns(t - 1)
                    k["scored"].of(dve, t)
                    k["probs_done"].of(dve, t - 1)
                    tables_in.held(dve, t)
                    for h in range(HEADS):
                        ins = nc.vector.tensor_tensor_reduce(
                            sc[:, h, :], SC[:, h // 2, h % 2, :], mask[:, p, :], SCALE, sink[:, h:h + 1],
                            ALU.add, ALU.max, mx[:, h:h + 1])
                    k["maxed"].mark(ins)
                    k["maxed"].of(dve, t)
                    nc.vector.tensor_scalar(nm, mx, -1.0, None, ALU.mult)
                    k["shifted"].mark(nc.vector.tensor_tensor(sd, sink[:], mx, ALU.subtract))
                    if not first:
                        add_residual(t - 1, 1 - p)
                    k["probs_done"].of(dve, t)
                    k["at_done"].of(dve, t - 1)
                    k["den_done"].mark(nc.vector.tensor_tensor(den, rs, es, ALU.add))
                    k["den_done"].of(dve, t)
                    k["rden_done"].mark(nc.vector.reciprocal(rden, den))
                    if first:
                        par.output_matrices(nc, dve)
                    if last:
                        par.input_matrices(nc, dve)
                    take_projection(t + 1, 1 - p)
                    k["p_turned"].of(dve, t)
                    k["weighed"].of(dve, t - 1)
                    nc.vector.tensor_copy(ptr[:, 8:12, :].rearrange("p a n -> p (a n)"), SCf[:, 1024:1536])
                    k["ptr_dve"].mark(nc.vector.tensor_copy(
                        ptr[:, 12:16, :].rearrange("p a n -> p (a n)"), SCf[:, 1536:2048]))

                dve.wait_ge(weights, 16 * N_W)
                normalise(0, 0)
                take_columns(0)
                par.on_vector(nc, dve)
                take_projection(0, 0)
                dve.wait_ge(late, 16 * 3)
                steps(dve, step)
                divide(PT - 1)
                normalise_out(PT - 1)
                take_out_columns(PT - 1)
                add_residual(PT - 1, 1)

            @block.tensor
            def _(pe):
                for n in ("x_turned", "projected", "qk_turned", "scored", "p_turned", "weighed", "a_turned", "mixed"):
                    k[n].prime(pe)

                def turn_x(t):
                    k["xs_done"].of(pe, t)
                    k["pj_done"].of(pe, t - 1)
                    for j in range(KD):
                        ins = nc.tensor.transpose(PJ[:, j // 4, (j % 4) * P:(j % 4 + 1) * P],
                                                  xs[:, j * P:(j + 1) * P], ident[:])
                    k["x_turned"].mark(ins)

                def project(t):
                    k["xT_done"].of(pe, t)
                    for b in (2, 0, 1):
                        lo, hi = W_COLS[b]
                        if isinstance(t, int) and t == 0:
                            pe.wait_ge(w_in_in[b], 16)
                        if b == 0:
                            k["x1_done"].of(pe, t - 2)
                        for j in range(KD):
                            ins = nc.tensor.matmul(PJ[:, b, 0:hi - lo], xT[:, j, :], w_in[:, j, lo:hi],
                                                   start=(j == 0), stop=(j == KD - 1))
                    k["projected"].mark(ins)

                def turn_out(t):
                    k["at2_done"].of(pe, t)
                    for j in range(AW // P):
                        ins = nc.tensor.transpose(X[:, j * P:(j + 1) * P], at2[:, j * P:(j + 1) * P], ident[:])
                    k["a_turned"].mark(ins)

                def mix(t):
                    k["aT_done"].of(pe, t)
                    for b in range(2):
                        for j in range(AW // P):
                            ins = nc.tensor.matmul(PJ[:, b, :], aT[:, j, :], w_top[:, j, 512 * b:512 * b + 512],
                                                   start=(j == 0), stop=(j == AW // P - 1))
                    k["mixed"].mark(ins)

                def step(t, p, first=False, last=False):
                    k["roped"].of(pe, t)
                    k["ptr_act"].of(pe, t - 1)
                    k["ptr_dve"].of(pe, t - 1)
                    for r in range(REP):
                        nc.tensor.transpose(QK[:, r * P:(r + 1) * P], pj[:, p, r * P:(r + 1) * P], ident[:])
                    k["qk_turned"].mark(nc.tensor.transpose(
                        QK[:, 512:512 + P], pj[:, p, AW:AW + KV * HD], ident[:]))
                    turn_x(t + 1)
                    if not first:
                        turn_out(t - 1)
                    k["qkT_done"].of(pe, t)
                    for h in range(HEADS):
                        g, r = divmod(h, REP)
                        ins = nc.tensor.matmul(SC[:, h // 2, h % 2, :], qT[g * HD:(g + 1) * HD, r, :],
                                               kT[g * HD:(g + 1) * HD, :, :].rearrange("p a n -> p (a n)"),
                                               start=True, stop=True)
                    k["scored"].mark(ins)
                    if not first:
                        k["xT_done"].of(pe, t + 1)
                        mix(t - 1)
                    project(t + 1)
                    k["probs_done"].of(pe, t)
                    k["maxed"].of(pe, t)
                    for h in range(HEADS):
                        for w in range(2):
                            n = 2 * h + w
                            ins = nc.tensor.transpose(SCf[:, n * P:(n + 1) * P], pr[:, h, w * W:(w + 1) * W], ident[:])
                    k["p_turned"].mark(ins)
                    k["ptr_act"].of(pe, t)
                    k["ptr_dve"].of(pe, t)
                    k["v_kept"].of(pe, t)
                    k["aT_done"].of(pe, t - 1)
                    for h in range(HEADS):
                        g = h // REP
                        for w in range(2):
                            ins = nc.tensor.matmul(X[:, h * HD:(h + 1) * HD], ptr[:, 2 * h + w, :],
                                                   vb[:, w, g * HD:(g + 1) * HD], start=(w == 0), stop=(w == 1))
                    k["weighed"].mark(ins)

                pe.wait_ge(weights, 16 * N_W)
                turn_x(0)
                project(0)
                pe.wait_ge(late, 16 * 3)
                steps(pe, step)
                turn_out(PT - 1)
                k["pj_done"].of(pe, PT)
                mix(PT - 1)


class Once:

    def __init__(self, core, phase):
        self.core, self.phase, self.sems = core, phase, {}

    def __getitem__(self, name):
        if name not in self.sems:
            self.sems[name] = self.core.sem(f"{self.phase}_{name}")
        return self.sems[name]


def mix_samples(nc, sems, a, s, shared):
    with ExitStack() as ctx:
        c = Core(nc, ctx, sems)
        w_top, g_attn, ident, half = shared.w_top, shared.g_attn, shared.ident, shared.half
        R, NK = NS_ROWS, W + DEC
        qkv = c.sb("qkv_s", [R, U_COL])
        kc, vc, mask, sink = shared.kc, shared.vc, shared.mask_s, shared.sink_s
        xr = c.sb("xr_s", [R, D])
        vn = c.sb("vn", [DEC, NB, P])
        qT = c.sb("qT_s", [P, NB, REP, DEC])
        kT = c.sb("kT_s", [P, NB, NK])
        sc = c.sb("sc_s", [P, 4, NK])
        pr = c.sb("pr_s", [P, 4, NK])
        ptb = c.sb("ptb", [P, 4, P])
        ptn = c.sb("ptn", [DEC, 4, P])
        small = c.sb("small_s", [P, 8, 4])
        stat = c.sb("stat_s", [P, 4])
        oS = c.sb("o_s", [P, 4, HD])
        at = c.sb("at_s", [R, AW])
        at2 = c.sb("at2_s", [R, AW])
        aT = c.sb("aT_s", [P, AW // P, R])
        mx, nm, sd, es, rs, den, rden = (small[:, i, :] for i in range(7))
        ss, ms, rstd = (stat[0:R, i:i + 1] for i in range(3))
        TR = c.ps("TR", [P, 512])
        KB = c.ps("KB", [P, NB, P])
        SS = c.ps("SS", [P, KV, 512])
        PO = c.ps("PO", [P, 2, 512])
        ev = Once(c, "s")
        xr_in = c.sem("xr_in_s")
        vn_in, qkv_in, back_in, stores = c.sem("vn_in"), c.sem("qkv_in"), c.sem("back_in"), c.sem("stores_s")

        def back(eng, hf):
            eng.wait_ge(ev["o_out"], 16)
            for b in range(4 * hf, 4 * hf + 4):
                for g in range(KV):
                    src = s["attn_s"][32 * (b % 4):32 * (b % 4) + 32, (2 * g + hf) * HD:(2 * g + hf + 1) * HD]
                    eng.dma_start(at[b * DEC:(b + 1) * DEC, g * 256:(g + 1) * 256].rearrange("i (r d) -> i r d", d=HD),
                                  src.rearrange("(r i) d -> i r d", i=DEC)).then_inc(back_in, 16)

        with nc.Block() as block:

            @block.sync
            def _(sp):
                sp.dma_start(qkv[:], s["pj"]).then_inc(qkv_in, 16)
                sp.dma_start(vn[:], s["pj"][:, AW + KV * HD:U_COL].rearrange("(b i) n -> i b n", i=DEC)).then_inc(vn_in, 16)
                sp.dma_start(xr[:], a["x"][SEQ:SEQ + R, :]).then_inc(xr_in, 16)
                for n, lo in (("k", AW), ("v", AW + KV * HD)):
                    out = a[f"new_{n}_sample"]
                    sp.dma_start(out[:, 0:W - DEC, :], a[f"cache_{n}"][:, DEC:W, :]).then_inc(stores, 16)
                    sp.dma_start(out[:, W - DEC:W, :], s["pj"][:, lo:lo + KV * HD].rearrange("(b i) n -> b i n", i=DEC)).then_inc(stores, 16)
                sp.wait_ge(ev["o_done"], 1)
                sp.dma_start(s["attn_s"], oS[:].rearrange("p n d -> p (n d)")).then_inc(ev["o_out"], 16)
                back(sp, 0)
                sp.wait_ge(ev["x1"], 1)
                for lo in (SEQ, SEQ + R):
                    sp.dma_start(s["x1"][lo:lo + R, :], xr[:]).then_inc(stores, 16)
                sp.wait_ge(stores, 16 * 6)

            @block.gpsimd
            def _(pool):
                pool.wait_ge(ev["ss"], 1)
                pool.tensor_scalar(ms, ss, 1.0 / AW, EPS, ALU.mult, ALU.add).then_inc(ev["ms"], 1)
                pool.wait_ge(ev["ms"], 1)
                pool.tensor_tensor(rstd, ms, half[0:R, :], ALU.pow).then_inc(ev["rstd"], 1)

            @block.scalar
            def _(act):
                act.wait_ge(ev["q_turned"], 1)
                nc.scalar.activation(qT[:], TR[:, 0:REP * R].rearrange("p (r b i) -> p b r i", r=REP, i=DEC), ACT.Copy)
                nc.scalar.activation(kT[:, :, W:NK], TR[:, REP * R:5 * R].rearrange("p (b i) -> p b i", i=DEC),
                                     ACT.Copy).then_inc(ev["qT"], 1)
                act.wait_ge(ev["shifted"], 1)
                for n in range(4):
                    nc.scalar.activation(pr[:, n, :], sc[:, n, :], ACT.Exp, bias=nm[:, n:n + 1], accum_out=rs[:, n:n + 1])
                nc.scalar.activation(es, sd, ACT.Exp).then_inc(ev["probs"], 1)
                act.wait_ge(ev["p_turned"], 1)
                nc.scalar.activation(ptb[:].rearrange("p n m -> p (n m)"), KB[:, 0:4, :].rearrange("p n m -> p (n m)"),
                                     ACT.Copy).then_inc(ev["ptb"], 1)
                nc.scalar.activation(ptn[:].rearrange("p n m -> p (n m)"),
                                     KB[0:DEC, 4:8, :].rearrange("p n m -> p (n m)"), ACT.Copy).then_inc(ev["ptn"], 1)
                back(act, 1)

            @block.vector
            def _(dve):
                dve.wait_ge(ev["k_turned"], 1)
                nc.vector.tensor_copy(kT[:, :, 0:W], KB[:]).then_inc(ev["kT"], 1)
                dve.wait_ge(shared.caches_in, 16 * 4)
                dve.wait_ge(ev["scored"], 1)
                for g in range(KV):
                    for hf in range(2):
                        n = 2 * g + hf
                        ins = nc.vector.tensor_tensor_reduce(
                            sc[:, n, :], SS[:, g, hf * NK:(hf + 1) * NK], mask[:], SCALE, sink[:, g:g + 1],
                            ALU.add, ALU.max, mx[:, n:n + 1])
                ins.then_inc(ev["maxed"], 1)
                dve.wait_ge(ev["maxed"], 1)
                nc.vector.tensor_scalar(nm, mx, -1.0, None, ALU.mult)
                nc.vector.tensor_tensor(sd.rearrange("p (g f) -> p g f", g=KV), bcast(sink[:], 2, 2),
                                        mx.rearrange("p (g f) -> p g f", g=KV), ALU.subtract).then_inc(ev["shifted"], 1)
                dve.wait_ge(ev["probs"], 1)
                nc.vector.tensor_tensor(den, rs, es, ALU.add).then_inc(ev["den"], 1)
                dve.wait_ge(ev["den"], 1)
                nc.vector.reciprocal(rden, den).then_inc(ev["rden"], 1)
                dve.wait_ge(ev["rden"], 1)
                dve.wait_ge(ev["weighed"], 1)
                nc.vector.tensor_tensor(oS[:], PO[:, 0, 0:4 * HD].rearrange("p (n d) -> p n d", d=HD),
                                        bcast(rden, HD, 2), ALU.mult).then_inc(ev["o_done"], 1)
                dve.wait_ge(xr_in, 16)
                dve.wait_ge(back_in, 16 * NB * KV)
                nc.vector.tensor_tensor_reduce(at2[:], at[:], at[:], 1.0, 0.0, ALU.mult, ALU.add, ss).then_inc(ev["ss"], 1)
                dve.wait_ge(ev["ss"], 1)
                dve.wait_ge(ev["rstd"], 1)
                nc.vector.tensor_scalar(at2[:], at[:], rstd, None, ALU.mult).then_inc(ev["at2"], 1)
                dve.wait_ge(ev["a_turned"], 1)
                nc.vector.tensor_tensor(aT[:], TR[:, 0:4 * R].rearrange("p (k n) -> p k n", n=R), bcast(g_attn[:], R, 2),
                                        ALU.mult).then_inc(ev["aT"], 1)
                dve.wait_ge(ev["mixed"], 1)
                for b in range(2):
                    row = xr[:, 512 * b:512 * b + 512]
                    ins = nc.vector.tensor_tensor(row, PO[0:R, b, :], row, ALU.add)
                ins.then_inc(ev["x1"], 1)

            @block.tensor
            def _(pe):
                pe.wait_ge(qkv_in, 16)
                for r in range(5):
                    ins = nc.tensor.transpose(TR[:, r * R:(r + 1) * R], qkv[:, r * P:(r + 1) * P], ident[0:R, 0:R])
                ins.then_inc(ev["q_turned"], 1)
                pe.wait_ge(shared.caches_in, 16 * 4)
                for b in range(NB):
                    ins = nc.tensor.transpose(KB[:, b, :], kc[:, b, :], ident[:])
                ins.then_inc(ev["k_turned"], 1)
                pe.wait_ge(ev["qT"], 1)
                pe.wait_ge(ev["kT"], 1)
                for g in range(KV):
                    for b in range(NB):
                        row = 32 * (b % 4)
                        ins = nc.tensor.matmul(SS[row:row + 32, g, (b // 4) * NK:(b // 4 + 1) * NK],
                                               qT[g * HD:(g + 1) * HD, b].rearrange("p r i -> p (r i)"),
                                               kT[g * HD:(g + 1) * HD, b, :], start=True, stop=True)
                ins.then_inc(ev["scored"], 1)
                pe.wait_ge(ev["probs"], 1)
                for n in range(4):
                    nc.tensor.transpose(KB[:, n, :], pr[:, n, 0:W], ident[:])
                for n in range(4):
                    ins = nc.tensor.transpose(KB[0:DEC, 4 + n, :], pr[:, n, W:NK], ident[:])
                ins.then_inc(ev["p_turned"], 1)
                pe.wait_ge(ev["ptb"], 1)
                pe.wait_ge(ev["ptn"], 1)
                pe.wait_ge(vn_in, 16)
                for b in range(NB):
                    for g in range(KV):
                        n, row = 2 * g + b // 4, 32 * (b % 4)
                        out = PO[row:row + 32, 0, n * HD:(n + 1) * HD]
                        nc.tensor.matmul(out, ptb[:, n, row:row + 32], vc[:, b, g * HD:(g + 1) * HD], start=True, stop=False)
                        ins = nc.tensor.matmul(out, ptn[:, n, row:row + 32], vn[:, b, g * HD:(g + 1) * HD],
                                               start=False, stop=True)
                ins.then_inc(ev["weighed"], 1)
                pe.wait_ge(ev["at2"], 1)
                for j in range(AW // P):
                    ins = nc.tensor.transpose(TR[:, j * R:(j + 1) * R], at2[:, j * P:(j + 1) * P], ident[0:R, 0:R])
                ins.then_inc(ev["a_turned"], 1)
                pe.wait_ge(ev["aT"], 1)
                for b in range(2):
                    for j in range(AW // P):
                        ins = nc.tensor.matmul(PO[0:R, b, :], aT[:, j, :], w_top[:, j, 512 * b:512 * b + 512],
                                               start=(j == 0), stop=(j == AW // P - 1))
                ins.then_inc(ev["mixed"], 1)


def mul(eng, st, dst, x, y, t1, t2, part):
    if part == 0:
        eng.tensor_tensor(t1, x[0], y[0], ALU.mult)
        st.chain(eng, eng.tensor_tensor(t2, x[1], y[1], ALU.mult))
        st.chain(eng, eng.tensor_tensor(dst, t1, t2, ALU.subtract))
        return
    eng.tensor_tensor(t1, x[0], y[1], ALU.mult)
    st.chain(eng, eng.tensor_tensor(t2, x[1], y[0], ALU.mult))
    st.chain(eng, eng.tensor_tensor(dst, t1, t2, ALU.add))


def reduce_angle(eng, st, r, k, x, quarter):
    st.chain(eng, eng.tensor_scalar(k, x, 1.0 / TWO_PI, 0.25 if quarter else 0.0, ALU.mult, ALU.add))
    st.chain(eng, eng.tensor_scalar(k, k, ROUND, None, ALU.add))
    st.chain(eng, eng.tensor_scalar(k, k, ROUND, None, ALU.subtract))
    st.chain(eng, eng.scalar_tensor_tensor(r, k, -PI_HI, x, ALU.mult, ALU.add))
    st.chain(eng, eng.scalar_tensor_tensor(r, k, -PI_LO, r, ALU.mult, ALU.add))
    if quarter:
        st.chain(eng, eng.tensor_scalar(r, r, float(np.float32(np.pi / 2)), None, ALU.add))
    st.chain(eng, eng.tensor_scalar(r, r, PI_MAX, -PI_MAX, ALU.min, ALU.max))


class SsmParameters:

    def __init__(self, c):
        self.WBt = [c.sb(f"WBt_{x}", [P, PAIRS, P]) for x in "ri"]
        self.WC = [c.sb(f"WC_{x}", [P, PAIRS, (L + 1) * CH]) for x in "ri"]
        self.T1, self.T2 = (c.sb(f"T{i}", [P, PAIRS * (L + 1) * CH]) for i in (1, 2))
        self.lam = [c.sb(f"lam_{x}", [P, PAIRS]) for x in "ri"]
        self.lstep = c.sb("lstep", [P, PAIRS])
        self.Bm = [c.sb(f"Bm_{x}", [P, PAIRS, CH]) for x in "ri"]
        self.Cm = [c.sb(f"Cm_{x}", [P, PAIRS, CH]) for x in "ri"]
        self.BB = [c.sb(f"BB_{x}", [P, PAIRS, CH]) for x in "ri"]
        self.PW = [c.sb(f"PW_{x}", [P, L + 1, PAIRS]) for x in "ri"]
        self.PR = [c.sb(f"PR_{x}", [P, L, PAIRS]) for x in "ri"]
        self.h0 = [c.sb(f"h0_{x}", [P, PAIRS, NB]) for x in "ri"]
        self.v = {n: c.sb(f"v_{n}", [P, PAIRS]) for n in
                  "dt lrdt th mag mag8 k r1 r2 k2 sin cos den t t2 m1 zr zi ph k3 q1 q2 k4 us uc g1 g2".split()}
        self.loads = c.sem("loads_p")
        self.ev = Once(c, "p")
        self.dv, self.ac = c.steps("dve_steps_p"), c.steps("act_steps_p")

    def load(self, sp, a):
        sp.dma_start(self.lstep[:], a["log_step"]).then_inc(self.loads, 16)
        for x, part in enumerate(("re", "im")):
            sp.dma_start(self.lam[x][:], a[f"lam_{part}"]).then_inc(self.loads, 16)
            sp.dma_start(self.Bm[x][:], a[f"b_{part}"]).then_inc(self.loads, 16)
            sp.dma_start(self.Cm[x][:], a[f"c_{part}"]).then_inc(self.loads, 16)
            sp.dma_start(self.h0[x][:], a[f"h0_{part}"]).then_inc(self.loads, 16)

    def on_scalar(self, nc, act):
        ev, v, lstep = self.ev, self.v, self.lstep

        def f(dst, src, func, **kw):
            self.ac.chain(act, nc.scalar.activation(dst, src, func, **kw))

        act.wait_ge(self.loads, 16 * 9)
        f(v["dt"][:], lstep[:], ACT.Exp)
        act.sem_inc(ev["dt"], 1)
        act.wait_ge(ev["angle"], 1)
        nc.scalar.activation(v["mag8"][:], v["lrdt"][:], ACT.Exp, scale=float(L))
        nc.scalar.activation(v["mag"][:], v["lrdt"][:], ACT.Exp).then_inc(ev["mag"], 1)
        nc.scalar.activation(v["sin"][:], v["r1"][:], ACT.Sin)
        nc.scalar.activation(v["cos"][:], v["r2"][:], ACT.Sin).then_inc(ev["sincos"], 1)
        act.wait_ge(ev["phase"], 1)
        nc.scalar.activation(v["us"][:], v["q1"][:], ACT.Sin)
        nc.scalar.activation(v["uc"][:], v["q2"][:], ACT.Sin).then_inc(ev["unit"], 1)

    def on_vector(self, nc, dve):
        ev, v, lam, dv = self.ev, self.v, self.lam, self.dv
        T1, T2, Bm, BB, PW, PR = self.T1, self.T2, self.Bm, self.BB, self.PW, self.PR
        tt, ts = nc.vector.tensor_tensor, nc.vector.tensor_scalar

        def link(ins):
            dv.chain(dve, ins)

        def tell(eng, name):
            eng.sem_inc(ev[name], 1)

        dve.wait_ge(self.loads, 16 * 9)
        dve.wait_ge(ev["dt"], 1)
        lr, li = lam[0][:], lam[1][:]
        tt(v["lrdt"][:], lr, v["dt"][:], ALU.mult)
        link(tt(v["th"][:], li, v["dt"][:], ALU.mult))
        reduce_angle(dve, dv, v["r1"][:], v["k"][:], v["th"][:], False)
        reduce_angle(dve, dv, v["r2"][:], v["k2"][:], v["th"][:], True)
        link(ts(v["ph"][:], v["r1"][:], float(L), None, ALU.mult))
        tell(dve, "angle")
        reduce_angle(dve, dv, v["q1"][:], v["k3"][:], v["ph"][:], False)
        reduce_angle(dve, dv, v["q2"][:], v["k4"][:], v["ph"][:], True)
        tell(dve, "phase")
        dve.wait_ge(ev["mag"], 1)
        dve.wait_ge(ev["sincos"], 1)
        nc.vector.memset(PW[0][:, 0, :], 1.0)
        nc.vector.memset(PW[1][:, 0, :], 0.0)
        tt(PW[0][:, 1, :], v["mag"][:], v["cos"][:], ALU.mult)
        link(tt(PW[1][:, 1, :], v["mag"][:], v["sin"][:], ALU.mult))
        ab = [PW[i][:, 1, :] for i in range(2)]
        for n in (1, 2, 4):
            x = [bcast(PW[i][:, n, :], n, 1) for i in range(2)]
            y = [PW[i][:, 1:n + 1, :] for i in range(2)]
            t1, t2 = (t[:, 0:n * PAIRS].rearrange("p (n q) -> p n q", n=n) for t in (T1, T2))
            mul(nc.vector, dv, PW[0][:, n + 1:2 * n + 1, :], x, y, t1, t2, 0)
            mul(nc.vector, dv, PW[1][:, n + 1:2 * n + 1, :], x, y, t1, t2, 1)
        for i in range(2):
            for j in range(L):
                ins = nc.vector.tensor_copy(PR[i][:, j, :], PW[i][:, L - 1 - j, :])
        link(ins)
        tt(v["t"][:], lr, lr, ALU.mult)
        link(tt(v["t2"][:], li, li, ALU.mult))
        link(tt(v["den"][:], v["t"][:], v["t2"][:], ALU.add))
        link(nc.vector.reciprocal(v["den"][:], v["den"][:]))
        link(ts(v["m1"][:], ab[0], 1.0, None, ALU.subtract))
        tt(v["t"][:], v["m1"][:], lr, ALU.mult)
        link(tt(v["t2"][:], ab[1], li, ALU.mult))
        link(tt(v["zr"][:], v["t"][:], v["t2"][:], ALU.add))
        tt(v["t"][:], ab[1], lr, ALU.mult)
        link(tt(v["t2"][:], v["m1"][:], li, ALU.mult))
        link(tt(v["zi"][:], v["t"][:], v["t2"][:], ALU.subtract))
        tt(v["zr"][:], v["zr"][:], v["den"][:], ALU.mult)
        link(tt(v["zi"][:], v["zi"][:], v["den"][:], ALU.mult))
        z = [bcast(v["zr"][:], CH, 2), bcast(v["zi"][:], CH, 2)]
        t1, t2 = (t[:, 0:PAIRS * CH].rearrange("p (q n) -> p q n", n=CH) for t in (T1, T2))
        mul(nc.vector, dv, BB[0][:], z, [m[:] for m in Bm], t1, t2, 0)
        mul(nc.vector, dv, BB[1][:], z, [m[:] for m in Bm], t1, t2, 1)

    def input_matrices(self, nc, dve):
        WBt, T1, T2, BB, PR, dv = self.WBt, self.T1, self.T2, self.BB, self.PR, self.dv

        x = [bcast(PR[i][:].rearrange("p t q -> p q t"), CH, 3) for i in range(2)]
        y = [bcast(BB[i][:], L, 2) for i in range(2)]
        t1, t2 = (t[:, 0:PAIRS * P].rearrange("p (q t n) -> p q t n", t=L, n=CH) for t in (T1, T2))
        for i in range(2):
            mul(nc.vector, dv, WBt[i][:].rearrange("p q (t n) -> p q t n", n=CH), x, y, t1, t2, i)

    def output_matrices(self, nc, dve):
        WC, T1, T2, Cm, PW, ev, dv = self.WC, self.T1, self.T2, self.Cm, self.PW, self.ev, self.dv

        def link(ins):
            dv.chain(dve, ins)

        x = [bcast(PW[i][:].rearrange("p t q -> p q t"), CH, 3) for i in range(2)]
        y = [bcast(Cm[i][:], L + 1, 2) for i in range(2)]
        t1, t2 = (t[:].rearrange("p (q t n) -> p q t n", t=L + 1, n=CH) for t in (T1, T2))
        mul(nc.vector, dv, WC[0][:].rearrange("p q (t n) -> p q t n", n=CH), x, y, t1, t2, 0)
        nc.vector.tensor_tensor(t1, x[0], y[1], ALU.mult)
        link(nc.vector.tensor_tensor(t2, x[1], y[0], ALU.mult))
        nc.vector.scalar_tensor_tensor(WC[1][:].rearrange("p q m -> p (q m)"), T1[:], -1.0, T2[:],
                                       ALU.mult, ALU.subtract).then_inc(ev["wc"], 1)
        dve.wait_ge(ev["wc"], 1)


class Shared:

    def __init__(self, c):
        self.kc = c.sb("kc", [P, NB, P])
        self.vc = c.sb("vc", [P, NB, P])
        self.mask_s = c.sb("mask_s", [P, W + DEC])
        self.sink_s = c.sb("sink_s", [P, KV])
        self.caches_in = c.sem("caches_in")
        self.w_top = c.sb("w_top", [P, AW // P, D])
        self.g_attn = c.sb("g_attn", [P, AW // P])
        self.ident = c.sb("ident", [P, P])
        self.half = c.sb("minus_half", [P, 1])


def run_ssm(nc, sems, a, s, par):
    with ExitStack() as ctx:
        c = Core(nc, ctx, sems)
        ident = c.sb("ident_c", [P, P])
        U2 = c.sb("U2", [P, L * SW])
        U2g = c.sb("U2g", [P, GRP * L * CH])
        Us = c.sb("Us", [NB, GRP, L, CH])
        XT = c.sb("XT", [P, GRP, NC])
        K16 = U2[0:CH, :].rearrange("p (g m) -> p g m", g=GRP)
        TOE = U2g[:].rearrange("p (g m) -> p g m", g=GRP)
        WBt, WC, BB, PW, h0, v, T1, T2 = par.WBt, par.WC, par.BB, par.PW, par.h0, par.v, par.T1, par.T2
        WB = [c.sb(f"WB_{x}", [P, PAIRS, P]) for x in "ri"]
        BU = [c.sb(f"BU_{x}", [P, PAIRS, NC]) for x in "ri"]
        G = [c.sb(f"G_{x}", [P, PAIRS, CK]) for x in "ri"]
        H = [c.sb(f"H_{x}", [P, PAIRS, NC + 1]) for x in "ri"]
        ROTt = WBt
        HS = [c.sb(f"HS_{x}", [P, PAIRS, NB]) for x in "ri"]
        dsk = c.sb("dsk", [CH, GRP, CH])
        dd = c.sb("dd", [CH, GRP, CH])
        tp1, tp2 = c.sb("tp1", [P, PAIRS * 64]), c.sb("tp2", [P, PAIRS * 64])
        PA = c.ps("PA", [P, 8, 512])
        ev = Once(c, "m")
        dv, pl = c.steps("dve_steps"), c.steps("pool_steps")
        loads, u_in, us_in, toe, stores = (c.sem(n) for n in ("loads_m", "u_in", "us_in", "toe_in", "stores_m"))
        copied = c.sem("bu_copied")
        y_copied = c.sem("y_copied")

        def tell(eng, name):
            eng.sem_inc(ev[name], 1)

        with nc.Block() as block:

            @block.sync
            def _(sp):
                sp.dma_start(ident[:], a["ident"]).then_inc(loads, 16)
                sp.dma_start(dsk[:].rearrange("p g c -> p (g c)"), a["d_skip"].to_broadcast([CH, SW])).then_inc(loads, 16)
                sp.dma_start(U2[:], s["u"][0:SEQ, :].rearrange("(c j) n -> c (j n)", j=L)).then_inc(u_in, 16)
                for j in range(L):
                    src = s["u"][SEQ:SEQ + NS_ROWS, :].rearrange("(b j) (g n) -> j b g n", j=L, n=CH)
                    sp.dma_start(Us[:, :, j, :], src[j]).then_inc(us_in, 16)
                sp.wait_ge(ev["k16"], 1)
                sp.wait_ge(ev["toe_zero"], 1)
                for j in range(L):
                    sp.dma_start(TOE[j * CH:(j + 1) * CH, :, j * CH:], K16[:, :, 0:(L - j) * CH]).then_inc(toe, 16)
                sp.wait_ge(y_copied, 8)
                for lo in (SEQ, SEQ + NS_ROWS):
                    sp.dma_start(s["y_ssm"][lo:lo + NS_ROWS, :].rearrange("(b j) n -> b (j n)", j=L),
                                 Us[:].rearrange("b g j n -> b (g j n)")).then_inc(stores, 16)
                sp.wait_ge(ev["h_prompt"], 1)
                sp.dma_start(a["ssm_re_prompt"], v["g1"][:]).then_inc(stores, 16)
                sp.dma_start(a["ssm_im_prompt"], v["g2"][:]).then_inc(stores, 16)
                sp.wait_ge(ev["h_sample"], 1)
                sp.dma_start(a["ssm_re_sample"], HS[0][:]).then_inc(stores, 16)
                sp.dma_start(a["ssm_im_sample"], HS[1][:]).then_inc(stores, 16)
                sp.wait_ge(y_copied, 16)
                sp.dma_start(s["y_ssm"][0:SEQ, :].rearrange("(c j) n -> c (j n)", j=L), U2[:]).then_inc(stores, 16)
                sp.wait_ge(stores, 16 * 7)

            @block.gpsimd
            def _(pool):
                pool.wait_ge(ev["wb_turned"], 1)
                pool.tensor_copy(ROTt[0][:, :, 0:1].rearrange("p q o -> p (q o)"), v["uc"][:])
                pl.chain(pool, pool.tensor_copy(ROTt[1][:, :, 0:1].rearrange("p q o -> p (q o)"), v["us"][:]))
                n = 1
                while n < CK:
                    x = [bcast(ROTt[i][:, :, n - 1], n, 2) for i in range(2)]
                    y = [ROTt[i][:, :, 0:n] for i in range(2)]
                    t1, t2 = (t[:, 0:PAIRS * n].rearrange("p (q n) -> p q n", n=n) for t in (tp1, tp2))
                    mul(pool, pl, ROTt[0][:, :, n:2 * n], x, y, t1, t2, 0)
                    mul(pool, pl, ROTt[1][:, :, n:2 * n], x, y, t1, t2, 1)
                    n *= 2
                tell(pool, "rot")
                pool.wait_ge(ev["u_turned"], 8)
                pool.memset(U2g[:], 0.0).then_inc(ev["toe_zero"], 1)

            @block.scalar
            def _(act):
                for b in range(8):
                    act.wait_ge(ev["wb_part"], b + 1)
                    nc.scalar.activation(WB[b // 4][:, 4 * (b % 4):4 * (b % 4) + 4, :],
                                         PA[:, b, :].rearrange("p (q n) -> p q n", n=P), ACT.Copy).then_inc(ev["wb"], 1)
                act.wait_ge(u_in, 16)
                nc.scalar.activation(U2g[:].rearrange("p (g j n) -> p j g n", j=L, n=CH),
                                     U2[:].rearrange("p (j g n) -> p j g n", j=L, n=CH), ACT.Copy).then_inc(ev["u_grouped"], 1)
                act.wait_ge(ev["k_done"], 1)
                act.wait_ge(ev["u_grouped"], 1)
                for b in range(8):
                    ins = nc.scalar.activation(
                        K16.rearrange("p (q s) m -> p s q m", s=2)[:, b // 4, 4 * (b % 4):4 * (b % 4) + 4, :],
                        PA[0:CH, b, :].rearrange("p (q n) -> p q n", n=P), ACT.Copy)
                ins.then_inc(ev["k_copied"], 1)
                for b in range(8):
                    act.wait_ge(ev["u_turned"], b + 1)
                    nc.scalar.activation(XT[:, 4 * b:4 * b + 4, 0:CK], PA[:, b, :].rearrange("p (g n) -> p g n", n=CK),
                                         ACT.Copy).then_inc(ev["xt"], 1)
                act.wait_ge(ev["us_turned"], 1)
                nc.scalar.activation(XT[:, :, CK:NC], PA[:, 0, 0:GRP * NB].rearrange("p (g n) -> p g n", n=NB),
                                     ACT.Copy).then_inc(ev["xt"], 1)
                for n in range(12):
                    x, q = n // 6, 3 * (n % 6)
                    w = min(3, PAIRS - q)
                    act.wait_ge(ev["bu_part"], n + 1)
                    nc.scalar.activation(BU[x][:, q:q + w, :], PA[:, n % 8, 0:w * NC].rearrange("p (q n) -> p q n", n=NC),
                                         ACT.Copy).then_inc(copied, 1)
                act.wait_ge(toe, 16 * L)
                for b in range(8):
                    act.wait_ge(ev["ys_part"], b + 1)
                    out = Us[:].rearrange("b g j n -> b (g j n)").rearrange(
                        "p (j q s n) -> p s q j n", j=L, q=PAIRS, s=2)[:, b // 4, 4 * (b % 4):4 * (b % 4) + 4]
                    nc.scalar.activation(out, PA[0:NB, b, :].rearrange("p (q j n) -> p q j n", q=4, j=L),
                                         ACT.Copy).then_inc(y_copied, 1)
                for b in range(8):
                    act.wait_ge(ev["y_part"], b + 1)
                    out = U2[:].rearrange("p (j q s n) -> p s q j n", j=L, q=PAIRS, s=2)[:, b // 4, 4 * (b % 4):4 * (b % 4) + 4]
                    nc.scalar.activation(out, PA[:, b, :].rearrange("p (q j n) -> p q j n", q=4, j=L),
                                         ACT.Copy).then_inc(y_copied, 1)

            @block.vector
            def _(dve):
                tt, ts = nc.vector.tensor_tensor, nc.vector.tensor_scalar

                def link(ins):
                    dv.chain(dve, ins)

                for i in range(2):
                    nc.vector.memset(H[i][:, :, 0:1], 0.0)
                    ins = nc.vector.tensor_copy(H[i][:, :, CK + 1:NC + 1], h0[i][:])
                link(ins)
                tell(dve, "h_begun")
                dve.wait_ge(loads, 16 * 2)
                link(tt(dd[:], dsk[:], bcast(ident[0:CH, 0:CH], GRP, 1), ALU.mult))
                dve.wait_ge(ev["k_copied"], 1)
                tt(K16[:, :, 0:CH], K16[:, :, 0:CH], dd[:], ALU.add).then_inc(ev["k16"], 1)
                dve.wait_ge(copied, 12)
                dve.wait_ge(ev["rot"], 1)
                rot = [r[:] for r in ROTt]
                bu = [b[:, :, 0:CK] for b in BU]
                t1, t2 = (t[:, 0:PAIRS * CK].rearrange("p (q n) -> p q n", n=CK) for t in (T1, T2))
                tt(t1, rot[0], bu[0], ALU.mult)
                link(tt(t2, rot[1], bu[1], ALU.mult))
                link(tt(G[0][:], t1, t2, ALU.add))
                tt(t1, rot[0], bu[1], ALU.mult)
                link(tt(t2, rot[1], bu[0], ALU.mult))
                link(tt(G[1][:], t1, t2, ALU.subtract))
                for i in range(2):
                    for q in range(PAIRS):
                        ins = nc.vector.tensor_tensor_scan(G[i][:, q, :], v["mag8"][:, q:q + 1].to_broadcast([P, CK]),
                                                           G[i][:, q, :], 0.0, ALU.mult, ALU.add)
                link(ins)
                g = [x[:] for x in G]
                for i in range(2):
                    mul(nc.vector, dv, H[i][:, :, 1:CK + 1], rot, g, t1, t2, i)
                tell(dve, "h")
                nc.vector.tensor_copy(v["g1"][:], H[0][:, :, CK])
                nc.vector.tensor_copy(v["g2"][:], H[1][:, :, CK]).then_inc(ev["h_prompt"], 1)
                x = [bcast(PW[i][:, L, :], NB, 2) for i in range(2)]
                y = [h0[i][:] for i in range(2)]
                t1, t2 = (t[:, 0:PAIRS * NB].rearrange("p (q n) -> p q n", n=NB) for t in (T1, T2))
                for i in range(2):
                    mul(nc.vector, dv, HS[i][:], x, y, t1, t2, i)
                    link(tt(HS[i][:], HS[i][:], BU[i][:, :, CK:NC], ALU.add))
                tell(dve, "h_sample")

            @block.tensor
            def _(pe):
                pe.wait_ge(loads, 16 * 2)
                for b in range(8):
                    for n in range(4):
                        q = 4 * (b % 4) + n
                        ins = nc.tensor.transpose(PA[:, b, n * P:(n + 1) * P], WBt[b // 4][:, q, :], ident[:])
                    ins.then_inc(ev["wb_part"], 1)
                pe.wait_ge(ev["wb"], 8)
                tell(pe, "wb_turned")
                for q in range(PAIRS):
                    for h in range(2):
                        rows = slice(h * ST, (h + 1) * ST)
                        out = PA[0:CH, 4 * h + q // 4, (q % 4) * P:(q % 4 + 1) * P]
                        for i in range(2):
                            ins = nc.tensor.matmul(out, BB[i][rows, q, :], WC[i][rows, q, 0:P], start=(i == 0), stop=(i == 1))
                ins.then_inc(ev["k_done"], 1)
                pe.wait_ge(ev["k_copied"], 1)
                pe.wait_ge(ev["u_grouped"], 1)
                for g in range(GRP):
                    ins = nc.tensor.transpose(PA[:, g // 4, (g % 4) * P:(g % 4 + 1) * P], U2g[:, g * P:(g + 1) * P], ident[:])
                    if g % 4 == 3:
                        ins.then_inc(ev["u_turned"], 1)
                pe.wait_ge(us_in, 16 * L)
                pe.wait_ge(ev["xt"], 1)
                for g in range(GRP):
                    ins = nc.tensor.transpose(PA[:, 0, g * NB:(g + 1) * NB], Us[:, g].rearrange("b j n -> b (j n)"),
                                              ident[0:NB, 0:NB])
                ins.then_inc(ev["us_turned"], 1)
                pe.wait_ge(ev["xt"], 9)
                for n in range(12):
                    x, q0 = n // 6, 3 * (n % 6)
                    if n >= 8:
                        pe.wait_ge(copied, n - 7)
                    for q in range(q0, min(q0 + 3, PAIRS)):
                        for h in range(2):
                            rows = slice(h * ST, (h + 1) * ST)
                            ins = nc.tensor.matmul(PA[rows, n % 8, (q - q0) * NC:(q - q0 + 1) * NC],
                                                   WB[x][:, q, rows], XT[:, 2 * q + h, :], start=True, stop=True)
                    ins.then_inc(ev["bu_part"], 1)
                pe.wait_ge(copied, 12)
                pe.wait_ge(ev["h_begun"], 1)
                pe.wait_ge(toe, 16 * L)

                def outputs(b, lo, hi, xlo, part):
                    h = b // 4
                    rows = slice(h * ST, (h + 1) * ST)
                    for n in range(4):
                        q = 4 * (b % 4) + n
                        out = PA[0:hi - lo, b, n * P:(n + 1) * P]
                        nc.tensor.matmul(out, XT[:, 2 * q + h, xlo:xlo + hi - lo], TOE[:, 2 * q + h, :], start=True, stop=False)
                        nc.tensor.matmul(out, H[0][rows, q, lo:hi], WC[0][rows, q, CH:], start=False, stop=False)
                        ins = nc.tensor.matmul(out, H[1][rows, q, lo:hi], WC[1][rows, q, CH:], start=False, stop=True)
                    ins.then_inc(part, 1)

                for b in range(8):
                    outputs(b, CK + 1, NC + 1, CK, ev["ys_part"])
                pe.wait_ge(ev["h"], 1)
                for b in range(8):
                    pe.wait_ge(y_copied, b + 1)
                    outputs(b, 0, CK, 0, ev["y_part"])


class PerTile:

    def __init__(self, sem, per):
        self.sem, self.n, self.base, self.per = sem, 0, 0, per

    def chain(self, eng, t, ins, nop=False):
        self.n += 1
        ins.then_inc(self.sem, 1)
        eng.wait_ge(self.sem, self.n if t is None else self.base + t * self.per + self.n)
        if nop:
            eng.nop(nofuse=True)

    def loop_begins(self):
        self.base, self.n = self.n, 0

    def turn_ends(self):
        assert self.n == self.per, (self.n, self.per)
        self.n = 0


def retrieve_experts(nc, sems, a, s):
    with ExitStack() as ctx:
        c = Core(nc, ctx, sems)
        KS, NSLOT, UR, VR, DG = TOPK, EH * TOPK, 8, 4, 4
        DVE_STEPS = 130
        HC = 2 * EH
        BLOCKS = ((0, 2, 16), (2, 4, 5), (4, 8, 3), (8, 16, 1))
        NCAND = sum((a1 - a0) * b for a0, a1, b in BLOCKS)
        LOWEST = float(np.finfo(np.float32).min)
        wq = c.sb("wq", [P, KD, EH * 2 * QH])
        keys = c.sb("keys", [QH, HC, KEYS])
        w_bot = c.sb("w_bot", [P, SW // P, D])
        w_glu = c.sb("w_glu", [P, SW // P, SW])
        b_glu = c.sb("b_glu", [P, SW])
        g_ffn = c.sb("g_ffn", [P, D])
        g_fin = c.sb("g_fin", [P, D])
        g_ssm = c.sb("g_ssm", [P, SW // P])
        ident = c.sb("ident_d", [P, P])
        fold = c.sb("fold", [P, P])
        place = c.sb("place", [P, NCAND])
        u_ring = c.sb("u_ring", [P, UR, D])
        v_ring = c.sb("v_ring", [P, VR, D])
        xr = c.sb("xr", [P, D])
        xn_next = c.sb("xn_next", [P, D])
        xn = c.sb("xn", [P, D])
        xo = c.sb("xo", [P, D])
        xnT = c.sb("xnT", [P, KD, P])
        qT = c.sb("qTe", [P, EH, P])
        S = c.sb("S", [P, EH, KEYS])
        y = c.sb("y", [P, SW])
        z = c.sb("z", [P, SW])
        yT = c.sb("yT", [P, SW // P, P])
        dg = c.sb("dg", [P, DG, P])
        top_v = c.sb("top_v", [P, EH, 2, KS])
        top_i = c.sb("top_i", [P, EH, 2, KS], U32)
        top_f = c.sb("top_f", [P, EH, 2, KS])
        left = c.sb("left", [P, KEYS])
        cand = c.sb("cand", [P, EH, NCAND])
        cid = c.sb("cid", [P, EH, NCAND])
        best = c.sb("best", [P, EH, KS])
        pos = c.sb("pos", [P, EH, KS], U32)
        pos_f = c.sb("pos_f", [P, EH, KS])
        idx_f = c.sb("idx_f", [P, EH, KS])
        idx_next = c.sb("idx_next", [P, NSLOT], U32)
        idx = c.sb("idx", [P, NSLOT], U32)
        idx_first = c.sb("idx_first", [P, KS], U32)
        idx_last = c.sb("idx_last", [P, KS], U32)
        ex = c.sb("ex", [P, EH, KS])
        gate_next = c.sb("gate_next", [P, NSLOT])
        gate = c.sb("gate", [P, NSLOT])
        dot = c.sb("dot", [P, NSLOT])
        act_w = c.sb("act_w", [P, NSLOT])
        wgt = c.sb("wgt", [P, NSLOT])
        stat = c.sb("stat_e", [P, 16])
        nmax, esum = c.sb("nmax", [P, EH]), c.sb("esum", [P, EH])
        match = S[:].rearrange("p h n -> p (h n)")[:, 0:KS * NCAND].rearrange("p (k n) -> p k n", n=NCAND)
        squares = S[:].rearrange("p h n -> p (h n)")
        (ss_y, ms_y, sd_y, rs_y, ss_x, ms_x, sd_x, rs_x, ss_o, ms_o, sd_o, rs_o) = (stat[:, i:i + 1] for i in range(12))
        ACC = c.ps("ACC", [P, 2, 512])
        TQ = c.ps("TQ", [P, 2, 512])
        ZS = c.ps("ZS", [P, 2, 512])
        OP = c.ps("OP", [P, 2, 512])
        acc = ACC[:].rearrange("p b n -> p (b n)")

        weights = c.sem("weights_e")
        early, bottom = c.sem("weights_e1"), c.sem("weights_e2")
        y_in, xr_in = c.count("y_in", 16), c.count("xr_in", 16)
        stored = c.sem("stored_e")
        k = {n: c.count(n) for n in (
            "y_gelu y_turned yT_done z_done zb_done gate_y sd_y_done yn_done yn_turned ynT_done bot_done xr_done "
            "sd_x_done xn_done xn_turned xnT_done q_a q_b q_c q_d qT_a qT_b qT_c qT_d s_a s_b S_a S_b topped_a topped_b "
            "idx_ready nmax_done ex_done gate_ready idx_taken first_taken last_taken xn_taken gate_taken acc_begun acc_taken "
            "ss_o_done ms_y_done ms_x_done ms_o_done sd_o_done out_ready out_stored").split()}
        u_in = [c.sem(f"u_in{i}") for i in range(UR)]
        v_in = [c.sem(f"v_in{i}") for i in range(VR)]
        dots = c.sem("dots_done")
        pv = c.sem("v_used")
        gelus, wgts, diags = c.sem("gelus"), c.sem("weights_done"), c.sem("diags_done")
        dch = PerTile(c.sem("dve_steps_e"), DVE_STEPS)

        def ring_in(eng, sems, t, s_):
            n = len(sems)
            eng.wait_ge(sems[s_ % n], t * (16 * NSLOT // n) + 16 * (s_ // n + 1))

        def blocks(turn, t):
            if turn == "samples":
                return [(h, (t, h) if h < EH // 2 else None, None) for h in range(1, EH // 2 + 1)]
            return ([(h, (t, h), (t + 1, h)) for h in range(1, EH)]
                    + [(EH, (t + 1, 0), (t + 2, 0) if turn == "steady" else None)])

        with nc.Block() as block:

            @block.sync
            def _(sp):
                def load_y(t):
                    k["yn_turned"].held(sp, t - 1)
                    y_in.mark(sp.dma_start(y[:], s["y_ssm"][bass.ts(t, P), :]))

                def load_xr(t):
                    k["acc_begun"].held(sp, t - 1)
                    xr_in.mark(sp.dma_start(xr[:], s["x1"][bass.ts(t, P), :]))

                def out(t, n):
                    k["out_ready"].held(sp, t)
                    dst = a["y"][bass.ts(t, P), :] if n == P else a["y"][SEQ:SEQ + n, :]
                    sp.dma_start(dst, xo[0:n, :]).then_inc(stored, 16)
                    sp.wait_ge(stored, (t + 1) * 16)
                    sp.nop(nofuse=True)
                    sp.sem_inc(k["out_stored"].sem, 1)

                k["out_stored"].prime(sp)
                load_y(0)
                load_xr(0)
                sp.dma_start(ident[:], a["ident"]).then_inc(early, 16)
                sp.dma_start(w_glu[:], a["w_glu"].rearrange("(k p) n -> p k n", p=P)).then_inc(early, 16)
                sp.dma_start(b_glu[:], a["b_glu"].to_broadcast([P, SW])).then_inc(early, 16)
                sp.dma_start(g_ssm[:], a["g_ssm"]).then_inc(early, 16)
                sp.dma_start(w_bot[:], a["w_out"][AW:D, :].rearrange("(k p) n -> p k n", p=P)).then_inc(bottom, 16)
                sp.dma_start(g_ffn[:], a["g_ffn"].to_broadcast([P, D])).then_inc(bottom, 16)
                sp.dma_start(fold[:], a["fold"]).then_inc(weights, 16)
                sp.dma_start(g_fin[:], a["g_final"].to_broadcast([P, D])).then_inc(weights, 16)
                sp.dma_start(place[:], a["place"].to_broadcast([P, NCAND])).then_inc(weights, 16)
                sp.dma_start(keys[:].rearrange("d c n -> d (c n)"), a["keys"]).then_inc(weights, 16)
                sp.dma_start(wq[:], a["w_query"].rearrange("(k p) n -> p k n", p=P)).then_inc(weights, 16)
                load_y(1)
                with sp.Fori(0, PT - 1) as t:
                    load_xr(t + 1)
                    load_y(t + 2)
                    out(t, P)
                load_xr(PT)
                out(PT - 1, P)
                out(PT, NS_ROWS)

            @block.gpsimd
            def _(pool):
                def gather(ring, table, which, col, sems, s_):
                    pool.indirect_dma_start(
                        out=ring[:, s_ % len(sems), :], out_offset=None, in_=a[table],
                        in_offset=bass.IndirectOffsetOnAxis(ap=which[:, col:col + 1], axis=0)
                        ).then_inc(sems[s_ % len(sems)], 16)

                def gather_u(t, h, j):
                    s_ = KS * h + j
                    pool.wait_ge(dots, t * NSLOT + s_ + 1)
                    pool.nop(nofuse=True)
                    gather(u_ring, "u_table", *((idx_first, j) if h == 0 else (idx, s_)), u_in, s_)

                def gather_v(t, h, j):
                    s_ = KS * h + j
                    pool.wait_ge(pv, t * NSLOT + s_ + 1)
                    pool.nop(nofuse=True)
                    gather(v_ring, "v_table", *((idx_last, j) if h == EH - 1 else (idx, s_)), v_in, s_)

                def retrieve(turn, t):
                    k["idx_taken"].held(pool, t)
                    for h, u, _ in blocks(turn, t):
                        if h == EH:
                            k["last_taken"].held(pool, t)
                            k["first_taken"].held(pool, t + 1)
                        for j in range(KS):
                            if u:
                                gather_u(*u, j)
                            gather_v(t, h - 1, j)

                k["first_taken"].held(pool, 0)
                for j in range(KS):
                    gather_u(0, 0, j)
                with pool.Fori(0, PT - 1) as t:
                    retrieve("steady", t)
                retrieve("eighth", PT - 1)
                retrieve("samples", PT)

            @block.scalar
            def _(act):
                A = nc.scalar.activation

                def flat(x):
                    return x.rearrange("p b n -> p (b n)")

                def prepare(t, h, j):
                    at = (h, j)
                    if at == (0, 3):
                        y_in.of(act, t)
                        k["y_gelu"].mark(A(y[:], y[:], ACT.Gelu))
                    elif at == (0, 6):
                        k["y_turned"].of(act, t)
                        k["yT_done"].mark(A(flat(yT[:]), TQ[:, 0, :], ACT.Copy))
                    elif at == (0, 14):
                        k["zb_done"].of(act, t)
                        k["gate_y"].mark(A(z[:], z[:], ACT.Sigmoid))
                    elif at == (1, 6):
                        k["ms_y_done"].of(act, t)
                        k["sd_y_done"].mark(A(sd_y, ms_y, ACT.Sqrt))
                    elif at == (2, 9):
                        k["ms_x_done"].of(act, t)
                        k["sd_x_done"].mark(A(sd_x, ms_x, ACT.Sqrt))
                    elif at == (3, 2):
                        k["xn_turned"].of(act, t)
                        A(flat(xnT[:, 0:4, :]), TQ[:, 0, :], ACT.Copy)
                        k["xnT_done"].mark(A(flat(xnT[:, 4:8, :]), TQ[:, 1, :], ACT.Copy))
                    elif at in ((3, 8), (3, 12), (4, 4), (4, 8)):
                        n = "abcd"[((3, 8), (3, 12), (4, 4), (4, 8)).index(at)]
                        b = n in "bd"
                        k[f"q_{n}"].of(act, t)
                        k[f"qT_{n}"].mark(A(flat(qT[:, 4 * b:4 * b + 4, :]), TQ[:, int(b), :], ACT.Copy))
                    elif at in ((3, 15), (5, 0)):
                        n = "ab"[at == (5, 0)]
                        k[f"s_{n}"].of(act, t)
                        if n == "b":
                            k["topped_a"].of(act, t)
                        A(flat(S[:, 0:4, :]), ZS[:, 0, :], ACT.Copy)
                        k[f"S_{n}"].mark(A(flat(S[:, 4:8, :]), ZS[:, 1, :], ACT.Copy))
                    elif at == (6, 12):
                        k["nmax_done"].of(act, t)
                        for e in range(EH):
                            ins = A(ex[:, e, :], best[:, e, :], ACT.Exp, bias=nmax[:, e:e + 1], accum_out=esum[:, e:e + 1])
                        k["ex_done"].mark(ins)

                def take_rows(t):
                    k["xn_done"].of(act, t)
                    act.wait_ge(dots, t * NSLOT + UR)
                    k["xn_taken"].mark(A(xn[:], xn_next[:], ACT.Copy))

                def take_gates(t, halves):
                    k["gate_ready"].of(act, t)
                    if not isinstance(t, int) or t > 0:
                        act.wait_ge(wgts, t * EH)
                    for lo, hi, up in ((0, NS_ROWS, NSLOT // 2), (NS_ROWS, P, NSLOT)) if halves else ((0, P, NSLOT),):
                        n = NSLOT // 2 if halves else NSLOT
                        ins = A(gate[lo:hi, 0:n], gate_next[lo:hi, up - n:up], ACT.Copy)
                    k["gate_taken"].mark(ins)

                def activate(t, h):
                    act.wait_ge(dots, t * NSLOT + KS * (h + 1) + UR)
                    cols = slice(KS * h, KS * (h + 1))
                    A(act_w[:, cols], dot[:, cols], ACT.Gelu).then_inc(gelus, 1)

                def root_out(t, n):
                    k["ms_o_done"].of(act, t)
                    k["sd_o_done"].mark(A(sd_o[0:n], ms_o[0:n], ACT.Sqrt))

                def retrieve(turn, t):
                    diag = fold if turn == "samples" else ident
                    for h, u, prep in blocks(turn, t):
                        for j in range(KS):
                            s_ = KS * (h - 1) + j
                            if j == 0:
                                act.wait_ge(wgts, t * EH + h)
                            act.wait_ge(pv, t * NSLOT + s_ + 1)
                            A(dg[:, s_ % DG, :], diag[:], ACT.Copy, scale=wgt[:, s_:s_ + 1]).then_inc(diags, 1)
                            if (h, j) == (EH, KS // 2):
                                take_gates(t + 1, turn == "eighth")
                            if prep:
                                prepare(*prep, j)
                        if u and u[1] == EH - 1:
                            take_rows(t + 1)
                        if u:
                            activate(*u)
                    root_out(t, NS_ROWS if turn == "samples" else P)

                for n in ("y_gelu yT_done gate_y sd_y_done sd_x_done xnT_done qT_a qT_b qT_c qT_d S_a S_b ex_done "
                          "xn_taken gate_taken sd_o_done").split():
                    k[n].prime(act)
                act.wait_ge(early, 64)
                for h in range(EH):
                    for j in range(KS):
                        prepare(0, h, j)
                take_rows(0)
                take_gates(0, False)
                for j in range(KS):
                    prepare(1, 0, j)
                activate(0, 0)
                with act.Fori(0, PT - 1) as t:
                    retrieve("steady", t)
                retrieve("eighth", PT - 1)
                retrieve("samples", PT)

            @block.vector
            def _(dve):
                V = nc.vector

                turn_now = [None]

                def dch_(ins, nop=False):
                    dch.chain(dve, turn_now[0], ins, nop)

                def best16(vals, where, src, tmp):
                    dch_(V.max(vals[:, 0:8], src), True)
                    V.max_index(where[:, 0:8], vals[:, 0:8], src)
                    dch_(V.match_replace(tmp, vals[:, 0:8], src, LOWEST), True)
                    dch_(V.max(vals[:, 8:16], tmp), True)
                    dch_(V.max_index(where[:, 8:16], vals[:, 8:16], tmp), True)

                def pairwise(src, dst, op):
                    n = 0
                    for a0, a1, w in BLOCKS:
                        m = a1 - a0
                        x = bcast(src[:, :, 0, a0:a1], w, 3)
                        yy = bcast(src[:, :, 1, 0:w], m, 2)
                        ins = V.tensor_tensor(dst[:, :, n:n + m * w].rearrange("p h (m w) -> p h m w", w=w), x, yy, op)
                        n += m * w
                    return ins

                def prepare(t, h, j):
                    at = (h, j)
                    if at == (0, 13):
                        k["z_done"].of(dve, t)
                        k["zb_done"].mark(V.tensor_tensor(z[:], ZS[:, 0, :], b_glu[:], ALU.add))
                    elif at == (1, 3):
                        k["gate_y"].of(dve, t)
                        dch_(V.tensor_tensor(y[:], y[:], z[:], ALU.mult))
                        dch_(V.tensor_tensor_reduce(z[:], y[:], y[:], 1.0, 0.0, ALU.mult, ALU.add, ss_y))
                        k["ms_y_done"].mark(V.tensor_scalar(ms_y, ss_y, 1.0 / SW, EPS, ALU.mult, ALU.add))
                    elif at == (1, 9):
                        k["sd_y_done"].of(dve, t)
                        dch_(V.reciprocal(rs_y, sd_y))
                        k["yn_done"].mark(V.tensor_scalar(y[:], y[:], rs_y, None, ALU.mult))
                    elif at == (1, 13):
                        k["yn_turned"].of(dve, t)
                        k["ynT_done"].mark(V.tensor_tensor(yT[:], TQ[:, 0, :].rearrange("p (k n) -> p k n", n=P),
                                                           bcast(g_ssm[:], P, 2), ALU.mult))
                    elif at == (2, 6):
                        k["bot_done"].of(dve, t)
                        xr_in.of(dve, t)
                        k["xn_taken"].of(dve, t - 1)
                        V.tensor_tensor(xr[:, 0:512], OP[:, 0, :], xr[:, 0:512], ALU.add)
                        dch_(V.tensor_tensor(xr[:, 512:D], OP[:, 1, :], xr[:, 512:D], ALU.add))
                        k["xr_done"].mark(V.tensor_tensor_reduce(xn_next[:], xr[:], xr[:], 1.0, 0.0, ALU.mult, ALU.add, ss_x))
                        k["xr_done"].of(dve, t)
                        k["ms_x_done"].mark(V.tensor_scalar(ms_x, ss_x, 1.0 / D, EPS, ALU.mult, ALU.add))
                    elif at == (2, 12):
                        k["sd_x_done"].of(dve, t)
                        dch_(V.reciprocal(rs_x, sd_x))
                        k["xn_done"].mark(V.scalar_tensor_tensor(xn_next[:], xr[:], rs_x, g_ffn[:], ALU.mult, ALU.mult))
                    elif h in (4, 5) and j % 2 == 1:
                        n, i = "ab"[h == 5], j // 2
                        e = 4 * (h == 5) + i // 2
                        if i == 0:
                            k[f"S_{n}"].held(dve, t)
                        best16(top_v[:, e, i % 2, :], top_i[:, e, i % 2, :], S[:, i, :], left[:])
                        if i == 7:
                            dve.sem_inc(k[f"topped_{n}"].sem, 1)
                    elif at == (6, 1):
                        dch_(V.tensor_copy(top_f[:], top_i[:]))
                        dch_(V.tensor_scalar(top_f[:, :, 0, :], top_f[:, :, 0, :], float(KEYS), None, ALU.mult))
                        pairwise(top_v, cand, ALU.add)
                        dch_(pairwise(top_f, cid, ALU.add), True)
                    elif h == 6 and 2 <= j < 2 + EH:
                        e = j - 2
                        best16(best[:, e, :], pos[:, e, :], cand[:, e, :], left[:, 0:NCAND])
                    elif at == (6, 10):
                        V.tensor_copy(pos_f[:], pos[:])
                        k["nmax_done"].mark(V.tensor_scalar(nmax[:], best[:, :, 0:1].rearrange("p h o -> p (h o)"), -1.0, None, ALU.mult))
                        k["nmax_done"].of(dve, t)
                    elif at == (6, 14) or (h == 7 and j <= 12 and j % 2 == 0):
                        e = 0 if h == 6 else 1 + j // 2
                        dch_(V.tensor_tensor(match, bcast(place[:], KS, 1), bcast(pos_f[:, e, :], NCAND, 2), ALU.is_equal))
                        dch_(V.tensor_tensor(match, match, bcast(cid[:, e, :], KS, 1), ALU.mult))
                        dch_(V.tensor_reduce(idx_f[:, e, :], match, AX.X, ALU.add))
                    elif at == (7, 13):
                        k["idx_taken"].of(dve, t - 1)
                        k["gate_taken"].of(dve, t - 1)
                        k["idx_ready"].mark(V.tensor_copy(idx_next[:], idx_f[:].rearrange("p h k -> p (h k)")))
                        k["idx_ready"].of(dve, t)
                        k["ex_done"].of(dve, t)
                        dch_(V.reciprocal(esum[:], esum[:]))
                        k["gate_ready"].mark(V.tensor_tensor(gate_next[:].rearrange("p (h k) -> p h k", k=KS), ex[:],
                                                             bcast(esum[:], KS, 2), ALU.mult))

                def take(t, mark, dst, h0, n, halves, src=idx_next):
                    for lo, hi, up in ((0, NS_ROWS, 0), (NS_ROWS, P, EH // 2)) if halves else ((0, P, 0),):
                        cols = slice(KS * (h0 + up), KS * (h0 + up + n))
                        ins = V.tensor_copy(dst[lo:hi, 0:KS * n], src[lo:hi, cols])
                    mark.mark(ins)

                def first_known(t):
                    k["first_taken"].mark(V.tensor_copy(idx_first[:], idx_f[:, 0, :]))

                def take_first(t):
                    k["idx_ready"].of(dve, t)
                    take(t, k["first_taken"], idx_first, 0, 1, True)

                def take_rest(t, halves):
                    take(t, k["idx_taken"], idx, 0, EH // 2 if halves else EH, halves)

                def take_last(t):
                    k["idx_taken"].of(dve, t)
                    take(t, k["last_taken"], idx_last, EH - 1, 1, False, src=idx)

                def product(t, h, j):
                    s_ = KS * h + j
                    if s_ == 0:
                        k["xn_taken"].held(dve, t)
                    ring_in(dve, u_in, t, s_)
                    row = u_ring[:, s_ % UR, :]
                    V.tensor_tensor_reduce(row, row, xn[:], 1.0, 0.0, ALU.mult, ALU.add, dot[:, s_:s_ + 1]).then_inc(dots, 1)

                def weigh(t, h):
                    cols = slice(KS * h, KS * (h + 1))
                    dve.wait_ge(gelus, t * EH + h + 1)
                    V.tensor_tensor(wgt[:, cols], act_w[:, cols], gate[:, cols], ALU.mult).then_inc(wgts, 1)

                def sum_out(t, n, used):
                    k["out_stored"].of(dve, t - 1)
                    dve.wait_ge(pv, used + VR)
                    k["acc_taken"].mark(V.tensor_copy(xo[0:n, :], acc[0:n, :]))
                    k["acc_taken"].of(dve, t)
                    k["ss_o_done"].mark(V.tensor_tensor_reduce(squares[0:n, :], xo[0:n, :], xo[0:n, :], 1.0, 0.0,
                                                               ALU.mult, ALU.add, ss_o[0:n]))
                    k["ss_o_done"].of(dve, t)
                    k["ms_o_done"].mark(V.tensor_scalar(ms_o[0:n], ss_o[0:n], 1.0 / D, EPS, ALU.mult, ALU.add))

                def norm_out(t, n):
                    k["sd_o_done"].of(dve, t)
                    dch_(V.reciprocal(rs_o[0:n], sd_o[0:n]))
                    k["out_ready"].mark(V.scalar_tensor_tensor(xo[0:n, :], xo[0:n, :], rs_o[0:n], g_fin[0:n, :],
                                                               ALU.mult, ALU.mult))

                def retrieve(turn, t):
                    turn_now[0] = t
                    for h, u, prep in blocks(turn, t):
                        for j in range(KS):
                            if u:
                                product(*u, j)
                            if j == 0:
                                weigh(t, h - 1)
                            if (h, j) == (2, 0) and turn != "samples":
                                take_last(t)
                            if prep:
                                prepare(*prep, j)
                            if (h, j) == (EH - 2, KS - 1) and turn == "steady":
                                first_known(t + 1)
                            if (h, j) == (EH - 1, KS - 3) and turn == "eighth":
                                take_first(t + 1)
                            if (h, j) == (EH, KS // 2):
                                dve.wait_ge(pv, t * NSLOT + NSLOT - KS + VR)
                                take_rest(t + 1, turn == "eighth")
                    n, slots = (NS_ROWS, NSLOT // 2) if turn == "samples" else (P, NSLOT)
                    sum_out(t, n, t * NSLOT + slots)
                    norm_out(t, n)

                for n in ("zb_done yn_done ynT_done xr_done xn_done topped_a topped_b first_taken last_taken idx_taken idx_ready nmax_done gate_ready "
                          "acc_taken ss_o_done ms_y_done ms_x_done ms_o_done out_ready").split():
                    k[n].prime(dve)
                dve.sem_inc(dots, UR)
                dve.wait_ge(early, 64)
                for h in range(EH):
                    for j in range(KS):
                        if (h, j) == (2, 0):
                            dve.wait_ge(bottom, 16 * 2)
                        elif (h, j) == (3, 0):
                            dve.wait_ge(weights, 16 * 5)
                        prepare(0, h, j)
                        if (h, j) == (EH - 2, KS - 1):
                            first_known(0)
                take_rest(0, False)
                for j in range(KS):
                    product(0, 0, j)
                    prepare(1, 0, j)
                dch.loop_begins()
                with dve.Fori(0, PT - 1) as t:
                    retrieve("steady", t)
                dch.turn_ends()
                retrieve("eighth", PT - 1)
                dch.turn_ends()
                retrieve("samples", PT)

            @block.tensor
            def _(pe):
                def prepare(t, h, j):
                    at = (h, j)
                    if at == (0, 4):
                        k["y_gelu"].of(pe, t)
                        k["xnT_done"].of(pe, t - 1)
                        for n in range(SW // P):
                            ins = nc.tensor.transpose(TQ[:, 0, n * P:(n + 1) * P], y[:, n * P:(n + 1) * P], ident[:])
                        k["y_turned"].mark(ins)
                    elif at == (0, 9):
                        k["yT_done"].of(pe, t)
                        k["S_b"].of(pe, t - 1)
                        for n in range(SW // P):
                            ins = nc.tensor.matmul(ZS[:, 0, :], yT[:, n, :], w_glu[:, n, :], start=(n == 0), stop=(n == SW // P - 1))
                        k["z_done"].mark(ins)
                    elif at == (1, 11):
                        k["yn_done"].of(pe, t)
                        for n in range(SW // P):
                            ins = nc.tensor.transpose(TQ[:, 0, n * P:(n + 1) * P], y[:, n * P:(n + 1) * P], ident[:])
                        k["yn_turned"].mark(ins)
                    elif at in ((2, 1), (2, 3)):
                        b = int(at == (2, 3))
                        k["ynT_done"].of(pe, t)
                        k["xr_done"].of(pe, t - 1)
                        for n in range(SW // P):
                            ins = nc.tensor.matmul(OP[:, b, :], yT[:, n, :], w_bot[:, n, 512 * b:512 * b + 512],
                                                   start=(n == 0), stop=(n == SW // P - 1))
                        if b:
                            k["bot_done"].mark(ins)
                    elif at == (2, 15):
                        k["xn_done"].of(pe, t)
                        for n in range(KD):
                            ins = nc.tensor.transpose(TQ[:, n // 4, (n % 4) * P:(n % 4 + 1) * P],
                                                      xn_next[:, n * P:(n + 1) * P], ident[:])
                        k["xn_turned"].mark(ins)
                    elif (h == 3 and 3 <= j < 11) or (h == 4 and j < 8):
                        i = j - 3 if h == 3 else j
                        if i == 0:
                            k["xnT_done"].of(pe, t)
                            k["qT_b"].of(pe, t if h == 4 else t - 1)
                            k["s_a"].of(pe, t if h == 4 else t - 1)
                        hc = i + 8 * (h == 4)
                        for n in range(KD):
                            ins = nc.tensor.matmul(TQ[:, i // 4, (i % 4) * P:(i % 4 + 1) * P],
                                                   wq[:, n, hc * QH:(hc + 1) * QH], xnT[:, n, :],
                                                   start=(n == 0), stop=(n == KD - 1))
                        if i % 4 == 3:
                            k["q_" + "abcd"[2 * (h == 4) + i // 4]].mark(ins)
                    elif at in ((3, 13), (4, 10)):
                        n = "ab"[h == 4]
                        k["qT_" + "bd"[h == 4]].of(pe, t)
                        if n == "b":
                            k["S_a"].of(pe, t)
                        for i in range(EH):
                            ins = nc.tensor.matmul(ZS[:, i // 4, (i % 4) * P:(i % 4 + 1) * P], qT[:, i, :],
                                                   keys[:, i + 8 * (h == 4), :], start=True, stop=True)
                        k[f"s_{n}"].mark(ins)

                def begin(t):
                    k["xr_done"].of(pe, t)
                    k["acc_taken"].of(pe, t - 1)
                    for b in range(2):
                        ins = nc.tensor.matmul(ACC[:, b, :], ident[:], xr[:, 512 * b:512 * b + 512],
                                               start=True, stop=False)
                    k["acc_begun"].mark(ins)

                def add_v(t, s_, last):
                    pe.wait_ge(diags, t * NSLOT + s_ + 1)
                    ring_in(pe, v_in, t, s_)
                    for b in range(2):
                        ins = nc.tensor.matmul(ACC[:, b, :], dg[:, s_ % DG, :], v_ring[:, s_ % VR, 512 * b:512 * b + 512],
                                               start=False, stop=last)
                    ins.then_inc(pv, 1)

                def retrieve(turn, t):
                    begin(t)
                    last = (NSLOT // 2 if turn == "samples" else NSLOT) - 1
                    for h, u, prep in blocks(turn, t):
                        for j in range(KS):
                            s_ = KS * (h - 1) + j
                            add_v(t, s_, s_ == last)
                            if prep:
                                prepare(*prep, j)

                for n in ("y_turned z_done yn_turned bot_done xn_turned q_a q_b q_c q_d s_a s_b acc_begun").split():
                    k[n].prime(pe)
                pe.sem_inc(pv, VR)
                pe.wait_ge(early, 64)
                for h in range(EH):
                    for j in range(KS):
                        if (h, j) == (2, 0):
                            pe.wait_ge(bottom, 16 * 2)
                        elif (h, j) == (3, 0):
                            pe.wait_ge(weights, 16 * 5)
                        prepare(0, h, j)
                for j in range(KS):
                    prepare(1, 0, j)
                with pe.Fori(0, PT - 1) as t:
                    retrieve("steady", t)
                retrieve("eighth", PT - 1)
                retrieve("samples", PT)


def hybrid_layer(nc, a, s):
    sems = []

    def phase_ends():
        nc.clear_and_free_semaphores(sems)
        sems.clear()
        nc.all_engine_barrier()

    with ExitStack() as kept:
        par = SsmParameters(Core(nc, kept, sems))
        with ExitStack() as ctx:
            shared = Shared(Core(nc, ctx, sems))
            mix_tokens(nc, sems, a, s, shared, par)
            mix_samples(nc, sems, a, s, shared)
        phase_ends()
        run_ssm(nc, sems, a, s, par)
    phase_ends()
    retrieve_experts(nc, sems, a, s)


def host_layout(x):
    f = {n: np.ascontiguousarray(np.asarray(v)) for n, v in x.items()}
    rows = np.zeros((ROWS_PAD, D), np.float32)
    rows[:SEQ] = f["x_prompt"].reshape(SEQ, D)
    rows[SEQ:SEQ + NS_ROWS] = f["x_sample"].reshape(NS_ROWS, D)
    pos = np.zeros(ROWS_PAD, np.float32)
    pos[:SEQ] = np.arange(SEQ)
    pos[SEQ:SEQ + NS_ROWS] = np.tile(PAST + np.arange(DEC), NB)
    inv = np.float32(500000.0) ** (-np.arange(HALF, dtype=np.float32) * np.float32(2.0) / np.float32(ROT))
    ang = pos[:, None] * inv[None, :].astype(np.float32)
    rope = np.concatenate([np.cos(ang), np.sin(ang)], axis=1).astype(np.float32)
    q, key = np.arange(P)[:, None], np.arange(W)[None, :]
    off = np.float32(NEG / SCALE)
    mask = np.zeros((ROWS_PAD, 2 * W), np.float32)
    for t in range(PT):
        own = np.where(key <= q, 0, off)
        before = np.where((key > q) & (t > 0), 0, off)
        mask[t * P:(t + 1) * P] = np.concatenate([own, before] if t % 2 == 0 else [before, own], axis=1)
    i, key = (np.arange(P) % DEC)[:, None], np.arange(W + DEC)[None, :]
    mask_s = np.where((key > i) & (key <= W + i), 0, off).astype(np.float32)

    def pairs(v):
        v = v.reshape(PAIRS, 2, ST, *v.shape[2:])
        return np.ascontiguousarray(np.moveaxis(v, 0, 2).reshape(2 * ST, PAIRS, *v.shape[3:]))

    cols = np.concatenate([np.arange(AW).reshape(KV, REP, HD).transpose(1, 0, 2).ravel(), np.arange(AW, IN_W)])
    out = {
        "x": rows, "rope": rope, "mask": mask, "mask_s": mask_s,
        "ident": np.eye(P, dtype=np.float32), "fold": np.tile(np.eye(P // 2, P, dtype=np.float32), (2, 1)),
        "minus_half": np.full((P, 1), -0.5, np.float32),
        "w_in": f["w_in"][0][:, cols], "b_in": f["b_in"].reshape(1, IN_W)[:, cols],
        "g_mix": np.ascontiguousarray(f["norm_mix"].reshape(KD, P).T),
        "g_attn": np.ascontiguousarray(f["norm_attn_out"].reshape(AW // P, P).T),
        "g_ssm": np.ascontiguousarray(f["norm_ssm_out"].reshape(SW // P, P).T),
        "g_ffn": f["norm_ffn"].reshape(1, D), "g_final": f["norm_final"].reshape(1, D),
        "sink": f["attn_sinks"].reshape(1, HEADS),
        "sink_s": np.ascontiguousarray(np.broadcast_to(
            f["attn_sinks"].reshape(KV, 1, REP, 1), (KV, 4, REP, DEC)).reshape(KV, P).T),
        "w_out": f["w_out"][0], "w_glu": f["ssm_w_glu"][0], "b_glu": f["ssm_b_glu"].reshape(1, SW),
        "cache_k": f["cache_k"].reshape(NB, W, KV * HD), "cache_v": f["cache_v"].reshape(NB, W, KV * HD),
        "h0_re": pairs(np.moveaxis(f["state_ssm_re"][0], 0, 2)), "h0_im": pairs(np.moveaxis(f["state_ssm_im"][0], 0, 2)),
        "lam_re": pairs(f["ssm_lam_re"][0]), "lam_im": pairs(f["ssm_lam_im"][0]),
        "log_step": pairs(np.broadcast_to(f["ssm_log_step"][0][:, None], (GRP, ST))),
        "b_re": pairs(f["ssm_b_re"][0]), "b_im": pairs(f["ssm_b_im"][0]),
        "c_re": pairs(np.swapaxes(f["ssm_c_re"][0], 1, 2)), "c_im": pairs(np.swapaxes(f["ssm_c_im"][0], 1, 2)),
        "d_skip": f["ssm_d"].reshape(1, SW),
        "w_query": f["peer_w_query"][0],
        "keys": np.ascontiguousarray(np.transpose(f["peer_sub_keys"][0], (3, 0, 1, 2)).reshape(QH, EH * 2 * KEYS)),
        "place": np.arange(62, dtype=np.float32).reshape(1, 62),
        "u_table": f["peer_u"][0], "v_table": f["peer_v"][0],
    }
    return {n: np.ascontiguousarray(v) for n, v in out.items()}


OUTPUTS = {
    "y": (SEQ + NS_ROWS, D), "new_k_prompt": (W, KV * HD), "new_v_prompt": (W, KV * HD),
    "ssm_re_prompt": (P, PAIRS), "ssm_im_prompt": (P, PAIRS),
    "new_k_sample": (NB, W, KV * HD), "new_v_sample": (NB, W, KV * HD),
    "ssm_re_sample": (P, PAIRS, NB), "ssm_im_sample": (P, PAIRS, NB),
}
SCRATCH = {
    "u": (ROWS_PAD, SW), "x1": (ROWS_PAD, D), "pj": (NS_ROWS, U_COL),
    "attn_s": (P, 4 * HD), "y_ssm": (ROWS_PAD, SW),
}


def kernel(**inputs):
    import concourse.bacc as bacc
    from concourse.bass_utils import run_bass_kernel_spmd

    nc = bacc.Bacc("TRN2", target_bir_lowering=False, num_devices=1)
    laid = host_layout(inputs)
    a = {n: nc.dram_tensor(f"in_{n}", v.shape, mybir.dt.from_np(v.dtype), kind="ExternalInput").ap()
         for n, v in laid.items()}
    a |= {n: nc.dram_tensor(f"out_{n}", shape, F32, kind="ExternalOutput").ap() for n, shape in OUTPUTS.items()}
    s = {n: nc.dram_tensor(f"scratch_{n}", shape, F32, kind="Internal").ap() for n, shape in SCRATCH.items()}
    hybrid_layer(nc, a, s)
    r = run_bass_kernel_spmd(nc, [{f"in_{n}": v for n, v in laid.items()}], core_ids=[0]).results[0]
    got = {n: np.asarray(r[f"out_{n}"]) for n in OUTPUTS}

    def groups(v):
        v = np.moveaxis(v.reshape(2, ST, PAIRS, *v.shape[2:]), 2, 0)
        return v.reshape(GRP, ST, *v.shape[3:])

    def state(n, sample):
        v = groups(got[n])
        return np.moveaxis(v, 2, 0)[None] if sample else v[None, None]

    window = (1, 1, W, KV, HD)
    windows = (1, NB, W, KV, HD)
    return (got["y"][:SEQ].reshape(1, SEQ, D), got["y"][SEQ:].reshape(NB, DEC, D),
            got["new_k_prompt"].reshape(window), got["new_v_prompt"].reshape(window),
            state("ssm_re_prompt", False), state("ssm_im_prompt", False),
            got["new_k_sample"].reshape(windows), got["new_v_sample"].reshape(windows),
            state("ssm_re_sample", True), state("ssm_im_sample", True))
```
